# Optimizing a Trainium2 kernel written in Bass

```python
import jax, jax.numpy as jnp
from jax import lax
import numpy as np

D_MODEL = 1024
BATCH = 1
SEQ = 1024
DEPTH = 1

BRANCH_WIDTH = D_MODEL // 2
HEAD_DIM = 64
N_BRANCH = 4
CONV_WIDTH_A = BRANCH_WIDTH
CONV_K = 3
NSA_HEADS = BRANCH_WIDTH // HEAD_DIM
NSA_KV_GROUPS = 2
NSA_REP = NSA_HEADS // NSA_KV_GROUPS
NSA_WIDTH = NSA_HEADS * HEAD_DIM
KV_WIDTH = NSA_KV_GROUPS * HEAD_DIM
CMP_BLOCK = 32
CMP_STRIDE = 16
SLC_BLOCK = 64
SLC_TOPN = 16
WIN = 512
Q_BLOCK = 128
NEG = -1e30
FORCE = 1e6
POOL_WINDOWS = (2, 4, 8, 16)
POOL_GROUPS = len(POOL_WINDOWS)
POOL_GROUP_DIM = BRANCH_WIDTH // POOL_GROUPS
POOL_WIDTH = BRANCH_WIDTH
SGU_CHUNK = 128
SGU_GROUPS = 4
SGU_WIDTH = BRANCH_WIDTH
SGU_GROUP_DIM = SGU_WIDTH // SGU_GROUPS
D_FF = 2816
FF_CONV_K = 3
RMS_EPS = 1e-6
IN_SPLITS = (CONV_WIDTH_A, CONV_WIDTH_A, CONV_WIDTH_A, NSA_WIDTH, 6 * KV_WIDTH, 3 * NSA_HEADS,
             POOL_WIDTH, 2 * SGU_WIDTH, N_BRANCH * D_MODEL)
N_IN = sum(IN_SPLITS)

kernel_name = 'hybrid_gated_parallel_mixer'

def rms_norm(x, g, eps=RMS_EPS):
    xf = x.astype(jnp.float32)
    y = xf * lax.rsqrt(jnp.mean(xf * xf, axis=-1, keepdims=True) + eps)
    return (y * g.astype(jnp.float32)).astype(x.dtype)

def causal_dwconv(x, w):
    k, s = w.shape[0], x.shape[1]
    xp = jnp.pad(x, ((0, 0), (k - 1, 0), (0, 0)))
    return sum(w[j] * xp[:, j:j + s] for j in range(k))

def split_columns(z):
    offs, acc = [], 0
    for n in IN_SPLITS[:-1]:
        acc += n
        offs.append(acc)
    return jnp.split(z, offs, axis=-1)

def overlap_matrix(n_cmp, n_slc):
    cs = np.arange(n_cmp) * CMP_STRIDE
    ce = cs + CMP_BLOCK
    ss = np.arange(n_slc) * SLC_BLOCK
    se = ss + SLC_BLOCK
    ov = np.minimum(ce[:, None], se[None]) - np.maximum(cs[:, None], ss[None])
    return np.clip(ov, 0, None).astype(np.float32) / CMP_BLOCK

def nsa_mixer(q, kv, gates, qk_g, cmp_pe, cmp_w1, cmp_w2):
    b, s, _ = q.shape
    g_, r_, dk = NSA_KV_GROUPS, NSA_REP, HEAD_DIM
    q = rms_norm(q.reshape(b, s, g_, r_, dk), qk_g[0])
    kv = kv.reshape(b, s, 6, g_, dk)
    k_c, v_c, k_s, v_s, k_w, v_w = [kv[:, :, i] for i in range(6)]
    n_cmp = (s - CMP_BLOCK) // CMP_STRIDE + 1
    cidx = np.arange(n_cmp)[:, None] * CMP_STRIDE + np.arange(CMP_BLOCK)[None]

    def compress(t, j):
        blk = t[:, cidx] + cmp_pe[j][None, None, :, None, :]
        flat = blk.transpose(0, 1, 3, 2, 4).reshape(b, n_cmp, g_, CMP_BLOCK * dk)
        return jax.nn.silu(flat @ cmp_w1[j]) @ cmp_w2[j]

    kc = rms_norm(compress(k_c, 0), qk_g[1])
    vc = compress(v_c, 1)
    c_end = jnp.asarray(cidx[:, -1])
    n_slc = s // SLC_BLOCK
    top_n = min(SLC_TOPN, n_slc)
    ks = rms_norm(k_s, qk_g[2]).reshape(b, n_slc, SLC_BLOCK, g_, dk).transpose(0, 3, 1, 2, 4)
    vs = v_s.reshape(b, n_slc, SLC_BLOCK, g_, dk).transpose(0, 3, 1, 2, 4)
    ov = jnp.asarray(overlap_matrix(n_cmp, n_slc))
    pad = ((0, 0), (WIN, 0), (0, 0), (0, 0))
    kw = jnp.pad(rms_norm(k_w, qk_g[3]), pad)
    vw = jnp.pad(v_w, pad)
    scale = HEAD_DIM ** -0.5
    bi = jnp.arange(b)[:, None, None, None]
    gi = jnp.arange(g_)[None, None, :, None]
    jblk = jnp.arange(n_slc)

    def block(i):
        start = i * Q_BLOCK
        qb = lax.dynamic_slice_in_dim(q, start, Q_BLOCK, axis=1)
        t = start + jnp.arange(Q_BLOCK)
        sc = jnp.einsum('bqgrd,bngd->bqgrn', qb, kc).astype(jnp.float32) * scale
        cval = c_end[None, :] <= t[:, None]
        pc = jax.nn.softmax(jnp.where(cval[None, :, None, None, :], sc, NEG), axis=-1)
        pc = pc * jnp.any(cval, axis=-1)[None, :, None, None, None]
        o_c = jnp.einsum('bqgrn,bngd->bqgrd', pc.astype(vc.dtype), vc)
        imp = jnp.einsum('bqgrn,nj->bqgj', pc, ov)
        jt = (t // SLC_BLOCK)[:, None]
        future = jblk[None, :] > jt
        forced = (jblk[None, :] == 0) | (jblk[None, :] == jt) | (jblk[None, :] == jt - 1)
        imp = jnp.where(forced[None, :, None, :], FORCE, jnp.where(future[None, :, None, :], NEG, imp))
        _, idx = lax.top_k(imp, top_n)
        ksel = ks[bi, gi, idx].reshape(b, Q_BLOCK, g_, top_n * SLC_BLOCK, dk)
        vsel = vs[bi, gi, idx].reshape(b, Q_BLOCK, g_, top_n * SLC_BLOCK, dk)
        kpos = (idx[..., None] * SLC_BLOCK + jnp.arange(SLC_BLOCK)).reshape(b, Q_BLOCK, g_, top_n * SLC_BLOCK)
        ss_ = jnp.einsum('bqgrd,bqgkd->bqgrk', qb, ksel).astype(jnp.float32) * scale
        smask = (kpos <= t[None, :, None, None])[:, :, :, None, :]
        ps = jax.nn.softmax(jnp.where(smask, ss_, NEG), axis=-1)
        o_s = jnp.einsum('bqgrk,bqgkd->bqgrd', ps.astype(vsel.dtype), vsel)
        kwb = lax.dynamic_slice_in_dim(kw, start, Q_BLOCK + WIN, axis=1)
        vwb = lax.dynamic_slice_in_dim(vw, start, Q_BLOCK + WIN, axis=1)
        kp = start - WIN + jnp.arange(Q_BLOCK + WIN)
        wmask = (kp[None, :] <= t[:, None]) & (kp[None, :] > t[:, None] - WIN) & (kp[None, :] >= 0)
        sw = jnp.einsum('bqgrd,bkgd->bqgrk', qb, kwb).astype(jnp.float32) * scale
        pw = jax.nn.softmax(jnp.where(wmask[None, :, None, None, :], sw, NEG), axis=-1)
        o_w = jnp.einsum('bqgrk,bkgd->bqgrd', pw.astype(vwb.dtype), vwb)
        return o_c, o_s, o_w

    o_c, o_s, o_w = lax.map(block, jnp.arange(s // Q_BLOCK))

    def unblock(o):
        return o.transpose(1, 0, 2, 3, 4, 5).reshape(b, s, NSA_HEADS, dk)

    gt = jax.nn.sigmoid(gates.reshape(b, s, NSA_HEADS, 3))
    o = gt[..., 0:1] * unblock(o_c) + gt[..., 1:2] * unblock(o_s) + gt[..., 2:3] * unblock(o_w)
    return o.reshape(b, s, NSA_WIDTH)

def pool_mixer(p, w_pool, scale):
    b, s, c = p.shape
    maxw = max(POOL_WINDOWS)
    cs = jnp.pad(jnp.cumsum(p.astype(jnp.float32), axis=1), ((0, 0), (maxw, 0), (0, 0)))
    cnt = jnp.arange(1, s + 1).astype(jnp.float32)
    groups = []
    for gi, w in enumerate(POOL_WINDOWS):
        c0, c1 = gi * POOL_GROUP_DIM, (gi + 1) * POOL_GROUP_DIM
        wsum = cs[:, maxw:, c0:c1] - cs[:, maxw - w:maxw - w + s, c0:c1]
        groups.append(wsum / jnp.minimum(cnt, float(w))[None, :, None])
    pooled = jnp.concatenate(groups, axis=-1).astype(p.dtype) - p
    y = jnp.einsum('bsgc,gcd->bsgd', pooled.reshape(b, s, POOL_GROUPS, POOL_GROUP_DIM), w_pool)
    return y.reshape(b, s, c) * scale

def spatial_gating(z, norm_g, w_s, b_s):
    b, s, _ = z.shape
    z = jax.nn.gelu(z, approximate=False)
    u, v = jnp.split(z, 2, axis=-1)
    v = rms_norm(v, norm_g).reshape(b, s // SGU_CHUNK, SGU_CHUNK, SGU_GROUPS, SGU_GROUP_DIM)
    w = w_s * jnp.tril(jnp.ones((SGU_CHUNK, SGU_CHUNK), w_s.dtype))
    mixed = jnp.einsum('gts,bnsgc->bntgc', w, v) + b_s.T[None, None, :, :, None]
    return u * mixed.reshape(b, s, SGU_WIDTH)

def setup_inputs(seed: int = 0) -> dict:
    key = jax.random.key(seed)
    k = jax.random.split(key, 20)
    f32 = jnp.float32
    nrm = lambda kk, shape: jax.random.normal(kk, shape, f32)
    L = DEPTH
    return {
        'x': nrm(k[0], (BATCH, SEQ, D_MODEL)),
        'norm1_g': 1.0 + 0.1 * nrm(k[1], (L, D_MODEL)),
        'w_in': nrm(k[2], (L, D_MODEL, N_IN)) * D_MODEL ** -0.5,
        'conv_a_w': nrm(k[3], (L, CONV_K, CONV_WIDTH_A)) * CONV_K ** -0.5,
        'qk_norm_g': 1.0 + 0.1 * nrm(k[4], (L, 4, HEAD_DIM)),
        'cmp_pe': 0.5 * nrm(k[5], (L, 2, CMP_BLOCK, HEAD_DIM)),
        'cmp_w1': nrm(k[6], (L, 2, CMP_BLOCK * HEAD_DIM, HEAD_DIM)) * (CMP_BLOCK * HEAD_DIM) ** -0.5,
        'cmp_w2': nrm(k[7], (L, 2, HEAD_DIM, HEAD_DIM)) * HEAD_DIM ** -0.5,
        'pool_w': nrm(k[8], (L, POOL_GROUPS, POOL_GROUP_DIM, POOL_GROUP_DIM)) * POOL_GROUP_DIM ** -0.5,
        'pool_scale': 1.0 + 0.1 * nrm(k[9], (L, POOL_WIDTH)),
        'sgu_norm_g': 1.0 + 0.1 * nrm(k[10], (L, SGU_WIDTH)),
        'sgu_w': nrm(k[11], (L, SGU_GROUPS, SGU_CHUNK, SGU_CHUNK)) * SGU_CHUNK ** -0.5,
        'sgu_b': 1.0 + 0.1 * nrm(k[12], (L, SGU_GROUPS, SGU_CHUNK)),
        'w_branch': nrm(k[13], (L, N_BRANCH, BRANCH_WIDTH, D_MODEL)) * BRANCH_WIDTH ** -0.5,
        'w_o': nrm(k[14], (L, D_MODEL, D_MODEL)) * D_MODEL ** -0.5,
        'norm2_g': 1.0 + 0.1 * nrm(k[15], (L, D_MODEL)),
        'w_up': nrm(k[16], (L, D_MODEL, 2 * D_FF)) * D_MODEL ** -0.5,
        'conv_ff_w': nrm(k[17], (L, FF_CONV_K, D_FF)) * FF_CONV_K ** -0.5,
        'w_down': nrm(k[18], (L, D_FF, D_MODEL)) * D_FF ** -0.5,
    }

def reference(x, norm1_g, w_in, conv_a_w, qk_norm_g, cmp_pe, cmp_w1, cmp_w2, pool_w, pool_scale,
              sgu_norm_g, sgu_w, sgu_b, w_branch, w_o, norm2_g, w_up, conv_ff_w, w_down):
    b, s, d = x.shape
    for l in range(DEPTH):
        h = rms_norm(x, norm1_g[l])
        a_b, a_c, a_x, q, kv, nsa_g, pool_in, sgu_in, merge_g = split_columns(h @ w_in[l])
        out_a = a_b * causal_dwconv(a_c * a_x, conv_a_w[l])
        out_b = nsa_mixer(q, kv, nsa_g, qk_norm_g[l], cmp_pe[l], cmp_w1[l], cmp_w2[l])
        out_c = pool_mixer(pool_in, pool_w[l], pool_scale[l])
        out_d = spatial_gating(sgu_in, sgu_norm_g[l], sgu_w[l], sgu_b[l])
        gm = jax.nn.sigmoid(merge_g.reshape(b, s, N_BRANCH, d))
        merged = (gm[:, :, 0] * (out_a @ w_branch[l, 0]) + gm[:, :, 1] * (out_b @ w_branch[l, 1])
                  + gm[:, :, 2] * (out_c @ w_branch[l, 2]) + gm[:, :, 3] * (out_d @ w_branch[l, 3]))
        x = x + merged @ w_o[l]
        h2 = rms_norm(x, norm2_g[l])
        gate, up = jnp.split(h2 @ w_up[l], 2, axis=-1)
        x = x + (jax.nn.silu(causal_dwconv(gate, conv_ff_w[l])) * up) @ w_down[l]
    return x


_drawn_inputs = setup_inputs


def setup_inputs(seed=0):
    import zlib

    import numpy as np

    out = dict(_drawn_inputs(seed))
    spreads = {}
    factors = {'qk_norm_g': 8.0, 'sgu_norm_g': 2.76}
    for name, (base, spread) in spreads.items():
        noise = np.random.default_rng([zlib.crc32(name.encode()), seed]).standard_normal(out[name].shape)
        drawn = base * np.exp(spread * noise) if base else spread * noise
        out[name] = __import__('jax').numpy.asarray(drawn.astype(out[name].dtype))
    for name, factor in factors.items():
        out[name] = (out[name] * factor).astype(out[name].dtype)
    return out
```

```python
from contextlib import ExitStack

import numpy as np

import concourse.bass as bass
from concourse import mybir

ALU = mybir.AluOpType
ACT = mybir.ActivationFunctionType
F32 = mybir.dt.float32
F32R = mybir.dt.float32r
BF16 = mybir.dt.bfloat16
AX = mybir.AxisListType.X

P = 128
S = 1024
DM = 1024
BW = 512
HD = 64
GROUPS = 2
REP = 4
N_BRANCH = 4
CMP_STRIDE = 16
CMP_BLOCK = 32
WIN = 512
D_FF = 2816
EPS = 1e-6
NEG = -1e30
POOL_WINDOWS = (2, 4, 8, 16)

TT = S // P
KT = DM // P
BK = BW // P
FT = D_FF // P
HALF = 512
NCMP = (S - CMP_BLOCK) // CMP_STRIDE + 1
CW = NCMP + 1
L16 = CMP_BLOCK // 2
KV = GROUPS * HD

COL_CONV = 0
COL_Q = 3 * BW
COL_KV = COL_Q + BW
COL_GATE = COL_KV + 6 * KV
COL_POOL = COL_GATE + 3 * GROUPS * REP
COL_SGU = COL_POOL + BW
COL_MERGE = COL_SGU + 2 * BW

QW = REP * HD
GW = 3 * REP
PW = QW + 6 * HD + GW
SPLITS = 7
CHAIN_TURN = 8 * TT + 11 + 3 * TT + 1

C_G1, C_G2, C_CA = 0, KT, 2 * KT
C_CF = C_CA + 3 * BK
C_PS = C_CF + 3 * FT
CHAN = C_PS + BK
SBUF_BASE = 16512
KB = 1024


class Chain:

    def __init__(self, eng, sem):
        self.eng, self.sem, self.n, self.base, self.at = eng, sem, 0, 0, 0

    def enter(self, i, per_turn):
        self.base, self.at, self.per_turn = i * per_turn, self.n, per_turn

    def leave(self, turns):
        assert self.n - self.at == self.per_turn, (self.n - self.at, self.per_turn)
        self.n, self.base = self.at + turns * self.per_turn, 0

    def mark(self, ins):
        ins.then_inc(self.sem, 1)
        self.n += 1

    def wait(self):
        self.eng.wait_ge(self.sem, self.base + self.n)

    def link(self, ins):
        self.mark(ins)
        self.wait()


STAGES = (("merge1", 16, 16), ("conv", 12, 12), ("merge0", 16, 16), ("pool", 4, 4), ("v", 4, 0), ("merge2", 16, 16),
          ("u", 4, 4), ("merge3", 16, 16), ("wo", 8, 0), ("ff", 2 * FT, 2 * FT))
PIECE = {name: sum(n for _, n, _ in STAGES[:i]) for i, (name, _, _) in enumerate(STAGES)}
CHUNK = {name: sum(n for _, _, n in STAGES[:i]) for i, (name, _, _) in enumerate(STAGES)}


def after(eng, semaphore, base, n):
    if n > 0:
        eng.wait_ge(semaphore, base + n)


def attention_tasks():
    tasks = []
    for i in range(TT):
        first = max(0, i - WIN // P)
        tasks.append((i, "slc", 0, (i + 1) * P, i + 1))
        tasks.append((i, "win", first * P, (i + 1 - first) * P, i + 1 - first))
        tasks.append((i, "cmp", 0, CW, 1))
    return tasks


def attention_steps():
    tasks = attention_tasks()
    unit_of, u = [], 0
    for t in tasks:
        unit_of.append(u)
        u += t[4]
    steps = []
    for n in range(len(tasks) + 2):
        old = n - 2
        units = list(range(tasks[old][4])) if old >= 0 else []
        share = -(-len(units) // REP)
        for r in range(REP):
            mine = units[r * share:(r + 1) * share] if n < len(tasks) else (units if r == 0 else [])
            if n < len(tasks) or mine:
                steps.append((n, r, [(old, j) for j in mine]))
    return tasks, steps, unit_of, u


def build(nc, x, norm1_g, w_in, conv_a_w, qk_norm_g, cmp_pe, cmp_w1, cmp_w2, pool_w, pool_scale,
          sgu_norm_g, sgu_w, sgu_b, w_branch, w_o, norm2_g, w_up, conv_ff_w, w_down, out):
    tasks, steps, unit_of, UNITS = attention_steps()
    NT = len(tasks)
    SS = NT * REP

    with ExitStack() as ctx:
        def place(name, at_kb, shape, dt):
            return nc.alloc_sbuf_tensor_at(name, shape, dt, offset=SBUF_BASE + int(at_kb * KB))

        def sem(name):
            return ctx.enter_context(nc.semaphore(name))

        actT_h = place("actT_h", 0, [P, KT, S], F32R)
        actT_l = place("actT_l", 32, [P, KT, S], F32R)
        outb_h = place("outb_h", 64, [P, BK, S], F32R)
        outb_l = place("outb_l", 80, [P, BK, S], F32R)
        x_in = place("x_in", 64, [P, TT, DM], F32)
        w1 = place("w1", 72, [P, 2, L16, HD], F32)
        kcT = place("kcT", 88, [P, 2, S], F32)
        raw = place("raw", 96, [P, 2, 1024], F32)

        wp_h = place("wp_h", 104, [P, KT, PW], F32R)
        wp_l = place("wp_l", 104 + KT * PW * 4 / KB, [P, KT, PW], F32R)
        p_slc = place("p_slc", 104, [P, REP, S], F32)
        p_win = place("p_win", 120, [P, REP, 640], F32)
        p_cmp = place("p_cmp", 130, [P, REP, CW], F32)
        pT_h = place("pT_h", 131, [P, 2, HALF], F32R)
        pT_l = place("pT_l", 135, [P, 2, HALF], F32R)
        qT = place("qT", 146, [P, REP, S], F32R)
        kAB = place("kAB", 162, [P, 4, S], F32R)
        v_h = place("v_h", 178, [P, 2, TT, HD], F32R)
        v_l = place("v_l", 182, [P, 2, TT, HD], F32R)
        xn = place("xn", 146, [P, 2, DM], F32)
        xv = place("xv", 154, [P, 2, KT, P], F32)
        junk = place("junk", 162, [P, DM], F32)
        proj = place("proj", 186, [P, 2, PW], F32)
        dup = place("dup", 186 + 5.125, [P, 2, 10, P], F32)
        qkn = place("qkn", 186 + 15.125, [P, 6, HD], F32)
        h1 = place("h1", 186, [HD, 2, CW], F32)
        ck = place("ck", 187, [CW, HD], F32)
        ck2 = place("ck2", 187.25, [CW, HD], F32)
        ckd = place("ckd", 187.5, [CW, 2, 2, HD], F32)

        ring_h = place("ring_h", 104, [P, 2, 1024], F32R)
        ring_l = place("ring_l", 112, [P, 2, 1024], F32R)
        merged = place("merged", 120, [P, KT, S], F32)
        x2 = place("x2", 120, [P, TT, DM], F32)
        sig = place("sig", 152, [P, 2, S], F32)
        conv_c = place("conv_c", 160, [P, 2, S], F32)
        conv_u = place("conv_u", 168, [P, 2, S + 2], F32)
        conv_o = place("conv_o", 176.25, [P, 2, S], F32)
        pool_p = place("pool_p", 160, [P, 2, S + 16], F32)
        pool_s = place("pool_s", 168.25, [P, 2, S + 16], F32)
        pool_d = place("pool_d", 176.5, [P, S], F32)
        pool_dh = place("pool_dh", 180.5, [P, S], F32R)
        pool_dl = place("pool_dl", 184.5, [P, S], F32R)
        pool_w32 = place("pool_w32", 188.5, [P, BK, P], F32)
        pool_wh = place("pool_wh", 190.5, [P, BK, P], F32R)
        pool_wl = place("pool_wl", 192.5, [P, BK, P], F32R)
        pool_inv = place("pool_inv", 194.5, [P, BK, 16], F32)
        pool_t16 = place("pool_t16", 194.75, [P, 16], F32)
        wv_h = place("wv_h", 152, [P, KT, BW], F32R)
        wv_l = place("wv_l", 168, [P, KT, BW], F32R)
        sgu_v = place("sgu_v", 184, [P, TT, BW], F32)
        sgu_sq = place("sgu_sq", 200, [P, BW], F32)
        sgu_g = place("sgu_g", 160, [P, BW], F32)
        sgu_bias = place("sgu_bias", 162, [P, BK, P], F32)
        sgu_w32 = place("sgu_w32", 164, [P, BK, P], F32)
        sgu_wh = place("sgu_wh", 166, [P, BK, P], F32R)
        sgu_wl = place("sgu_wl", 200, [P, BK, P], F32R)
        sgu_u = place("sgu_u", 168, [P, BK, S], F32)
        sgu_vh = place("sgu_vh", 152, [P, 2, BW], F32R)
        sgu_vl = place("sgu_vl", 156, [P, 2, BW], F32R)
        sgu_m = [place("sgu_m0", 160, [P, BK, P], F32), place("sgu_m1", 164, [P, BK, P], F32)]
        wo_h = place("wo_h", 64, [P, KT, DM], F32R)
        wo_l = place("wo_l", 152, [P, KT, DM], F32R)
        x2a = place("x2a", 202.5, [P, 4, TT], F32)
        xn2 = place("xn2", 184, [P, 2, DM], F32)
        xv2 = place("xv2", 192, [P, 2, KT, P], F32)
        wd_raw = place("wd_raw", 64, [P, 2, DM], F32)
        wd_h = place("wd_h", 72, [P, 2, DM], F32R)
        wd_l = place("wd_l", 80, [P, 2, DM], F32R)
        ffc = place("ffc", 88, [P, 2, S], F32)
        ffa_h = place("ffa_h", 152, [P, 2, S], F32R)
        ffa_l = place("ffa_l", 160, [P, 2, S], F32R)
        ffg = place("ffg", 168, [P, 2, S + 2], F32)

        cur = [202.75]

        def small(name, shape, dt=F32):
            n = int(np.prod(shape[1:])) * (2 if dt == BF16 else 4)
            t = place(name, cur[0], shape, dt)
            cur[0] += -(-n // 32) * 32 / KB
            assert cur[0] <= 207.8, cur[0]
            return t

        ident = small("ident", [P, P])
        identb = small("identb", [P, P], BF16)
        tri = small("tri", [P, P], BF16)
        wstart = small("wstart", [P, P], BF16)
        cmask = small("cmask", [P, TT, CW], BF16)
        gains = small("gains", [P, 4, HD])
        chan = small("chan", [P, CHAN])
        graw = small("graw", [P, KT, GW])
        glog = small("glog", [P, TT, GW])
        any31 = small("any31", [P, 1])
        ssq = small("ssq", [P, TT])
        xa = small("xa", [P, 2, 4])
        qa = small("qa", [P, 6])
        qr = small("qr", [P, 6])
        qy = small("qy", [P, 6])
        qt = small("qt", [P, 6])
        nmx = small("nmx", [P, 8])
        den = small("den", [P, 3, REP])
        wgt = small("wgt", [P, 3, REP])
        wtmp = small("wtmp", [P, REP])
        peT = small("peT", [P, 2, L16])
        cbias = small("cbias", [HD, 2])
        kcAB = place("kcAB", 139.5, [P, 2, CW], F32R)
        va = place("va", 202.25, [P, 4, TT], F32)
        vc_h = place("vc_h", 144.875, [CW, HD], F32R)
        vc_l = place("vc_l", 145.125, [CW, HD], F32R)
        w2 = place("w2", 145.375, [HD, 2, HD], F32)
        zc = place("zc", 186, [P, 2 * CW], F32)
        chan_rows = place("chan_rows", 187, [CHAN, P], F32)
        pe_rows = place("pe_rows", 187.5, [2 * L16, P], F32)

        bank = ctx.enter_context(nc.psum_tensor("bank", [P, 8, HALF], F32))
        flat = bank[:, :, :].rearrange("p b n -> p (b n)")

        x_loaded = [sem(f"x_loaded{t}") for t in range(TT)]
        const_loaded = sem("const_loaded")
        const2_loaded = sem("const2_loaded")
        w1_loaded = sem("w1_loaded")
        chan_turned = sem("chan_turned")
        chan_done = sem("chan_done")
        consts_made = sem("consts_made")
        sq_done = sem("sq_done")
        xa_done = sem("xa_done")
        xr_done = sem("xr_done")
        xn_done = sem("xn_done")
        xT_done = sem("xT_done")
        xv_done = sem("xv_done")
        xh_done = sem("xh_done")
        xl_done = sem("xl_done")
        raw_loaded = [sem("raw_loaded0"), sem("raw_loaded1")]
        graw_loaded = sem("graw_loaded")
        wph_done = sem("wph_done")
        wpl_done = sem("wpl_done")
        proj_done = sem("proj_done")
        pcopy_done = sem("pcopy_done")
        qa_done = sem("qa_done")
        qr_done = sem("qr_done")
        qn_done = sem("qn_done")
        qkh_done = sem("qkh_done")
        qkl_done = sem("qkl_done")
        qkT_done = sem("qkT_done")
        evq_done = sem("evq_done")
        evk_done = sem("evk_done")
        c_pe = sem("c_pe")
        c_act = sem("c_act")
        c_dve = sem("c_dve")
        glog_done = sem("glog_done")
        gate_done = sem("gate_done")
        s_done = sem("s_done")
        nmx_done = sem("nmx_done")
        exp_done = sem("exp_done")
        wgt_done = sem("wgt_done")
        scaled = sem("scaled")
        t_done = sem("t_done")
        pth_done = sem("pth_done")
        ptl_done = sem("ptl_done")
        pv_done = sem("pv_done")
        oh_done = sem("oh_done")
        ol_done = sem("ol_done")
        piece_loaded = [sem("piece_loaded0"), sem("piece_loaded1")]
        ph_done = sem("ph_done")
        pl_done = sem("pl_done")
        mm_done = sem("mm_done")
        freed = sem("freed")
        sig_done = sem("sig_done")
        acc_done = sem("acc_done")
        convc_done = sem("convc_done")
        obh_done = sem("obh_done")
        obl_done = sem("obl_done")
        poolw_loaded = sem("poolw_loaded")
        poolw_h = sem("poolw_h")
        poolw_l = sem("poolw_l")
        iota_done = sem("iota_done")
        poolp_done = sem("poolp_done")
        poold_done = sem("poold_done")
        pooldh_done = sem("pooldh_done")
        pooldl_done = sem("pooldl_done")
        pooly_mm = sem("pooly_mm")
        v_mm = sem("v_mm")
        gelu_done = sem("gelu_done")
        sguc_loaded = sem("sguc_loaded")
        sguw_masked = sem("sguw_masked")
        va_done = sem("va_done")
        vr_done = sem("vr_done")
        vn_done = sem("vn_done")
        swT_done = sem("swT_done")
        swh_done = sem("swh_done")
        swl_done = sem("swl_done")
        vsh_done = sem("vsh_done")
        vsl_done = sem("vsl_done")
        mix_mm = sem("mix_mm")
        mix_done = sem("mix_done")
        u_done = sem("u_done")
        mgh_done = sem("mgh_done")
        mgl_done = sem("mgl_done")
        x2_loaded = sem("x2_loaded")
        wo_mm = sem("wo_mm")
        x2_done = sem("x2_done")
        gcopy_done = sem("gcopy_done")
        ffc_done = sem("ffc_done")
        silu_done = sem("silu_done")
        ffh_done = sem("ffh_done")
        ffl_done = sem("ffl_done")
        wd_loaded = [sem("wd_loaded0"), sem("wd_loaded1")]
        wdh_done = sem("wdh_done")
        wdl_done = sem("wdl_done")
        d_mm = sem("d_mm")
        d_done = sem("d_done")
        out_done = sem("out_done")
        passed = sem("passed")
        dve_chain = sem("dve_chain")

        w_in_k = w_in[0].rearrange("(k p) n -> p k n", p=P)

        def wp_piece(t, c):
            if c < 2:
                return t[:, 4 * c:4 * c + 4, 0:QW]
            if c < 6:
                return t[:, 2 * (c - 2):2 * (c - 2) + 2, QW:QW + 6 * HD]
            return t[:, :, QW + 6 * HD:PW]

        def raw_piece(c):
            if c < 2:
                return raw[:, c % 2, 0:4 * QW].rearrange("p (k n) -> p k n", k=4)
            if c < 6:
                return raw[:, c % 2, 0:12 * HD].rearrange("p (k n) -> p k n", k=2)
            return graw[:, :, :]

        RAW_AT = {0: 16, 2: 48, 4: 80, 1: 16, 3: 48, 5: 80}

        block = ctx.enter_context(nc.Block())

        @block.sync
        def _(sp):
            sp.dma_start(x_in[:, 0, :], x[0, 0:P, :]).then_inc(x_loaded[0], 16)
            for at, src, n in ((C_G1, norm1_g[0], KT), (C_G2, norm2_g[0], KT), (C_CA, conv_a_w[0].rearrange("j c -> (j c)"), 3 * BK),
                               (C_CF, conv_ff_w[0].rearrange("j c -> (j c)"), 3 * FT), (C_PS, pool_scale[0], BK)):
                sp.dma_start(chan_rows[at:at + n, :], src.rearrange("(k p) -> k p", p=P)).then_inc(const_loaded, 16)
            for j in range(2):
                sp.dma_start(pe_rows[j * L16:(j + 1) * L16, :].rearrange("l (h d) -> l h d", h=2),
                             cmp_pe[0, j].rearrange("(h l) d -> l h d", h=2)).then_inc(const_loaded, 16)
            for t in range(1, TT):
                sp.dma_start(x_in[:, t, :], x[0, t * P:(t + 1) * P, :]).then_inc(x_loaded[t], 16)
            sp.dma_start(gains[:, :, :].rearrange("p a d -> p (a d)"),
                         qk_norm_g[0].rearrange("a d -> (a d)").partition_broadcast(P)).then_inc(const2_loaded, 16)
            sp.dma_start(w2[:, :, :], cmp_w2[0].rearrange("j d e -> d j e")).then_inc(const2_loaded, 16)
            with sp.Fori(0, GROUPS) as g:
                q0 = sp.snap(g * QW + COL_Q)
                kv0 = sp.snap(g * HD)
                ga0 = sp.snap(g * GW + COL_GATE)
                for c in range(6):
                    after(sp, wpl_done, g * SPLITS, c - 1)
                    if c < 2:
                        sp.dma_start(raw_piece(c), w_in_k[:, 4 * c:4 * c + 4, bass.ds(q0, QW)]).then_inc(raw_loaded[c % 2], 16)
                    else:
                        for k in range(2):
                            kt = 2 * (c - 2) + k
                            cols = w_in[0, kt * P:(kt + 1) * P, COL_KV:COL_KV + 6 * KV].rearrange("p (j n) -> p j n", n=KV)
                            sp.dma_start(raw[:, c % 2, k * 6 * HD:(k + 1) * 6 * HD].rearrange("p (j n) -> p j n", j=6),
                                         cols[:, :, bass.ds(kv0, HD)]).then_inc(raw_loaded[c % 2], 16)
                    if c == 0:
                        sp.dma_start(graw[:, :, :], w_in_k[:, :, bass.ds(ga0, GW)]).then_inc(graw_loaded, 16)
                sp.wait_ge(wpl_done, g * SPLITS + SPLITS)
                sp.sem_inc(passed, 1)

            def load(m, slot, dst, src):
                sp.wait_ge(pl_done, m + 1)
                sp.sem_inc(passed, 1)
                sp.dma_start(dst, src).then_inc(piece_loaded[slot], 16)

            def ring_piece(slot, k=KT):
                return raw[:, slot, 0:k * P].rearrange("p (k n) -> p k n", k=k)

            def load_merge(b, turn, m0):
                g0 = [sp_value((turn * 2 + a) * P + (COL_MERGE + b * DM)) for a in range(2)]
                y0 = [sp_value((turn * 2 + a) * P) for a in range(2)]
                wb = w_branch[0, b].rearrange("(k p) n -> p k n", p=P)
                for a in range(2):
                    load(turn * 4 + (m0 + 2 * a), 0, ring_piece(0), w_in_k[:, :, bass.ds(g0[a], P)])
                    load(turn * 4 + (m0 + 2 * a + 1), 1, ring_piece(1, BK), wb[:, :, bass.ds(y0[a], P)])

            def sp_value(v):
                return v if isinstance(v, int) else sp.snap(v)

            with sp.Fori(0, KT // 2) as t:
                load_merge(1, t, PIECE["merge1"])
            for c in range(3 * BK):
                col = (BW, 2 * BW, 0)[c % 3] + (c // 3) * P
                load(PIECE["conv"] + c, c % 2, ring_piece(c % 2), w_in_k[:, :, col:col + P])
            with sp.Fori(0, KT // 2) as t:
                load_merge(0, t, PIECE["merge0"])
            sp.dma_start(pool_w32[:, :, :], pool_w[0].rearrange("g c d -> c g d")).then_inc(poolw_loaded, 16)
            for c in range(BK):
                load(PIECE["pool"] + c, c % 2, ring_piece(c % 2), w_in_k[:, :, COL_POOL + c * P:COL_POOL + (c + 1) * P])
            for c in range(4):
                load(PIECE["v"] + c, c % 2, raw[:, c % 2, :].rearrange("p (k n) -> p k n", k=2),
                     w_in_k[:, 2 * c:2 * c + 2, COL_SGU + BW:COL_SGU + 2 * BW])
            with sp.Fori(0, KT // 2) as t:
                load_merge(2, t, PIECE["merge2"])
            for c in range(BK):
                load(PIECE["u"] + c, c % 2, ring_piece(c % 2), w_in_k[:, :, COL_SGU + c * P:COL_SGU + (c + 1) * P])
            with sp.Fori(0, KT // 2) as t:
                load_merge(3, t, PIECE["merge3"])
            for c in range(KT):
                load(PIECE["wo"] + c, c % 2, raw[:, c % 2, :], w_o[0, c * P:(c + 1) * P, :])
            for t in range(TT):
                sp.wait_ge(mgl_done, t + 1)
                sp.dma_start(x2[:, t, :], x[0, t * P:(t + 1) * P, :]).then_inc(x2_loaded, 16)
                sp.wait_ge(x2_loaded, 16 * (t + 1))
            with sp.Fori(0, FT // 2) as t:
                cols = [sp.snap((t * 2 + a) * P + up * D_FF) for a in range(2) for up in range(2)]
                rows = [sp.snap(t * (2 * P * DM) + a * P * DM) for a in range(2)]
                for c in range(4):
                    load(t * 4 + (PIECE["ff"] + c), c % 2, ring_piece(c % 2),
                         w_up[0].rearrange("(k p) n -> p k n", p=P)[:, :, bass.ds(cols[c], P)])
                for a in range(2):
                    sp.wait_ge(wdl_done, t * 2 + (a + 1))
                    sp.dma_start(wd_raw[:, a, :], w_down[0].rearrange("r n -> (r n)")[bass.ds(rows[a], P * DM)].rearrange("(p n) -> p n", p=P)).then_inc(wd_loaded[a], 16)
            for t in range(TT):
                sp.wait_ge(d_done, 2 + (FT // 2 - 1) * TT + t + 1)
                sp.dma_start(out[0, t * P:(t + 1) * P, :], x2[:, t, :]).then_inc(out_done, 16)
            sp.wait_ge(out_done, 16 * TT)

        @block.gpsimd
        def _(pool):
            nc.gpsimd.memset(ident[:, :], 0.0).then_inc(consts_made, 1)
            nc.gpsimd.memset(tri[:, :], 0.0).then_inc(consts_made, 1)
            nc.gpsimd.memset(wstart[:, :], 0.0).then_inc(consts_made, 1)
            nc.gpsimd.memset(cmask[:, :, :], 0.0).then_inc(consts_made, 1)
            nc.gpsimd.memset(any31[:, :], 1.0).then_inc(consts_made, 1)
            nc.gpsimd.memset(zc[:, :], 0.0).then_inc(consts_made, 1)
            pool.wait_ge(consts_made, 6)
            nc.gpsimd.affine_select(out=ident[:, :], in_=ident[:, :], compare_op=ALU.not_equal, fill=1.0,
                                    base=0, pattern=[[-1, P]], channel_multiplier=1).then_inc(consts_made, 1)
            nc.gpsimd.affine_select(out=tri[:, :], in_=tri[:, :], compare_op=ALU.is_ge, fill=NEG,
                                    base=0, pattern=[[-1, P]], channel_multiplier=1).then_inc(consts_made, 1)
            nc.gpsimd.affine_select(out=wstart[:, :], in_=wstart[:, :], compare_op=ALU.is_gt, fill=NEG,
                                    base=0, pattern=[[1, P]], channel_multiplier=-1).then_inc(consts_made, 1)
            nc.gpsimd.affine_select(out=cmask[:, :, :], in_=cmask[:, :, :], compare_op=ALU.is_ge, fill=NEG,
                                    base=1 - CMP_BLOCK, pattern=[[P, TT], [-CMP_STRIDE, CW]],
                                    channel_multiplier=1).then_inc(consts_made, 1)
            nc.gpsimd.affine_select(out=any31[:, :], in_=any31[:, :], compare_op=ALU.is_ge, fill=0.0,
                                    base=1 - CMP_BLOCK, pattern=[[0, 1]], channel_multiplier=1).then_inc(consts_made, 1)
            pool.wait_ge(consts_made, 11)
            nc.gpsimd.tensor_copy(identb[:, :], ident[:, :]).then_inc(consts_made, 1)

            with pool.Fori(0, GROUPS) as g:
                for n, (i, kind, k0, keys, blocks) in enumerate(tasks):
                    pool.wait_ge(wgt_done, g * NT + n + 1)
                    pool.sem_inc(passed, 1)
                    for r in range(REP):
                        p = {"slc": p_slc, "win": p_win, "cmp": p_cmp}[kind][:, r, 0:keys]
                        nc.gpsimd.tensor_scalar(p, p, wgt[:, n % 3, r:r + 1], None, ALU.mult).then_inc(scaled, 1)

            pool.wait_ge(mm_done, 2 + CHUNK["pool"])
            nc.gpsimd.iota(pool_t16[:, :], pattern=[[1, 16]], base=1, channel_multiplier=0,
                           allow_small_or_imprecise_dtypes=True).then_inc(iota_done, 1)
            pool.wait_ge(v_mm, TT)
            pool.dma_start(sgu_g[:, :], sgu_norm_g[0].partition_broadcast(P)).then_inc(sguc_loaded, 16)
            pool.dma_start(sgu_bias[:, :, :].rearrange("p g t -> p (g t)"),
                           sgu_b[0].rearrange("g t -> (g t)").partition_broadcast(P)).then_inc(sguc_loaded, 16)
            pool.dma_start(sgu_w32[:, :, :], sgu_w[0].rearrange("g t s -> t g s")).then_inc(sguc_loaded, 16)
            pool.wait_ge(sguc_loaded, 48)
            nc.gpsimd.affine_select(out=sgu_w32[:, :, :], in_=sgu_w32[:, :, :], compare_op=ALU.is_ge, fill=0.0,
                                    base=0, pattern=[[0, BK], [-1, P]], channel_multiplier=1).then_inc(sguw_masked, 1)

        @block.scalar
        def _(act):
            for t in range(TT + 2):
                if t < TT:
                    act.wait_ge(x_loaded[t], 16)
                    nc.scalar.activation(junk[:, :], x_in[:, t, :], ACT.Square,
                                         accum_out=ssq[:, t:t + 1]).then_inc(sq_done, 1)
                    act.wait_ge(xa_done, t + 1)
                    nc.scalar.activation(xa[:, t % 2, 1:2], xa[:, t % 2, 0:1], ACT.Sqrt).then_inc(xr_done, 1)
                if 1 <= t <= TT:
                    act.wait_ge(xv_done, t)
                    nc.scalar.activation(actT_h[:, :, (t - 1) * P:t * P], xv[:, (t - 1) % 2, :, :],
                                         ACT.Copy).then_inc(xh_done, 1)
            act.wait_ge(xn_done, TT)
            for j in range(2):
                for half in range(2):
                    rows = cmp_w1[0, j, half * L16 * HD:(half + 1) * L16 * HD, :]
                    act.dma_start(w1[half * HD:(half + 1) * HD, j, :, :],
                                  rows.rearrange("(l d) e -> d l e", d=HD)).then_inc(w1_loaded, 16)

            with act.Fori(0, GROUPS) as g:
                for c in range(SPLITS):
                    if c < 6:
                        act.wait_ge(raw_loaded[c % 2], g * 80 + RAW_AT[c])
                    else:
                        act.wait_ge(graw_loaded, g * 16 + 16)
                    nc.scalar.activation(wp_piece(wp_h, c), raw_piece(c), ACT.Copy).then_inc(wph_done, 1)

                def evacuate_transposes(t):
                    act.wait_ge(qkT_done, g * TT + t + 1)
                    nc.scalar.activation(qT[:, :, t * P:(t + 1) * P],
                                         bank[:, 4, :].rearrange("p (r n) -> p r n", r=REP), ACT.Copy)
                    kc = bank[:, 6, 0:2 * P].rearrange("p (j n) -> p j n", j=2)
                    nc.scalar.activation(kcT[0:HD, :, t * P:(t + 1) * P], kc[0:HD, :, :], ACT.Copy)
                    lo = CMP_STRIDE if t == 0 else 0
                    nc.scalar.activation(kcT[HD:P, :, t * P + lo - CMP_STRIDE:(t + 1) * P - CMP_STRIDE],
                                         kc[HD:P, :, lo:P], ACT.Copy).then_inc(evq_done, 1)

                for t in range(TT + 1):
                    if t < TT:
                        act.wait_ge(proj_done, g * TT + t + 1)
                        after(act, qkl_done, g * TT, t - 1)
                        nc.scalar.activation(proj[:, t % 2, 0:QW], bank[:, 2 * (t % 2), 0:QW], ACT.Copy)
                        nc.scalar.activation(proj[:, t % 2, QW:PW], bank[:, 2 * (t % 2) + 1, 0:PW - QW],
                                             ACT.Copy).then_inc(pcopy_done, 1)
                    if t >= 1:
                        evacuate_transposes(t - 1)
                    if t < TT:
                        act.wait_ge(qa_done, g * TT + t + 1)
                        nc.scalar.activation(qr[:, :], qa[:, :], ACT.Sqrt).then_inc(qr_done, 1)
                        after(act, qkT_done, g * TT, t - 1)
                        act.wait_ge(qn_done, g * TT + t + 1)
                        d = dup[:, t % 2, :, :]
                        nc.scalar.activation(d[:, 0:REP, 0:HD].bitcast(F32R), qkn[:, 0:REP, :], ACT.Copy)
                        kd = d[:, 4:8, :].rearrange("p (t a) (u d) -> p t a u d", a=2, u=2)
                        for ty in range(2):
                            nc.scalar.activation(kd[:, ty, 0, :, :].bitcast(F32R),
                                                 qkn[:, 4 + ty, :].unsqueeze(1).broadcast_to([P, 2, HD]), ACT.Copy)
                        pv = proj[:, t % 2, QW:QW + 6 * HD].rearrange("p (t d) -> p t d", d=HD)
                        cd = d[:, 8:10, :].rearrange("p t (u d) -> p t u d", u=2)
                        nc.scalar.activation(cd, pv[:, 0:2, :].unsqueeze(2).broadcast_to([P, 2, 2, HD]), ACT.Copy)
                        nc.scalar.activation(v_h[:, :, t, :], pv[:, 3:6:2, :], ACT.Copy).then_inc(qkh_done, 1)

                act.wait_ge(c_dve, g * 3 + 1)
                act.wait_ge(c_pe, g * 3 + 1)
                for j in range(2):
                    ins = nc.scalar.activation(h1[:, j, 0:NCMP], bank[0:HD, 7, j * HD:j * HD + NCMP], ACT.Silu,
                                               bias=cbias[:, j:j + 1])
                ins.then_inc(c_act, 1)
                act.wait_ge(c_dve, g * 3 + 2)
                nc.scalar.activation(qr[0:NCMP, 0:1], qa[0:NCMP, 0:1], ACT.Sqrt).then_inc(c_act, 1)
                act.wait_ge(c_pe, g * 3 + 3)
                nc.scalar.activation(kcAB[:, :, 0:NCMP], bank[:, 4, 0:2 * CW].rearrange("p (a n) -> p a n", a=2)[:, :, 0:NCMP],
                                     ACT.Copy).then_inc(c_act, 1)
                act.wait_ge(glog_done, g * TT + TT)
                nc.scalar.activation(glog[:, :, :], glog[:, :, :], ACT.Sigmoid).then_inc(gate_done, 1)

                def high_part(u, old, j):
                    act.wait_ge(t_done, g * UNITS + u + 1)
                    after(act, pv_done, g * UNITS, u - 1)
                    nr = CW if tasks[old][1] == "cmp" else P
                    nc.scalar.activation(pT_h[0:nr, u % 2, :], bank[0:nr, 4 + u % 2, :], ACT.Copy).then_inc(pth_done, 1)

                u = 0
                for n, r, units in steps:
                    if n < NT:
                        i, kind, k0, keys, blocks = tasks[n]
                        s = n * REP + r
                        act.wait_ge(nmx_done, g * SS + s + 1)
                        if r == 0 and n >= 3:
                            act.wait_ge(t_done, g * UNITS + unit_of[n - 3] + tasks[n - 3][4])
                        p = {"slc": p_slc, "win": p_win, "cmp": p_cmp}[kind][:, r, 0:keys]
                        nc.scalar.activation(p, flat[:, (s % 2) * 1024:(s % 2) * 1024 + keys], ACT.Exp,
                                             bias=nmx[:, s % 8:s % 8 + 1], accum_out=den[:, n % 3, r:r + 1]).then_inc(exp_done, 1)
                    for old, j in units:
                        high_part(u, old, j)
                        u += 1
                        if tasks[old][1] == "cmp":
                            i = tasks[old][0]
                            act.wait_ge(pv_done, g * UNITS + u)
                            for par in range(2):
                                src = bank[0:HD, 6 + i % 2, :].rearrange("p (a b n) -> p a b n", a=2, b=2)[:, :, par, :]
                                ins = nc.scalar.activation(outb_h[par * HD:(par + 1) * HD, bass.ds(g * 2, 2), i * P:(i + 1) * P],
                                                           src, ACT.Copy)
                            ins.then_inc(oh_done, 1)
                act.wait_ge(pv_done, g * UNITS + UNITS)

            def high(m, slot, dst, src):
                act.wait_ge(piece_loaded[slot], (m // 2) * 16 + 16 if isinstance(m, int) else m)
                nc.scalar.activation(dst, src, ACT.Copy).then_inc(ph_done, 1)

            def high_ring(turn, per, m, c, slot):
                act.wait_ge(piece_loaded[slot], turn * (per // 2 * 16) + (m // 2 * 16 + 16))
                act.wait_ge(mm_done, turn * per + (c + 1))
                nc.scalar.activation(ring_h[:, slot, :], raw[:, slot, :], ACT.Copy).then_inc(ph_done, 1)

            def merge(b, turn, m0, c0, t0, last=False):
                for a in range(2):
                    for p in (2 * a, 2 * a + 1):
                        if not (last and p == 3):
                            high_ring(turn, 4, m0 + p + 1, c0 + p + 1, (p + 1) % 2)
                        if p == 2 * a:
                            act.wait_ge(mm_done, turn * 4 + (2 + c0 + p + 1))
                            act.wait_ge(acc_done, turn * 2 + (t0 + a + 1))
                            nc.scalar.activation(sig[:, a, :], flat[:, p * 1024:(p + 1) * 1024], ACT.Sigmoid).then_inc(sig_done, 1)

            high_ring(0, 4, 0, 0, 0)
            with act.Fori(0, KT // 2) as t:
                merge(1, t, PIECE["merge1"], CHUNK["merge1"], 0)

            for c in range(3 * BK):
                m, ck_ = PIECE["conv"] + c, CHUNK["conv"] + c
                high_ring(0, 4, m + 1, ck_ + 1, (c + 1) % 2)
                q = c // 3
                if c % 3 == 0:
                    act.wait_ge(mm_done, 2 + ck_ + 1)
                    if q >= 2:
                        act.wait_ge(freed, 4 + ck_ - 6 + 2)
                    nc.scalar.activation(conv_c[:, q % 2, :], flat[:, (ck_ % 4) * 1024:(ck_ % 4 + 1) * 1024], ACT.Copy).then_inc(convc_done, 1)
                if c % 3 == 2:
                    act.wait_ge(freed, 4 + ck_ + 1)
                    nc.scalar.activation(outb_h[:, q, :], conv_o[:, q % 2, :], ACT.Copy).then_inc(obh_done, 1)
            with act.Fori(0, KT // 2) as t:
                merge(0, t, PIECE["merge0"], CHUNK["merge0"], KT)

            act.wait_ge(poolw_loaded, 16)
            nc.scalar.activation(pool_wh[:, :, :], pool_w32[:, :, :], ACT.Copy).then_inc(poolw_h, 1)

            def pool_out(q):
                act.wait_ge(pooly_mm, q + 1)
                nc.scalar.activation(outb_h[:, q, :], flat[:, (2 + q % 2) * 1024:(3 + q % 2) * 1024], ACT.Copy,
                                     scale=chan[:, C_PS + q:C_PS + q + 1]).then_inc(obh_done, 1)

            for q in range(BK):
                m, ck_ = PIECE["pool"] + q, CHUNK["pool"] + q
                if q < BK - 1:
                    high_ring(0, 4, m + 1, ck_ + 1, (q + 1) % 2)
                act.wait_ge(mm_done, 2 + ck_ + 1)
                if q >= 2:
                    act.wait_ge(poold_done, q - 1)
                if q == 0:
                    act.wait_ge(acc_done, 2 + 2 * KT)
                nc.scalar.activation(pool_p[:, q % 2, 16:], flat[:, (q % 2) * 1024:(q % 2 + 1) * 1024], ACT.Copy).then_inc(poolp_done, 1)
                if q >= 1:
                    pool_out(q - 1)
                act.wait_ge(poold_done, q + 1)
                if q >= 1:
                    act.wait_ge(pooly_mm, q)
                nc.scalar.activation(pool_dh[:, :], pool_d[:, :], ACT.Copy).then_inc(pooldh_done, 1)
            pool_out(BK - 1)

            act.wait_ge(obl_done, 2 * BK)
            for c in range(4):
                high(PIECE["v"] + c, c % 2, wv_h[:, 2 * c:2 * c + 2, :], raw[:, c % 2, :].rearrange("p (k n) -> p k n", k=2))
            high_ring(0, 4, PIECE["merge2"], CHUNK["merge2"], 0)
            for t in range(TT):
                act.wait_ge(v_mm, t + 1)
                nc.scalar.activation(sgu_v[:, t, :], bank[:, t, :], ACT.Gelu).then_inc(gelu_done, 1)
            act.wait_ge(va_done, 1)
            nc.scalar.activation(va[:, 1, :], va[:, 0, :], ACT.Sqrt).then_inc(vr_done, 1)
            with act.Fori(0, KT // 2) as t:
                merge(2, t, PIECE["merge2"], CHUNK["merge2"], 2 * KT)
            for q in range(BK):
                m, ck_ = PIECE["u"] + q, CHUNK["u"] + q
                high_ring(0, 4, m + 1, ck_ + 1, (q + 1) % 2)
                act.wait_ge(mm_done, 2 + ck_ + 1)
                nc.scalar.activation(sgu_u[:, q, :], flat[:, (ck_ % 4) * 1024:(ck_ % 4 + 1) * 1024], ACT.Gelu).then_inc(u_done, 1)
            act.wait_ge(swT_done, 1)
            nc.scalar.activation(sgu_wh[:, :, :], bank[:, 4, :].rearrange("p (g t) -> p g t", g=BK), ACT.Copy).then_inc(swh_done, 1)
            act.wait_ge(acc_done, 2 + 3 * KT)
            act.wait_ge(vn_done, TT)
            for t in range(TT + 1):
                if t < TT:
                    if t >= 2:
                        act.wait_ge(mix_mm, t - 1)
                    nc.scalar.activation(sgu_vh[:, t % 2, :], sgu_v[:, t, :], ACT.Copy).then_inc(vsh_done, 1)
                if t >= 1:
                    act.wait_ge(mix_done, t)
                    nc.scalar.activation(outb_h[:, :, (t - 1) * P:t * P], sgu_m[(t - 1) % 2][:, :, :], ACT.Copy).then_inc(obh_done, 1)
            act.wait_ge(mix_mm, TT)
            with act.Fori(0, KT // 2 - 1) as t:
                merge(3, t, PIECE["merge3"], CHUNK["merge3"], 3 * KT)
            merge(3, KT // 2 - 1, PIECE["merge3"], CHUNK["merge3"], 3 * KT, last=True)

            act.wait_ge(mm_done, 2 + CHUNK["ff"])
            for k in range(KT):
                act.wait_ge(acc_done, 2 + 3 * KT + k + 1)
                nc.scalar.activation(actT_h[:, k, :], merged[:, k, :], ACT.Copy).then_inc(mgh_done, 1)
                high(PIECE["wo"] + k, k % 2, wo_h[:, k, :], raw[:, k % 2, :])

            for tg in range(2):
                for t in range(4 * tg, 4 * tg + 4):
                    act.wait_ge(x2_done, t + 1)
                    if t:
                        act.wait_ge(sq_done, TT + t)
                    nc.scalar.activation(xv2[:, 1, :, :].rearrange("p k n -> p (k n)"), x2[:, t, :], ACT.Square,
                                         accum_out=ssq[:, t:t + 1]).then_inc(sq_done, 1)
                act.wait_ge(xa_done, TT + tg + 1)
                nc.scalar.activation(x2a[:, 1, 4 * tg:4 * tg + 4], x2a[:, 0, 4 * tg:4 * tg + 4], ACT.Sqrt).then_inc(xr_done, 1)
            for t in range(TT):
                act.wait_ge(xv_done, TT + t + 1)
                nc.scalar.activation(actT_h[:, :, t * P:(t + 1) * P], xv2[:, t % 2, :, :], ACT.Copy).then_inc(xh_done, 1)
            high_ring(0, 4, PIECE["ff"], CHUNK["ff"], 0)

            def ff(turn, last=False):
                m0, c0 = PIECE["ff"], CHUNK["ff"]
                for a in range(2):
                    high_ring(turn, 4, m0 + 2 * a + 1, c0 + 2 * a + 1, 1)
                    act.wait_ge(mm_done, turn * 4 + (2 + c0 + 2 * a + 1))
                    nc.scalar.activation(ffg[:, a, 2:], flat[:, 0:1024], ACT.Copy).then_inc(gcopy_done, 1)
                    if a == 1:
                        for k in range(2):
                            act.wait_ge(wd_loaded[k], turn * 16 + 16)
                            if not (isinstance(turn, int) and turn == 0):
                                act.wait_ge(d_mm, turn * TT)
                            nc.scalar.activation(wd_h[:, k, :], wd_raw[:, k, :], ACT.Copy).then_inc(wdh_done, 1)
                    if not (last and a == 1):
                        high_ring(turn, 4, m0 + 2 * a + 2, c0 + 2 * a + 2, 0)
                    act.wait_ge(ffc_done, turn * 2 + (a + 1))
                    nc.scalar.activation(ffc[:, a, :], ffc[:, a, :], ACT.Silu).then_inc(silu_done, 1)
                    act.wait_ge(freed, turn * 4 + (4 + c0 + 2 * a + 2))
                    nc.scalar.activation(ffa_h[:, a, :], ffc[:, a, :], ACT.Copy).then_inc(ffh_done, 1)

            ff(0)
            with act.Fori(1, FT // 2 - 1) as t:
                ff(t)
            ff(FT // 2 - 1, last=True)

        @block.vector
        def _(dve):
            ch = Chain(dve, dve_chain)

            def inverse_root(a, root, y, t, n, root_done, count):
                dve.wait_ge(root_done, count)
                ch.link(nc.vector.reciprocal(y, root))
                ch.link(nc.vector.tensor_tensor(t, y, y, ALU.mult))
                ch.link(nc.vector.tensor_tensor(t, t, a, ALU.mult))
                ch.link(nc.vector.tensor_scalar(t, t, -0.5, 1.5, ALU.mult, ALU.add))
                ch.link(nc.vector.tensor_tensor(y, y, t, ALU.mult))

            dve.sem_inc(freed, 4)
            dve.sem_inc(pl_done, 2)
            dve.sem_inc(wdl_done, 2)
            dve.sem_inc(acc_done, 2)
            dve.sem_inc(d_done, 2)
            dve.wait_ge(chan_turned, 1)
            ch.link(nc.vector.tensor_copy(chan[:, :], bank[:, 6, 0:CHAN]))
            nc.vector.tensor_copy(peT[:, :, :], bank[:, 6, CHAN:CHAN + 2 * L16].rearrange("p (j l) -> p j l", j=2)).then_inc(chan_done, 1)
            for t in range(TT + 2):
                if t < TT:
                    dve.wait_ge(sq_done, t + 1)
                    xs = xa[:, t % 2, :]
                    nc.vector.tensor_scalar(xs[:, 0:1], ssq[:, t:t + 1], 1.0 / DM, EPS, ALU.mult, ALU.add).then_inc(xa_done, 1)
                    inverse_root(xs[:, 0:1], xs[:, 1:2], xs[:, 2:3], xs[:, 3:4], 1, xr_done, t + 1)
                    if t >= 2:
                        dve.wait_ge(xT_done, t - 1)
                    nc.vector.tensor_scalar(xn[:, t % 2, :], x_in[:, t, :], xs[:, 2:3], None, ALU.mult).then_inc(xn_done, 1)
                if 1 <= t <= TT:
                    dve.wait_ge(xT_done, t)
                    b = (t - 1) % 2
                    if t >= 3:
                        dve.wait_ge(xl_done, t - 2)
                    src = bank[:, 2 * b:2 * b + 2, :].rearrange("p b (k n) -> p (b k) n", n=P)
                    nc.vector.tensor_tensor(xv[:, b, :, :], src, chan[:, C_G1:C_G1 + KT].unsqueeze(2).broadcast_to([P, KT, P]),
                                            ALU.mult).then_inc(xv_done, 1)
                if t >= 2:
                    b = (t - 2) % 2
                    dve.wait_ge(xh_done, t - 1)
                    cols = slice((t - 2) * P, (t - 1) * P)
                    nc.vector.tensor_tensor(actT_l[:, :, cols], xv[:, b, :, :], actT_h[:, :, cols].bitcast(F32),
                                            ALU.subtract).then_inc(xl_done, 1)
            dve.wait_ge(const2_loaded, 32)
            ch.link(nc.vector.tensor_scalar(gains[:, 0, :], gains[:, 0, :], HD ** -0.5, None, ALU.mult))
            dve.wait_ge(consts_made, 6)
            ch.link(nc.vector.tensor_copy(vc_h[:, :], zc[0:CW, 0:HD]))
            ch.link(nc.vector.tensor_copy(vc_l[:, :], zc[0:CW, 0:HD]))

            with dve.Fori(0, GROUPS) as g:
                ch.enter(g, CHAIN_TURN)
                for c in range(SPLITS):
                    dve.wait_ge(wph_done, g * SPLITS + c + 1)
                    nc.vector.tensor_tensor(wp_piece(wp_l, c), raw_piece(c), wp_piece(wp_h, c).bitcast(F32),
                                            ALU.subtract).then_inc(wpl_done, 1)

                for t in range(TT + 1):
                    if t < TT:
                        dve.wait_ge(pcopy_done, g * TT + t + 1)
                        pr = proj[:, t % 2, :]
                        q = pr[:, 0:QW].rearrange("p (r d) -> p r d", d=HD)
                        kv = pr[:, QW:QW + 6 * HD].rearrange("p (t d) -> p t d", d=HD)
                        k = kv[:, 2:6:2, :]
                        nc.vector.tensor_copy(glog[:, t, :], pr[:, QW + 6 * HD:PW]).then_inc(glog_done, 1)
                        after(dve, qkh_done, g * TT, t)
                        after(dve, qkl_done, g * TT, t)
                        nc.vector.tensor_tensor(qkn[:, 0:4, :], q, q, ALU.mult)
                        ch.link(nc.vector.tensor_tensor(qkn[:, 4:6, :], k, k, ALU.mult))
                        ch.link(nc.vector.tensor_reduce(qt[:, :], qkn[:, :, :], AX, ALU.add))
                        nc.vector.tensor_scalar(qa[:, :], qt[:, :], 1.0 / HD, EPS, ALU.mult, ALU.add).then_inc(qa_done, 1)
                    if t >= 1:
                        dve.wait_ge(qkT_done, g * TT + t)
                        nc.vector.tensor_copy(kAB[:, :, (t - 1) * P:t * P],
                                              bank[:, 5, :].rearrange("p (a n) -> p a n", a=4)).then_inc(evk_done, 1)
                    if t < TT:
                        inverse_root(qa[:, :], qr[:, :], qy[:, :], qt[:, :], 6, qr_done, g * TT + t + 1)
                        nc.vector.tensor_tensor(qkn[:, 0:4, :], q, qy[:, 0:4].unsqueeze(2).broadcast_to([P, 4, HD]), ALU.mult)
                        ch.link(nc.vector.tensor_tensor(qkn[:, 4:6, :], k, qy[:, 4:6].unsqueeze(2).broadcast_to([P, 2, HD]), ALU.mult))
                        nc.vector.tensor_tensor(qkn[:, 0:4, :], qkn[:, 0:4, :], gains[:, 0:1, :].broadcast_to([P, 4, HD]), ALU.mult)
                        nc.vector.tensor_tensor(qkn[:, 4:6, :], qkn[:, 4:6, :], gains[:, 2:4, :], ALU.mult).then_inc(qn_done, 1)
                        dve.wait_ge(qkh_done, g * TT + t + 1)
                        d = dup[:, t % 2, :, :]
                        nc.vector.tensor_tensor(d[:, 0:REP, HD:P], qkn[:, 0:4, :], d[:, 0:REP, 0:HD], ALU.subtract)
                        kd = d[:, 4:8, :].rearrange("p (t a) (u d) -> p t a u d", a=2, u=2)
                        for ty in range(2):
                            nc.vector.tensor_tensor(kd[:, ty, 1, :, :], qkn[:, 4 + ty, :].unsqueeze(1).broadcast_to([P, 2, HD]),
                                                    kd[:, ty, 0, :, :], ALU.subtract)
                        nc.vector.tensor_tensor(v_l[:, :, t, :], kv[:, 3:6:2, :], v_h[:, :, t, :].bitcast(F32),
                                                ALU.subtract).then_inc(qkl_done, 1)

                dve.wait_ge(c_pe, g * 3 + 1)
                nc.vector.tensor_copy(cbias[:, :], bank[0:HD, 7, 128:256:64]).then_inc(c_dve, 1)
                nc.vector.tensor_scalar(kcAB[:, :, NCMP:CW], ident[:, 0:2].unsqueeze(2), 0.0, None, ALU.mult)
                dve.wait_ge(c_pe, g * 3 + 2)
                ch.link(nc.vector.tensor_copy(ck[0:NCMP, :], bank[0:NCMP, 7, 256:256 + HD]))
                nc.vector.tensor_copy(vc_h[0:NCMP, :], bank[0:NCMP, 7, 320:320 + HD])
                ch.link(nc.vector.tensor_tensor(ck2[0:NCMP, :], ck[0:NCMP, :], ck[0:NCMP, :], ALU.mult))
                nc.vector.tensor_tensor(vc_l[0:NCMP, :], bank[0:NCMP, 7, 320:320 + HD], vc_h[0:NCMP, :].bitcast(F32), ALU.subtract)
                ch.link(nc.vector.tensor_reduce(qt[0:NCMP, 0:1], ck2[0:NCMP, :], AX, ALU.add))
                nc.vector.tensor_scalar(qa[0:NCMP, 0:1], qt[0:NCMP, 0:1], 1.0 / HD, EPS, ALU.mult, ALU.add).then_inc(c_dve, 1)
                inverse_root(qa[0:NCMP, 0:1], qr[0:NCMP, 0:1], qy[0:NCMP, 0:1], qt[0:NCMP, 0:1], 1, c_act, g * 3 + 2)
                ch.link(nc.vector.tensor_scalar(ck[0:NCMP, :], ck[0:NCMP, :], qy[0:NCMP, 0:1], None, ALU.mult))
                ch.link(nc.vector.tensor_tensor(ck[0:NCMP, :], ck[0:NCMP, :], gains[0:NCMP, 1, :], ALU.mult))
                twice = ck[0:NCMP, :].unsqueeze(1).broadcast_to([NCMP, 2, HD])
                ch.link(nc.vector.tensor_copy(ckd[0:NCMP, 0, :, :].bitcast(F32R), twice))
                nc.vector.tensor_tensor(ckd[0:NCMP, 1, :, :], twice, ckd[0:NCMP, 0, :, :], ALU.subtract).then_inc(c_dve, 1)

                def weights_of(n):
                    i, kind = tasks[n][0:2]
                    br = ("cmp", "slc", "win").index(kind)
                    dve.wait_ge(exp_done, g * SS + n * REP + REP)
                    ch.link(nc.vector.reciprocal(wtmp[:, :], den[:, n % 3, :]))
                    gate = glog[:, i, :].rearrange("p (r b) -> p r b", b=3)[:, :, br]
                    if kind == "cmp" and i == 0:
                        ch.link(nc.vector.tensor_scalar(wtmp[:, :], wtmp[:, :], any31[:, 0:1], None, ALU.mult))
                    nc.vector.tensor_tensor(wgt[:, n % 3, :], wtmp[:, :], gate, ALU.mult).then_inc(wgt_done, 1)

                dve.wait_ge(gate_done, g + 1)
                u = 0
                for n, r, units in steps:
                    if n < NT:
                        i, kind, k0, keys, blocks = tasks[n]
                        s = n * REP + r
                        dve.wait_ge(s_done, g * SS + s + 1)
                        nc.vector.tensor_reduce(nmx[:, s % 8:s % 8 + 1], flat[:, (s % 2) * 1024:(s % 2) * 1024 + keys],
                                                AX, ALU.max, negate=True).then_inc(nmx_done, 1)
                    if r == 0 and 1 <= n <= NT:
                        weights_of(n - 1)
                    for old, j in units:
                        dve.wait_ge(pth_done, g * UNITS + u + 1)
                        nr = CW if tasks[old][1] == "cmp" else P
                        nc.vector.tensor_tensor(pT_l[0:nr, u % 2, :], bank[0:nr, 4 + u % 2, :],
                                                pT_h[0:nr, u % 2, :].bitcast(F32), ALU.subtract).then_inc(ptl_done, 1)
                        u += 1
                        if tasks[old][1] == "cmp":
                            i = tasks[old][0]
                            dve.wait_ge(oh_done, g * TT + i + 1)
                            for par in range(2):
                                src = bank[0:HD, 6 + i % 2, :].rearrange("p (a b n) -> p a b n", a=2, b=2)[:, :, par, :]
                                rows = slice(par * HD, (par + 1) * HD)
                                ins = nc.vector.tensor_tensor(outb_l[rows, bass.ds(g * 2, 2), i * P:(i + 1) * P], src,
                                                              outb_h[rows, bass.ds(g * 2, 2), i * P:(i + 1) * P].bitcast(F32),
                                                              ALU.subtract)
                            ins.then_inc(ol_done, 1)
                ch.leave(GROUPS)

            def low(turn, per, m, dst, src, hi):
                dve.wait_ge(ph_done, turn * per + (m + 1))
                nc.vector.tensor_tensor(dst, src, hi.bitcast(F32), ALU.subtract).then_inc(pl_done, 1)

            def low_ring(turn, m, slot):
                low(turn, 4, m, ring_l[:, slot, :], raw[:, slot, :], ring_h[:, slot, :])

            def merge(b, turn, m0, c0, t0, last=False):
                for a in range(2):
                    low_ring(turn, m0 + 2 * a + 1, 1)
                    if not (last and a == 1):
                        low_ring(turn, m0 + 2 * a + 2, 0)
                    dve.wait_ge(sig_done, turn * 2 + (t0 + a + 1))
                    dve.wait_ge(mm_done, turn * 4 + (2 + c0 + 2 * a + 2))
                    for h in range(2):
                        o = sig[:, a, h * HALF:(h + 1) * HALF]
                        nc.vector.tensor_tensor(o, o, bank[:, 2 * (2 * a + 1) + h, :], ALU.mult).then_inc(freed, 1)
                    dve.wait_ge(freed, turn * 4 + (4 + c0 + 2 * a + 2))
                    dst = merged[:, bass.ds(turn * 2 + a, 1), :].rearrange("p a n -> p (a n)")
                    if b == 1:
                        nc.vector.tensor_copy(dst, sig[:, a, :]).then_inc(acc_done, 1)
                    else:
                        nc.vector.tensor_tensor(dst, dst, sig[:, a, :], ALU.add).then_inc(acc_done, 1)

            def own(semaphore, value):
                dve.wait_ge(semaphore, value)

            low_ring(0, 0, 0)
            with dve.Fori(0, KT // 2) as t:
                merge(1, t, PIECE["merge1"], CHUNK["merge1"], 0)

            ch.link(nc.vector.memset(conv_u[:, :, 0:2], 0.0))
            for c in range(3 * BK):
                m, ck_ = PIECE["conv"] + c, CHUNK["conv"] + c
                q = c // 3
                low_ring(0, m + 1, (c + 1) % 2)
                ps = flat[:, (ck_ % 4) * 1024:(ck_ % 4 + 1) * 1024]
                u_, o_ = conv_u[:, q % 2, :], conv_o[:, q % 2, :]
                if c % 3 == 1:
                    dve.wait_ge(convc_done, q + 1)
                    dve.wait_ge(mm_done, 2 + ck_ + 1)
                    for h in range(2):
                        nc.vector.tensor_tensor(u_[:, 2 + h * HALF:2 + (h + 1) * HALF], conv_c[:, q % 2, h * HALF:(h + 1) * HALF],
                                                ps[:, h * HALF:(h + 1) * HALF], ALU.mult).then_inc(freed, 1)
                    own(freed, 4 + ck_ + 1)
                    taps = [chan[:, C_CA + j * BK + q:C_CA + j * BK + q + 1] for j in range(3)]
                    if q >= 2:
                        dve.wait_ge(obl_done, q - 1)
                    ch.link(nc.vector.tensor_scalar(o_, u_[:, 0:S], taps[0], None, ALU.mult))
                    ch.link(nc.vector.scalar_tensor_tensor(o_, u_[:, 1:S + 1], taps[1], o_, ALU.mult, ALU.add))
                    ch.link(nc.vector.scalar_tensor_tensor(o_, u_[:, 2:S + 2], taps[2], o_, ALU.mult, ALU.add))
                if c % 3 == 2:
                    dve.wait_ge(mm_done, 2 + ck_ + 1)
                    nc.vector.tensor_tensor(o_, o_, ps, ALU.mult).then_inc(freed, 1)
                    dve.wait_ge(obh_done, q + 1)
                    nc.vector.tensor_tensor(outb_l[:, q, :], o_, outb_h[:, q, :].bitcast(F32), ALU.subtract).then_inc(obl_done, 1)
            with dve.Fori(0, KT // 2) as t:
                merge(0, t, PIECE["merge0"], CHUNK["merge0"], KT)

            dve.wait_ge(poolw_h, 1)
            own(obl_done, BK)
            nc.vector.tensor_tensor(pool_wl[:, :, :], pool_w32[:, :, :], pool_wh[:, :, :].bitcast(F32), ALU.subtract).then_inc(poolw_l, 1)
            dve.wait_ge(iota_done, 1)
            for q, w in enumerate(POOL_WINDOWS):
                ch.link(nc.vector.tensor_scalar(pool_inv[:, q, :], pool_t16[:, :], float(w), None, ALU.min))
            ch.link(nc.vector.reciprocal(pool_inv[:, :, :], pool_inv[:, :, :]))
            ch.link(nc.vector.memset(pool_p[:, :, 0:16], 0.0))
            ch.link(nc.vector.memset(pool_s[:, :, 0:16], 0.0))

            def pool_low(q):
                dve.wait_ge(obh_done, BK + q + 1)
                nc.vector.scalar_tensor_tensor(outb_l[:, q, :], flat[:, (2 + q % 2) * 1024:(3 + q % 2) * 1024],
                                               chan[:, C_PS + q:C_PS + q + 1], outb_h[:, q, :].bitcast(F32),
                                               ALU.mult, ALU.subtract).then_inc(obl_done, 1)

            for q, w in enumerate(POOL_WINDOWS):
                if q < BK - 1:
                    low_ring(0, PIECE["pool"] + q + 1, (q + 1) % 2)
                if q >= 1:
                    pool_low(q - 1)
                dve.wait_ge(poolp_done, q + 1)
                if q == 0:
                    dve.sem_inc(freed, 1)
                else:
                    dve.sem_inc(freed, 1)
                cur_, shift, k = pool_p[:, q % 2, :], 1, 0
                while shift < w:
                    nxt = pool_s[:, k % 2, :]
                    ch.link(nc.vector.tensor_tensor(nxt[:, 16:], cur_[:, 16:], cur_[:, 16 - shift:S + 16 - shift], ALU.add))
                    cur_, shift, k = nxt, shift * 2, k + 1
                p_ = pool_p[:, q % 2, 16:]
                if q >= 1:
                    dve.wait_ge(pooldl_done, q)
                ch.link(nc.vector.scalar_tensor_tensor(pool_d[:, :], cur_[:, 16:], 1.0 / w, p_, ALU.mult, ALU.subtract))
                ch.link(nc.vector.tensor_tensor(pool_t16[:, :], cur_[:, 16:32], pool_inv[:, q, :], ALU.mult))
                nc.vector.tensor_tensor(pool_d[:, 0:16], pool_t16[:, :], p_[:, 0:16], ALU.subtract).then_inc(poold_done, 1)
                dve.wait_ge(pooldh_done, q + 1)
                nc.vector.tensor_tensor(pool_dl[:, :], pool_d[:, :], pool_dh[:, :].bitcast(F32), ALU.subtract).then_inc(pooldl_done, 1)
            pool_low(BK - 1)

            own(obl_done, 2 * BK)
            for c in range(4):
                low(0, 4, PIECE["v"] + c, wv_l[:, 2 * c:2 * c + 2, :], raw[:, c % 2, :].rearrange("p (k n) -> p k n", k=2),
                    wv_h[:, 2 * c:2 * c + 2, :])
            low_ring(0, PIECE["merge2"], 0)
            for t in range(TT):
                dve.wait_ge(gelu_done, t + 1)
                ch.link(nc.vector.tensor_tensor(sgu_sq[:, :], sgu_v[:, t, :], sgu_v[:, t, :], ALU.mult))
                ch.link(nc.vector.tensor_reduce(va[:, 3, t:t + 1], sgu_sq[:, :], AX, ALU.add))
            nc.vector.tensor_scalar(va[:, 0, :], va[:, 3, :], 1.0 / BW, EPS, ALU.mult, ALU.add).then_inc(va_done, 1)
            inverse_root(va[:, 0, :], va[:, 1, :], va[:, 2, :], va[:, 3, :], TT, vr_done, 1)
            dve.wait_ge(sguc_loaded, 48)
            for t in range(TT):
                nc.vector.scalar_tensor_tensor(sgu_v[:, t, :], sgu_v[:, t, :], va[:, 2, t:t + 1], sgu_g[:, :],
                                               ALU.mult, ALU.mult).then_inc(vn_done, 1)
            with dve.Fori(0, KT // 2) as t:
                merge(2, t, PIECE["merge2"], CHUNK["merge2"], 2 * KT)
            for q in range(BK):
                low_ring(0, PIECE["u"] + q + 1, (q + 1) % 2)
                dve.wait_ge(u_done, q + 1)
                dve.sem_inc(freed, 1)
            dve.wait_ge(swh_done, 1)
            nc.vector.tensor_tensor(sgu_wl[:, :, :], bank[:, 4, :].rearrange("p (g t) -> p g t", g=BK),
                                    sgu_wh[:, :, :].bitcast(F32), ALU.subtract).then_inc(swl_done, 1)
            own(vn_done, TT)
            for t in range(TT + 1):
                if t < TT:
                    dve.wait_ge(vsh_done, t + 1)
                    nc.vector.tensor_tensor(sgu_vl[:, t % 2, :], sgu_v[:, t, :], sgu_vh[:, t % 2, :].bitcast(F32),
                                            ALU.subtract).then_inc(vsl_done, 1)
                if t >= 1:
                    k, o = t - 1, sgu_m[(t - 1) % 2][:, :, :]
                    dve.wait_ge(mix_mm, k + 1)
                    if k >= 2:
                        own(obl_done, 2 * BK + k - 1)
                    ch.link(nc.vector.tensor_tensor(o, bank[:, 6 + k % 2, :].rearrange("p (g t) -> p g t", g=BK),
                                                    sgu_bias[:, :, :], ALU.add))
                    nc.vector.tensor_tensor(o, o, sgu_u[:, :, k * P:(k + 1) * P], ALU.mult).then_inc(mix_done, 1)
                    dve.wait_ge(obh_done, 2 * BK + k + 1)
                    nc.vector.tensor_tensor(outb_l[:, :, k * P:(k + 1) * P], o, outb_h[:, :, k * P:(k + 1) * P].bitcast(F32),
                                            ALU.subtract).then_inc(obl_done, 1)
            with dve.Fori(0, KT // 2 - 1) as t:
                merge(3, t, PIECE["merge3"], CHUNK["merge3"], 3 * KT)
            merge(3, KT // 2 - 1, PIECE["merge3"], CHUNK["merge3"], 3 * KT, last=True)

            own(acc_done, 2 + 4 * KT)
            for k in range(KT):
                dve.wait_ge(mgh_done, k + 1)
                nc.vector.tensor_tensor(actT_l[:, k, :], merged[:, k, :], actT_h[:, k, :].bitcast(F32), ALU.subtract).then_inc(mgl_done, 1)
                low(0, 4, PIECE["wo"] + k, wo_l[:, k, :], raw[:, k % 2, :], wo_h[:, k, :])

            def normed(t):
                if t >= 2:
                    dve.wait_ge(xT_done, TT + t - 1)
                nc.vector.tensor_scalar(xn2[:, t % 2, :], x2[:, t, :], x2a[:, 2, t:t + 1], None, ALU.mult).then_inc(xn_done, 1)

            for tg in range(2):
                for t in range(4 * tg, 4 * tg + 4):
                    dve.wait_ge(x2_loaded, 16 * (t + 1))
                    dve.wait_ge(wo_mm, t + 1)
                    nc.vector.tensor_tensor(x2[:, t, :], x2[:, t, :], flat[:, (t % 4) * 1024:(t % 4 + 1) * 1024], ALU.add).then_inc(x2_done, 1)
                dve.wait_ge(sq_done, TT + 4 * tg + 4)
                some = slice(4 * tg, 4 * tg + 4)
                nc.vector.tensor_scalar(x2a[:, 0, some], ssq[:, some], 1.0 / DM, EPS, ALU.mult, ALU.add).then_inc(xa_done, 1)
                inverse_root(x2a[:, 0, some], x2a[:, 1, some], x2a[:, 2, some], x2a[:, 3, some], 4, xr_done, TT + tg + 1)
                if tg == 0:
                    normed(0)
                    normed(1)
            for t in range(TT + 1):
                if t < TT:
                    b = t % 2
                    dve.wait_ge(xT_done, TT + t + 1)
                    if t >= 2:
                        own(xl_done, TT + t - 1)
                    src = bank[:, 2 * b:2 * b + 2, :].rearrange("p b (k n) -> p (b k) n", n=P)
                    nc.vector.tensor_tensor(xv2[:, b, :, :], src, chan[:, C_G2:C_G2 + KT].unsqueeze(2).broadcast_to([P, KT, P]),
                                            ALU.mult).then_inc(xv_done, 1)
                    if t + 2 < TT:
                        normed(t + 2)
                if t >= 1:
                    dve.wait_ge(xh_done, TT + t)
                    cols = slice((t - 1) * P, t * P)
                    nc.vector.tensor_tensor(actT_l[:, :, cols], xv2[:, (t - 1) % 2, :, :], actT_h[:, :, cols].bitcast(F32),
                                            ALU.subtract).then_inc(xl_done, 1)
            low_ring(0, PIECE["ff"], 0)
            ch.link(nc.vector.memset(ffg[:, :, 0:2], 0.0))

            def add_down(turn):
                for t in range(TT):
                    dve.wait_ge(d_mm, (turn - 1) * TT + (t + 1))
                    nc.vector.tensor_tensor(x2[:, t, :], x2[:, t, :], flat[:, (2 + t % 2) * 1024:(3 + t % 2) * 1024],
                                            ALU.add).then_inc(d_done, 1)

            def ff(turn, last=False):
                m0, c0 = PIECE["ff"], CHUNK["ff"]
                for a in range(2):
                    low_ring(turn, m0 + 2 * a + 1, 1)
                    dve.wait_ge(gcopy_done, turn * 2 + (a + 1))
                    dve.sem_inc(freed, 1)
                    g_, o_ = ffg[:, a, :], ffc[:, a, :]
                    taps = [chan[:, bass.ds(turn * 2 + (C_CF + j * FT + a), 1)] for j in range(3)]
                    if not (isinstance(turn, int) and turn == 0):
                        own(ffl_done, (turn - 1) * 2 + (a + 1))
                    ch.link(nc.vector.tensor_scalar(o_, g_[:, 0:S], taps[0], None, ALU.mult))
                    ch.link(nc.vector.scalar_tensor_tensor(o_, g_[:, 1:S + 1], taps[1], o_, ALU.mult, ALU.add))
                    nc.vector.scalar_tensor_tensor(o_, g_[:, 2:S + 2], taps[2], o_, ALU.mult, ALU.add).then_inc(ffc_done, 1)
                    if a == 0 and not (isinstance(turn, int) and turn == 0):
                        add_down(turn)
                    if a == 1:
                        for k in range(2):
                            dve.wait_ge(wdh_done, turn * 2 + (k + 1))
                            nc.vector.tensor_tensor(wd_l[:, k, :], wd_raw[:, k, :], wd_h[:, k, :].bitcast(F32),
                                                    ALU.subtract).then_inc(wdl_done, 1)
                    if not (last and a == 1):
                        low_ring(turn, m0 + 2 * a + 2, 0)
                    dve.wait_ge(silu_done, turn * 2 + (a + 1))
                    dve.wait_ge(mm_done, turn * 4 + (2 + c0 + 2 * a + 2))
                    nc.vector.tensor_tensor(o_, o_, flat[:, 1024:2048], ALU.mult).then_inc(freed, 1)
                    dve.wait_ge(ffh_done, turn * 2 + (a + 1))
                    nc.vector.tensor_tensor(ffa_l[:, a, :], o_, ffa_h[:, a, :].bitcast(F32), ALU.subtract).then_inc(ffl_done, 1)

            ff(0)
            ch_base = ch.n
            with dve.Fori(1, FT // 2 - 1) as t:
                ch.enter(t - 1, 4)
                ff(t)
                ch.leave(FT // 2 - 2)
            ff(FT // 2 - 1, last=True)
            add_down(FT // 2)

        @block.tensor
        def _(pe):
            pe.wait_ge(consts_made, 12)
            pe.wait_ge(const_loaded, 16 * 7)
            nc.tensor.transpose(bank[:, 6, 0:CHAN], chan_rows[:, :], ident[0:CHAN, 0:CHAN])
            nc.tensor.transpose(bank[:, 6, CHAN:CHAN + 2 * L16], pe_rows[:, :], ident[0:2 * L16, 0:2 * L16]).then_inc(chan_turned, 1)
            for t in range(TT):
                pe.wait_ge(xn_done, t + 1)
                if t >= 2:
                    pe.wait_ge(xv_done, t - 1)
                for k in range(KT):
                    ins = nc.tensor.transpose(bank[:, 2 * (t % 2) + k // 4, (k % 4) * P:(k % 4 + 1) * P],
                                              xn[:, t % 2, k * P:(k + 1) * P], ident[:, :])
                ins.then_inc(xT_done, 1)
            pe.wait_ge(xv_done, TT)
            pe.wait_ge(chan_done, 1)

            with pe.Fori(0, GROUPS) as g:
                pe.wait_ge(wpl_done, g * SPLITS + SPLITS)

                def transposes(t):
                    pe.wait_ge(qkl_done, g * TT + t + 1)
                    after(pe, evq_done, g * TT, t)
                    after(pe, evk_done, g * TT, t)
                    for m in range(10):
                        ins = nc.tensor.transpose(bank[:, 4 + m // 4, (m % 4) * P:(m % 4 + 1) * P],
                                                  dup[:, t % 2, m, :], ident[:, :])
                    ins.then_inc(qkT_done, 1)

                for t in range(TT):
                    pe.wait_ge(xl_done, t + 1)
                    after(pe, pcopy_done, g * TT, t - 1)
                    A, B = bank[:, 2 * (t % 2), 0:QW], bank[:, 2 * (t % 2) + 1, 0:PW - QW]
                    for k in range(KT):
                        xh, xl = (a[:, k, t * P:(t + 1) * P] for a in (actT_h, actT_l))
                        first, last = k == 0, k == KT - 1
                        nc.tensor.matmul(A, xh, wp_h[:, k, 0:QW], start=first, stop=False)
                        nc.tensor.matmul(B, xh, wp_h[:, k, QW:PW], start=first, stop=False)
                        nc.tensor.matmul(A, xh, wp_l[:, k, 0:QW], start=False, stop=False)
                        nc.tensor.matmul(B, xh, wp_l[:, k, QW:PW], start=False, stop=False)
                        nc.tensor.matmul(A, xl, wp_h[:, k, 0:QW], start=False, stop=last)
                        ins = nc.tensor.matmul(B, xl, wp_h[:, k, QW:PW], start=False, stop=last)
                    ins.then_inc(proj_done, 1)
                    if t >= 1:
                        transposes(t - 1)
                transposes(TT - 1)

                pe.wait_ge(w1_loaded, 16 * 4)
                pe.wait_ge(evq_done, g * TT + TT)
                for j in range(2):
                    for l in range(L16):
                        nc.tensor.matmul(bank[0:HD, 7, j * HD:j * HD + NCMP], w1[:, j, l, :],
                                         kcT[:, j, l:l + CMP_STRIDE * (NCMP - 1) + 1:CMP_STRIDE],
                                         start=l == 0, stop=l == L16 - 1)
                    for l in range(L16):
                        ins = nc.tensor.matmul(bank[0:HD, 7, 128 + 64 * j:129 + 64 * j], w1[:, j, l, :],
                                               peT[:, j, l:l + 1], start=l == 0, stop=l == L16 - 1)
                ins.then_inc(c_pe, 1)
                pe.wait_ge(c_act, g * 3 + 1)
                pe.wait_ge(const2_loaded, 32)
                pe.sem_inc(passed, 1)
                for j in range(2):
                    ins = nc.tensor.matmul(bank[0:NCMP, 7, 256 + j * HD:256 + (j + 1) * HD], h1[:, j, 0:NCMP],
                                           w2[:, j, :], start=True, stop=True)
                ins.then_inc(c_pe, 1)
                pe.wait_ge(c_dve, g * 3 + 3)
                pe.sem_inc(passed, 1)
                for a in range(2):
                    ins = nc.tensor.transpose(bank[:, 4, a * CW:a * CW + NCMP],
                                              ckd[0:NCMP, a, :, :].rearrange("n u d -> n (u d)"), ident[0:NCMP, 0:NCMP])
                ins.then_inc(c_pe, 1)
                pe.wait_ge(c_act, g * 3 + 3)

                def scores(n, r):
                    i, kind, k0, keys, blocks = tasks[n]
                    s = n * REP + r
                    after(pe, exp_done, g * SS, s - 1)
                    qrow = qT[:, r, i * P:(i + 1) * P]
                    base = (s % 2) * 1024
                    for c in range(0, keys, HALF):
                        w = min(HALF, keys - c)
                        o = flat[:, base + c:base + c + w]
                        if kind == "cmp":
                            kh, kl = kcAB[:, 0, :], kcAB[:, 1, :]
                        else:
                            ty = 0 if kind == "slc" else 1
                            kh, kl = (kAB[:, 2 * ty + a, k0 + c:k0 + c + w] for a in range(2))
                        masks = []
                        if kind == "cmp":
                            masks.append((0, CW, cmask[:, i, :]))
                        else:
                            if kind == "win" and i >= WIN // P and c == 0:
                                masks.append((0, P, wstart[:, :]))
                            if c + w == keys:
                                masks.append((w - P, P, tri[:, :]))
                        nc.tensor.matmul(o, qrow, kh, start=True, stop=False)
                        ins = nc.tensor.matmul(o, qrow, kl, start=False, stop=not masks)
                        for m, (at, mw, mask) in enumerate(masks):
                            ins = nc.tensor.matmul(flat[:, base + c + at:base + c + at + mw], identb[:, :], mask,
                                                   start=False, stop=m == len(masks) - 1)
                    ins.then_inc(s_done, 1)

                def turn(u, old, j):
                    kind = tasks[old][1]
                    after(pe, ptl_done, g * UNITS, u - 1)
                    if j == 0:
                        pe.wait_ge(scaled, g * SS + old * REP + REP)
                    pe.sem_inc(passed, 1)
                    nr = CW if kind == "cmp" else P
                    p = {"slc": p_slc, "win": p_win, "cmp": p_cmp}[kind]
                    for r in range(REP):
                        ins = nc.tensor.transpose(bank[0:nr, 4 + u % 2, r * P:(r + 1) * P],
                                                  p[:, r, j * P:j * P + nr], ident[:, :])
                    ins.then_inc(t_done, 1)

                def values(u, old, j):
                    i, kind, k0, keys, blocks = tasks[old]
                    pe.wait_ge(ptl_done, g * UNITS + u + 1)
                    if kind == "slc" and j == 0:
                        after(pe, ol_done, g * TT, i - 1)
                    if kind == "cmp":
                        nr, vh, vl = CW, vc_h[:, :], vc_l[:, :]
                        pe.sem_inc(passed, 1)
                    else:
                        ty = 0 if kind == "slc" else 1
                        nr, vh, vl = P, v_h[:, ty, k0 // P + j, :], v_l[:, ty, k0 // P + j, :]
                    o = bank[0:HD, 6 + i % 2, :]
                    nc.tensor.matmul(o, vh, pT_h[0:nr, u % 2, :], start=kind == "slc" and j == 0, stop=False)
                    nc.tensor.matmul(o, vh, pT_l[0:nr, u % 2, :], start=False, stop=False)
                    nc.tensor.matmul(o, vl, pT_h[0:nr, u % 2, :], start=False, stop=kind == "cmp").then_inc(pv_done, 1)

                u, waiting = 0, None
                for n, r, units in steps:
                    if n < NT:
                        scores(n, r)
                    for old, j in units:
                        turn(u, old, j)
                        if waiting:
                            values(*waiting)
                        waiting = (u, old, j)
                        if tasks[old][1] == "cmp":
                            values(*waiting)
                            waiting = None
                        u += 1
                pe.wait_ge(exp_done, g * SS + SS)
                pe.wait_ge(ol_done, g * TT + TT)

            def product(k_tiles, wh, wl, ah, al, out_bank):
                for h in range(2):
                    cols = slice(h * HALF, (h + 1) * HALF)
                    for k in range(k_tiles):
                        o = bank[:, out_bank + h, :]
                        nc.tensor.matmul(o, wh(k), ah[:, k, cols], start=k == 0, stop=False)
                        nc.tensor.matmul(o, wh(k), al[:, k, cols], start=False, stop=False)
                        ins = nc.tensor.matmul(o, wl(k), ah[:, k, cols], start=False, stop=k == k_tiles - 1)
                return ins

            def chunk(turn, m, c, slot, k_tiles, ah, al, tile):
                pe.wait_ge(pl_done, turn * 4 + (2 + m + 1))
                pe.wait_ge(freed, turn * 4 + (c + 1))
                product(k_tiles, lambda k: ring_h[:, slot, k * P:(k + 1) * P], lambda k: ring_l[:, slot, k * P:(k + 1) * P],
                        ah, al, 2 * tile).then_inc(mm_done, 1)

            def merge(turn, m0, c0, branch_ready):
                for a in range(2):
                    chunk(turn, m0 + 2 * a, c0 + 2 * a, 0, KT, actT_h, actT_l, 2 * a)
                    if branch_ready:
                        pe.wait_ge(obl_done, branch_ready)
                    chunk(turn, m0 + 2 * a + 1, c0 + 2 * a + 1, 1, BK, outb_h, outb_l, 2 * a + 1)

            pe.sem_inc(mm_done, 2)
            with pe.Fori(0, KT // 2) as t:
                merge(t, PIECE["merge1"], CHUNK["merge1"], 0)
            for c in range(3 * BK):
                chunk(0, PIECE["conv"] + c, CHUNK["conv"] + c, c % 2, KT, actT_h, actT_l, (CHUNK["conv"] + c) % 4)
            with pe.Fori(0, KT // 2) as t:
                merge(t, PIECE["merge0"], CHUNK["merge0"], BK)

            def pool_product(q):
                pe.wait_ge(poolw_l, 1)
                pe.wait_ge(pooldl_done, q + 1)
                if q < 2:
                    pe.wait_ge(freed, 4 + CHUNK["pool"] - 2 + q + 1)
                else:
                    pe.wait_ge(obl_done, BK + q - 1)
                for h in range(2):
                    cols = slice(h * HALF, (h + 1) * HALF)
                    o = bank[:, 2 * (2 + q % 2) + h, :]
                    nc.tensor.matmul(o, pool_wh[:, q, :], pool_dh[:, cols], start=True, stop=False)
                    nc.tensor.matmul(o, pool_wh[:, q, :], pool_dl[:, cols], start=False, stop=False)
                    ins = nc.tensor.matmul(o, pool_wl[:, q, :], pool_dh[:, cols], start=False, stop=True)
                ins.then_inc(pooly_mm, 1)

            for q in range(BK):
                ready = CHUNK["pool"] + q - (4 if q < 2 else 2)
                pe.wait_ge(freed, 4 + ready + 1)
                chunk(0, PIECE["pool"] + q, CHUNK["pool"] + q, q % 2, KT, actT_h, actT_l, q % 2)
                if q >= 1:
                    pool_product(q - 1)
            pool_product(BK - 1)

            pe.wait_ge(pl_done, 2 + PIECE["v"] + 4)
            pe.wait_ge(freed, 4 + CHUNK["merge2"])
            for t in range(TT):
                if t >= 4:
                    pe.wait_ge(obl_done, 2 * BK)
                for k in range(KT):
                    xh, xl = (a[:, k, t * P:(t + 1) * P] for a in (actT_h, actT_l))
                    nc.tensor.matmul(bank[:, t, :], xh, wv_h[:, k, :], start=k == 0, stop=False)
                    nc.tensor.matmul(bank[:, t, :], xh, wv_l[:, k, :], start=False, stop=False)
                    ins = nc.tensor.matmul(bank[:, t, :], xl, wv_h[:, k, :], start=False, stop=k == KT - 1)
                ins.then_inc(v_mm, 1)
            pe.wait_ge(gelu_done, TT)
            with pe.Fori(0, KT // 2) as t:
                merge(t, PIECE["merge2"], CHUNK["merge2"], 2 * BK)
            for q in range(BK):
                chunk(0, PIECE["u"] + q, CHUNK["u"] + q, q % 2, KT, actT_h, actT_l, q)
            pe.wait_ge(sguw_masked, 1)
            pe.wait_ge(freed, 4 + CHUNK["merge3"])
            for g4 in range(BK):
                ins = nc.tensor.transpose(bank[:, 4, g4 * P:(g4 + 1) * P], sgu_w32[:, g4, :], ident[:, :])
            ins.then_inc(swT_done, 1)
            pe.wait_ge(swl_done, 1)
            for t in range(TT):
                pe.wait_ge(vsl_done, t + 1)
                if t >= 2:
                    pe.wait_ge(mix_done, t - 1)
                for g4 in range(BK):
                    o = bank[:, 6 + t % 2, g4 * P:(g4 + 1) * P]
                    vh, vl = (a[:, t % 2, g4 * P:(g4 + 1) * P] for a in (sgu_vh, sgu_vl))
                    nc.tensor.matmul(o, vh, sgu_wh[:, g4, :], start=True, stop=False)
                    nc.tensor.matmul(o, vh, sgu_wl[:, g4, :], start=False, stop=False)
                    ins = nc.tensor.matmul(o, vl, sgu_wh[:, g4, :], start=False, stop=True)
                ins.then_inc(mix_mm, 1)
            with pe.Fori(0, KT // 2) as t:
                merge(t, PIECE["merge3"], CHUNK["merge3"], 2 * BK + TT)

            for tg in range(2):
                for k in range(KT):
                    if tg == 0:
                        pe.wait_ge(mgl_done, k + 1)
                        pe.wait_ge(pl_done, 2 + PIECE["wo"] + k + 1)
                        if k == 0:
                            pe.wait_ge(freed, 4 + CHUNK["ff"])
                    for tl in range(4):
                        t = 4 * tg + tl
                        if tg == 1 and k == 0:
                            pe.wait_ge(x2_done, tl + 1)
                        mh, ml = (a[:, k, t * P:(t + 1) * P] for a in (actT_h, actT_l))
                        o = [bank[:, 2 * tl + h, :] for h in range(2)]
                        w = [[a[:, k, h * HALF:(h + 1) * HALF] for h in range(2)] for a in (wo_h, wo_l)]
                        first, last = k == 0, k == KT - 1
                        for h in range(2):
                            nc.tensor.matmul(o[h], mh, w[0][h], start=first, stop=False)
                        for h in range(2):
                            nc.tensor.matmul(o[h], mh, w[1][h], start=False, stop=False)
                        for h in range(2):
                            ins = nc.tensor.matmul(o[h], ml, w[0][h], start=False, stop=last)
                        if last:
                            ins.then_inc(wo_mm, 1)
            for t in range(TT):
                pe.wait_ge(xn_done, TT + t + 1)
                pe.wait_ge(x2_done, min(t + 5, TT))
                if t >= 2:
                    pe.wait_ge(xv_done, TT + t - 1)
                for k in range(KT):
                    ins = nc.tensor.transpose(bank[:, 2 * (t % 2) + k // 4, (k % 4) * P:(k % 4 + 1) * P],
                                              xn2[:, t % 2, k * P:(k + 1) * P], ident[:, :])
                ins.then_inc(xT_done, 1)
            pe.wait_ge(xl_done, 2 * TT)

            def down(turn):
                pe.wait_ge(ffl_done, turn * 2)
                pe.wait_ge(wdl_done, turn * 2 + 2)
                for t in range(TT):
                    pe.wait_ge(d_done, (turn - 1) * TT + (t + 1))
                    o = [bank[:, 4 + 2 * (t % 2) + h, :] for h in range(2)]
                    for k in range(2):
                        ah, al = (a[:, k, t * P:(t + 1) * P] for a in (ffa_h, ffa_l))
                        for n, (av, w) in enumerate(((ah, wd_h), (ah, wd_l), (al, wd_h))):
                            for h in range(2):
                                ins = nc.tensor.matmul(o[h], av, w[:, k, h * HALF:(h + 1) * HALF],
                                                       start=k == 0 and n == 0, stop=k == 1 and n == 2)
                    ins.then_inc(d_mm, 1)

            def ff(turn):
                m0, c0 = PIECE["ff"], CHUNK["ff"]
                for c in range(4):
                    if not (isinstance(turn, int) and turn == 0 and c < 2):
                        pe.wait_ge(freed, turn * 4 + (4 + c0 + c - 1))
                    chunk(turn, m0 + c, c0 + c, c % 2, KT, actT_h, actT_l, c % 2)
                    if c == 0 and not (isinstance(turn, int) and turn == 0):
                        down(turn)

            ff(0)
            with pe.Fori(1, FT // 2 - 1) as t:
                ff(t)
            ff(FT // 2 - 1)
            down(FT // 2)


_INS = ["x", "norm1_g", "w_in", "conv_a_w", "qk_norm_g", "cmp_pe", "cmp_w1", "cmp_w2", "pool_w", "pool_scale",
        "sgu_norm_g", "sgu_w", "sgu_b", "w_branch", "w_o", "norm2_g", "w_up", "conv_ff_w", "w_down"]


def kernel(**inputs):
    import concourse.bacc as bacc
    from concourse.bass_utils import run_bass_kernel_spmd as run

    nc = bacc.Bacc("TRN2", target_bir_lowering=False, num_devices=1)
    arrays, args = {}, []
    for name in _INS:
        a = np.ascontiguousarray(inputs[name])
        arrays[f"in_{name}"] = a
        args.append(nc.dram_tensor(f"in_{name}", a.shape, mybir.dt.from_np(a.dtype), kind="ExternalInput").ap())
    args.append(nc.dram_tensor("out_0", (1, S, DM), F32, kind="ExternalOutput").ap())
    build(nc, *args)
    return run(nc, [arrays], core_ids=[0]).results[0]["out_0"]
```

```python
from contextlib import ExitStack

import numpy as np

import concourse.bass as bass
from concourse import mybir

ALU = mybir.AluOpType
ACT = mybir.ActivationFunctionType
F32 = mybir.dt.float32
F32R = mybir.dt.float32r
BF16 = mybir.dt.bfloat16
AX = mybir.AxisListType.X

P = 128
S = 1024
DM = 1024
BW = 512
HD = 64
GROUPS = 2
REP = 4
N_BRANCH = 4
CMP_STRIDE = 16
CMP_BLOCK = 32
WIN = 512
D_FF = 2816
EPS = 1e-6
NEG = -1e30
POOL_WINDOWS = (2, 4, 8, 16)

TT = S // P
KT = DM // P
BK = BW // P
FT = D_FF // P
HALF = 512
NCMP = (S - CMP_BLOCK) // CMP_STRIDE + 1
CW = NCMP + 1
L16 = CMP_BLOCK // 2
KV = GROUPS * HD

COL_CONV = 0
COL_Q = 3 * BW
COL_KV = COL_Q + BW
COL_GATE = COL_KV + 6 * KV
COL_POOL = COL_GATE + 3 * GROUPS * REP
COL_SGU = COL_POOL + BW
COL_MERGE = COL_SGU + 2 * BW

QW = REP * HD
GW = 3 * REP
PW = QW + 6 * HD + GW
SPLITS = 7
CHAIN_TURN = 8 * TT + 11 + 2 * 3 * TT + 1

C_G1, C_G2, C_CA = 0, KT, 2 * KT
C_CF = C_CA + 3 * BK
C_PS = C_CF + 3 * FT
CHAN = C_PS + BK
SBUF_BASE = 16512
KB = 1024


class Chain:

    def __init__(self, eng, sem):
        self.eng, self.sem, self.n, self.base, self.at = eng, sem, 0, 0, 0

    def enter(self, i, per_turn):
        self.base, self.at, self.per_turn = i * per_turn, self.n, per_turn

    def leave(self, turns):
        assert self.n - self.at == self.per_turn, (self.n - self.at, self.per_turn)
        self.n, self.base = self.at + turns * self.per_turn, 0

    def mark(self, ins):
        ins.then_inc(self.sem, 1)
        self.n += 1

    def wait(self):
        self.eng.wait_ge(self.sem, self.base + self.n)

    def link(self, ins):
        self.mark(ins)
        self.wait()


STAGES = (("merge1", 16, 16), ("conv", 12, 12), ("merge0", 16, 16), ("pool", 4, 4), ("v", 4, 0), ("merge2", 16, 16),
          ("u", 4, 4), ("merge3", 16, 16), ("wo", 8, 0), ("ff", 2 * FT, 2 * FT))
PIECE = {name: sum(n for _, n, _ in STAGES[:i]) for i, (name, _, _) in enumerate(STAGES)}
CHUNK = {name: sum(n for _, _, n in STAGES[:i]) for i, (name, _, _) in enumerate(STAGES)}


def after(eng, semaphore, base, n):
    if n > 0:
        eng.wait_ge(semaphore, base + n)


TILE_ORDER = [7, 0, 6, 1, 5, 2, 4, 3]
COMPRESS = (1, 4, 8)


def attention_tasks():
    tasks = []
    for i in TILE_ORDER:
        first = max(0, i - WIN // P)
        tasks.append((i, "slc", 0, (i + 1) * P, i + 1))
        tasks.append((i, "win", first * P, (i + 1 - first) * P, i + 1 - first))
        tasks.append((i, "cmp", 0, CW, 1))
    return tasks


def attention_pieces(keys):
    pieces = []
    for c in range(0, keys, HALF):
        w = min(HALF, keys - c)
        heads = min(REP, HALF // w)
        heads = REP if heads == REP else 2 if heads >= 2 else 1
        pieces += [(r, heads, c, w) for r in range(0, REP, heads)]
    return pieces


LAG = 3
LEAD = 12
RING = 4
MAXIMA = 6


def attention_slots(tasks):
    units = [(n, j) for n, t in enumerate(tasks) for j in range(t[4])]
    pieces = [(n,) + p for n, t in enumerate(tasks) for p in attention_pieces(t[3])]
    first_unit = [units.index((n, 0)) for n in range(len(tasks))]
    last_unit = [first_unit[n] + tasks[n][4] - 1 for n in range(len(tasks))]
    slots, at = [], 0
    for u in range(len(units) + LAG + 4):
        slot = dict(n=u, pieces=[], unit=None, values=None, turn=None, sum=None, final=None, evacuate=None)
        ahead = units[min(u, len(units) - 1)][0] + MAXIMA - 1
        while at < len(pieces) and pieces[at][0] <= ahead and (tasks[pieces[at][0]][1] != "cmp" or u > COMPRESS[2]) and (at <= u + LEAD or first_unit[pieces[at][0]] <= u + 3):
            slot["pieces"].append((at,) + pieces[at])
            at += 1
        if u < len(units):
            slot["unit"] = (u,) + units[u]
        if LAG <= u < len(units) + LAG:
            slot["values"] = (u - LAG,) + units[u - LAG]
        for n, last in enumerate(last_unit):
            if last + LAG == u:
                slot["evacuate"] = n
            if last + LAG + 1 == u:
                slot["turn"] = n
            if last + LAG + 2 == u and n % 3 == 2:
                slot["sum"] = n // 3
            if last + LAG + 3 == u and n % 3 == 2:
                slot["final"] = n // 3
        slots.append(slot)
    assert at == len(pieces)
    return slots, last_unit, len(units), len(pieces)


def build(nc, x, norm1_g, w_in, conv_a_w, qk_norm_g, cmp_pe, cmp_w1, cmp_w2, pool_w, pool_scale,
          sgu_norm_g, sgu_w, sgu_b, w_branch, w_o, norm2_g, w_up, conv_ff_w, w_down, out):
    tasks = attention_tasks()
    slots, last_unit, UNITS, PIECES = attention_slots(tasks)
    NT = len(tasks)
    piece_end = [0] * NT
    for slot in slots:
        for at, n, *_ in slot["pieces"]:
            piece_end[n] = at + 1
    wide = [n for n, t in enumerate(tasks) if t[3] > HALF]
    both_at, BOTH = {n: k for k, n in enumerate(wide)}, len(wide)
    BRANCH = {"cmp": 0, "slc": 1, "win": 2}

    with ExitStack() as ctx:
        def place(name, at_kb, shape, dt):
            return nc.alloc_sbuf_tensor_at(name, shape, dt, offset=SBUF_BASE + int(at_kb * KB))

        def sem(name):
            return ctx.enter_context(nc.semaphore(name))

        actT_h = place("actT_h", 0, [P, KT, S], F32R)
        actT_l = place("actT_l", 32, [P, KT, S], F32R)
        outb_h = place("outb_h", 64, [P, BK, S], F32R)
        outb_l = place("outb_l", 80, [P, BK, S], F32R)
        x_in = place("x_in", 64, [P, TT, DM], F32)
        w1 = place("w1", 72, [P, 2, L16, HD], F32)
        kcT = place("kcT", 88, [P, 2, S], F32)
        raw = place("raw", 96, [P, 2, 1024], F32)

        wp_h = place("wp_h", 104, [P, KT, PW], F32R)
        wp_l = place("wp_l", 104 + KT * PW * 4 / KB, [P, KT, PW], F32R)
        pT = place("pT", 104, [P, RING, HALF], F32)
        pT_h = place("pT_h", 112, [P, RING, HALF], F32R)
        pT_l = place("pT_l", 120, [P, RING, HALF], F32R)
        shift = place("shift", 190, [P, MAXIMA, REP, P], F32R)
        oT = place("oT", 136, [HD + 1, 2, HALF], F32)
        o_gated = place("o_gated", 140.5, [P, 4, REP * HD], F32)
        qT = place("qT", 146, [P, REP, S], F32R)
        kAB = place("kAB", 162, [P, 4, S], F32R)
        v_h = place("v_h", 178, [P, 2, TT, HD + 1], F32R)
        v_l = place("v_l", 182.0625, [P, 2, TT, HD + 1], F32R)
        xn = place("xn", 146, [P, 2, DM], F32)
        xv = place("xv", 154, [P, 2, KT, P], F32)
        junk = place("junk", 162, [P, DM], F32)
        proj = place("proj", 186.125, [P, 2, PW], F32)
        dup = place("dup", 191.25, [P, 2, 10, P], F32)
        qkn = place("qkn", 201.25, [P, 6, HD], F32)
        ones = place("ones", 189, [P, P], F32R)
        h1 = place("h1", 186.25, [HD, 2, CW], F32)
        ck = place("ck", 187, [CW, HD], F32)
        ck2 = place("ck2", 187.25, [CW, HD], F32)
        ckd = place("ckd", 187.5, [CW, 2, 2, HD], F32)

        ring_h = place("ring_h", 104, [P, 2, 1024], F32R)
        ring_l = place("ring_l", 112, [P, 2, 1024], F32R)
        merged = place("merged", 120, [P, KT, S], F32)
        x2 = place("x2", 120, [P, TT, DM], F32)
        sig = place("sig", 152, [P, 2, S], F32)
        conv_c = place("conv_c", 160, [P, 2, S], F32)
        conv_u = place("conv_u", 168, [P, 2, S + 2], F32)
        conv_o = place("conv_o", 176.25, [P, 2, S], F32)
        pool_p = place("pool_p", 160, [P, 2, S + 16], F32)
        pool_s = place("pool_s", 168.25, [P, 2, S + 16], F32)
        pool_d = place("pool_d", 176.5, [P, S], F32)
        pool_dh = place("pool_dh", 180.5, [P, S], F32R)
        pool_dl = place("pool_dl", 184.5, [P, S], F32R)
        pool_w32 = place("pool_w32", 188.5, [P, BK, P], F32)
        pool_wh = place("pool_wh", 190.5, [P, BK, P], F32R)
        pool_wl = place("pool_wl", 192.5, [P, BK, P], F32R)
        pool_inv = place("pool_inv", 194.5, [P, BK, 16], F32)
        pool_t16 = place("pool_t16", 194.75, [P, 16], F32)
        wv_h = place("wv_h", 152, [P, KT, BW], F32R)
        wv_l = place("wv_l", 168, [P, KT, BW], F32R)
        sgu_v = place("sgu_v", 184, [P, TT, BW], F32)
        sgu_sq = place("sgu_sq", 200, [P, BW], F32)
        sgu_g = place("sgu_g", 160, [P, BW], F32)
        sgu_bias = place("sgu_bias", 162, [P, BK, P], F32)
        sgu_w32 = place("sgu_w32", 164, [P, BK, P], F32)
        sgu_wh = place("sgu_wh", 166, [P, BK, P], F32R)
        sgu_wl = place("sgu_wl", 200, [P, BK, P], F32R)
        sgu_u = place("sgu_u", 168, [P, BK, S], F32)
        sgu_vh = place("sgu_vh", 152, [P, 2, BW], F32R)
        sgu_vl = place("sgu_vl", 156, [P, 2, BW], F32R)
        sgu_m = [place("sgu_m0", 160, [P, BK, P], F32), place("sgu_m1", 164, [P, BK, P], F32)]
        wo_h = place("wo_h", 64, [P, KT, DM], F32R)
        wo_l = place("wo_l", 152, [P, KT, DM], F32R)
        x2a = place("x2a", 202.5, [P, 4, TT], F32)
        xn2 = place("xn2", 184, [P, 2, DM], F32)
        xv2 = place("xv2", 192, [P, 2, KT, P], F32)
        wd_raw = place("wd_raw", 64, [P, 2, DM], F32)
        wd_h = place("wd_h", 72, [P, 2, DM], F32R)
        wd_l = place("wd_l", 80, [P, 2, DM], F32R)
        ffc = place("ffc", 88, [P, 2, S], F32)
        ffa_h = place("ffa_h", 152, [P, 2, S], F32R)
        ffa_l = place("ffa_l", 160, [P, 2, S], F32R)
        ffg = place("ffg", 168, [P, 2, S + 2], F32)

        cur = [202.75]

        def small(name, shape, dt=F32):
            n = int(np.prod(shape[1:])) * (2 if dt == BF16 else 4)
            t = place(name, cur[0], shape, dt)
            cur[0] += -(-n // 32) * 32 / KB
            assert cur[0] <= 207.8, cur[0]
            return t

        ident = small("ident", [P, P])
        identb = small("identb", [P, P], BF16)
        tri = small("tri", [P, P], BF16)
        wstart = small("wstart", [P, P], BF16)
        cmask = small("cmask", [P, TT, CW], BF16)
        gains = small("gains", [P, 4, HD])
        chan = small("chan", [P, CHAN])
        graw = small("graw", [P, KT, GW])
        glog = small("glog", [P, TT, GW])
        any31 = small("any31", [P, 1])
        ssq = small("ssq", [P, TT])
        xa = small("xa", [P, 2, 4])
        qa = small("qa", [P, 6])
        qr = small("qr", [P, 6])
        qy = small("qy", [P, 6])
        qt = small("qt", [P, 6])
        nmx = small("nmx", [P, MAXIMA, 2, REP])
        wgt = small("wgt", [P, REP])
        wtmp = small("wtmp", [P, REP])
        peT = small("peT", [P, 2, L16])
        cbias = small("cbias", [HD, 2])
        kcAB = place("kcAB", 140, [P, 2, CW], F32R)
        va = place("va", 202.25, [P, 4, TT], F32)
        vc_h = place("vc_h", 144.75, [CW, HD + 1], F32R)
        vc_l = place("vc_l", 145.03125, [CW, HD + 1], F32R)
        w2 = place("w2", 145.375, [HD, 2, HD], F32)
        zc = place("zc", 186.25, [P, 2 * CW], F32)
        chan_rows = place("chan_rows", 187, [CHAN, P], F32)
        pe_rows = place("pe_rows", 187.5, [2 * L16, P], F32)

        bank = ctx.enter_context(nc.psum_tensor("bank", [P, 8, HALF], F32))
        flat = bank[:, :, :].rearrange("p b n -> p (b n)")

        x_loaded = [sem(f"x_loaded{t}") for t in range(TT)]
        const_loaded = sem("const_loaded")
        const2_loaded = sem("const2_loaded")
        w1_loaded = sem("w1_loaded")
        chan_turned = sem("chan_turned")
        chan_done = sem("chan_done")
        consts_made = sem("consts_made")
        sq_done = sem("sq_done")
        xa_done = sem("xa_done")
        xr_done = sem("xr_done")
        xn_done = sem("xn_done")
        xT_done = sem("xT_done")
        xv_done = sem("xv_done")
        xh_done = sem("xh_done")
        xl_done = sem("xl_done")
        raw_loaded = [sem("raw_loaded0"), sem("raw_loaded1")]
        graw_loaded = sem("graw_loaded")
        wph_done = sem("wph_done")
        wpl_done = sem("wpl_done")
        proj_done = sem("proj_done")
        pcopy_done = sem("pcopy_done")
        qa_done = sem("qa_done")
        qr_done = sem("qr_done")
        qn_done = sem("qn_done")
        qkh_done = sem("qkh_done")
        qkl_done = sem("qkl_done")
        qkT_done = sem("qkT_done")
        evq_done = sem("evq_done")
        evk_done = sem("evk_done")
        c_pe = sem("c_pe")
        c_act = sem("c_act")
        c_dve = sem("c_dve")
        glog_done = sem("glog_done")
        gate_done = sem("gate_done")
        rows_done = sem("rows_done")
        max_done = sem("max_done")
        both_done = sem("both_done")
        shift_done = sem("shift_done")
        s_done = sem("s_done")
        exp_done = sem("exp_done")
        pth_done = sem("pth_done")
        ptl_done = sem("ptl_done")
        pv_done = sem("pv_done")
        evac_done = sem("evac_done")
        turned = sem("turned")
        gated = sem("gated")
        summed = sem("summed")
        pool_chain = sem("pool_chain")
        final_done = sem("final_done")
        oh_done = sem("oh_done")
        ol_done = sem("ol_done")
        piece_loaded = [sem("piece_loaded0"), sem("piece_loaded1")]
        ph_done = sem("ph_done")
        pl_done = sem("pl_done")
        mm_done = sem("mm_done")
        freed = sem("freed")
        sig_done = sem("sig_done")
        acc_done = sem("acc_done")
        convc_done = sem("convc_done")
        obh_done = sem("obh_done")
        obl_done = sem("obl_done")
        poolw_loaded = sem("poolw_loaded")
        poolw_h = sem("poolw_h")
        poolw_l = sem("poolw_l")
        iota_done = sem("iota_done")
        poolp_done = sem("poolp_done")
        poold_done = sem("poold_done")
        pooldh_done = sem("pooldh_done")
        pooldl_done = sem("pooldl_done")
        pooly_mm = sem("pooly_mm")
        v_mm = sem("v_mm")
        gelu_done = sem("gelu_done")
        sguc_loaded = sem("sguc_loaded")
        sguw_masked = sem("sguw_masked")
        va_done = sem("va_done")
        vr_done = sem("vr_done")
        vn_done = sem("vn_done")
        swT_done = sem("swT_done")
        swh_done = sem("swh_done")
        swl_done = sem("swl_done")
        vsh_done = sem("vsh_done")
        vsl_done = sem("vsl_done")
        mix_mm = sem("mix_mm")
        mix_done = sem("mix_done")
        u_done = sem("u_done")
        mgh_done = sem("mgh_done")
        mgl_done = sem("mgl_done")
        x2_loaded = sem("x2_loaded")
        wo_mm = sem("wo_mm")
        x2_done = sem("x2_done")
        gcopy_done = sem("gcopy_done")
        ffc_done = sem("ffc_done")
        silu_done = sem("silu_done")
        ffh_done = sem("ffh_done")
        ffl_done = sem("ffl_done")
        wd_loaded = [sem("wd_loaded0"), sem("wd_loaded1")]
        wdh_done = sem("wdh_done")
        wdl_done = sem("wdl_done")
        d_mm = sem("d_mm")
        d_done = sem("d_done")
        out_done = sem("out_done")
        passed = sem("passed")
        dve_chain = sem("dve_chain")

        w_in_k = w_in[0].rearrange("(k p) n -> p k n", p=P)

        def wp_piece(t, c):
            if c < 2:
                return t[:, 4 * c:4 * c + 4, 0:QW]
            if c < 6:
                return t[:, 2 * (c - 2):2 * (c - 2) + 2, QW:QW + 6 * HD]
            return t[:, :, QW + 6 * HD:PW]

        def raw_piece(c):
            if c < 2:
                return raw[:, c % 2, 0:4 * QW].rearrange("p (k n) -> p k n", k=4)
            if c < 6:
                return raw[:, c % 2, 0:12 * HD].rearrange("p (k n) -> p k n", k=2)
            return graw[:, :, :]

        RAW_AT = {0: 16, 2: 48, 4: 80, 1: 16, 3: 48, 5: 80}

        block = ctx.enter_context(nc.Block())

        @block.sync
        def _(sp):
            sp.dma_start(x_in[:, 0, :], x[0, 0:P, :]).then_inc(x_loaded[0], 16)
            for at, src, n in ((C_G1, norm1_g[0], KT), (C_G2, norm2_g[0], KT), (C_CA, conv_a_w[0].rearrange("j c -> (j c)"), 3 * BK),
                               (C_CF, conv_ff_w[0].rearrange("j c -> (j c)"), 3 * FT), (C_PS, pool_scale[0], BK)):
                sp.dma_start(chan_rows[at:at + n, :], src.rearrange("(k p) -> k p", p=P)).then_inc(const_loaded, 16)
            for j in range(2):
                sp.dma_start(pe_rows[j * L16:(j + 1) * L16, :].rearrange("l (h d) -> l h d", h=2),
                             cmp_pe[0, j].rearrange("(h l) d -> l h d", h=2)).then_inc(const_loaded, 16)
            for t in range(1, TT):
                sp.dma_start(x_in[:, t, :], x[0, t * P:(t + 1) * P, :]).then_inc(x_loaded[t], 16)
            sp.dma_start(gains[:, :, :].rearrange("p a d -> p (a d)"),
                         qk_norm_g[0].rearrange("a d -> (a d)").partition_broadcast(P)).then_inc(const2_loaded, 16)
            sp.dma_start(w2[:, :, :], cmp_w2[0].rearrange("j d e -> d j e")).then_inc(const2_loaded, 16)
            with sp.Fori(0, GROUPS) as g:
                q0 = sp.snap(g * QW + COL_Q)
                kv0 = sp.snap(g * HD)
                ga0 = sp.snap(g * GW + COL_GATE)
                for c in range(6):
                    after(sp, wpl_done, g * SPLITS, c - 1)
                    if c < 2:
                        sp.dma_start(raw_piece(c), w_in_k[:, 4 * c:4 * c + 4, bass.ds(q0, QW)]).then_inc(raw_loaded[c % 2], 16)
                    else:
                        for k in range(2):
                            kt = 2 * (c - 2) + k
                            cols = w_in[0, kt * P:(kt + 1) * P, COL_KV:COL_KV + 6 * KV].rearrange("p (j n) -> p j n", n=KV)
                            sp.dma_start(raw[:, c % 2, k * 6 * HD:(k + 1) * 6 * HD].rearrange("p (j n) -> p j n", j=6),
                                         cols[:, :, bass.ds(kv0, HD)]).then_inc(raw_loaded[c % 2], 16)
                    if c == 0:
                        sp.dma_start(graw[:, :, :], w_in_k[:, :, bass.ds(ga0, GW)]).then_inc(graw_loaded, 16)
                sp.wait_ge(wpl_done, g * SPLITS + SPLITS)
                sp.sem_inc(passed, 1)

            def load(m, slot, dst, src):
                sp.wait_ge(pl_done, m + 1)
                sp.sem_inc(passed, 1)
                sp.dma_start(dst, src).then_inc(piece_loaded[slot], 16)

            def ring_piece(slot, k=KT):
                return raw[:, slot, 0:k * P].rearrange("p (k n) -> p k n", k=k)

            def load_merge(b, turn, m0):
                g0 = [sp_value((turn * 2 + a) * P + (COL_MERGE + b * DM)) for a in range(2)]
                y0 = [sp_value((turn * 2 + a) * P) for a in range(2)]
                wb = w_branch[0, b].rearrange("(k p) n -> p k n", p=P)
                for a in range(2):
                    load(turn * 4 + (m0 + 2 * a), 0, ring_piece(0), w_in_k[:, :, bass.ds(g0[a], P)])
                    load(turn * 4 + (m0 + 2 * a + 1), 1, ring_piece(1, BK), wb[:, :, bass.ds(y0[a], P)])

            def sp_value(v):
                return v if isinstance(v, int) else sp.snap(v)

            with sp.Fori(0, KT // 2) as t:
                load_merge(1, t, PIECE["merge1"])
            for c in range(3 * BK):
                col = (BW, 2 * BW, 0)[c % 3] + (c // 3) * P
                load(PIECE["conv"] + c, c % 2, ring_piece(c % 2), w_in_k[:, :, col:col + P])
            with sp.Fori(0, KT // 2) as t:
                load_merge(0, t, PIECE["merge0"])
            sp.dma_start(pool_w32[:, :, :], pool_w[0].rearrange("g c d -> c g d")).then_inc(poolw_loaded, 16)
            for c in range(BK):
                load(PIECE["pool"] + c, c % 2, ring_piece(c % 2), w_in_k[:, :, COL_POOL + c * P:COL_POOL + (c + 1) * P])
            for c in range(4):
                load(PIECE["v"] + c, c % 2, raw[:, c % 2, :].rearrange("p (k n) -> p k n", k=2),
                     w_in_k[:, 2 * c:2 * c + 2, COL_SGU + BW:COL_SGU + 2 * BW])
            with sp.Fori(0, KT // 2) as t:
                load_merge(2, t, PIECE["merge2"])
            for c in range(BK):
                load(PIECE["u"] + c, c % 2, ring_piece(c % 2), w_in_k[:, :, COL_SGU + c * P:COL_SGU + (c + 1) * P])
            with sp.Fori(0, KT // 2) as t:
                load_merge(3, t, PIECE["merge3"])
            for c in range(KT):
                load(PIECE["wo"] + c, c % 2, raw[:, c % 2, :], w_o[0, c * P:(c + 1) * P, :])
            for t in range(TT):
                sp.wait_ge(mgl_done, t + 1)
                sp.dma_start(x2[:, t, :], x[0, t * P:(t + 1) * P, :]).then_inc(x2_loaded, 16)
                sp.wait_ge(x2_loaded, 16 * (t + 1))
            with sp.Fori(0, FT // 2) as t:
                cols = [sp.snap((t * 2 + a) * P + up * D_FF) for a in range(2) for up in range(2)]
                rows = [sp.snap(t * (2 * P * DM) + a * P * DM) for a in range(2)]
                for c in range(4):
                    load(t * 4 + (PIECE["ff"] + c), c % 2, ring_piece(c % 2),
                         w_up[0].rearrange("(k p) n -> p k n", p=P)[:, :, bass.ds(cols[c], P)])
                for a in range(2):
                    sp.wait_ge(wdl_done, t * 2 + (a + 1))
                    sp.dma_start(wd_raw[:, a, :], w_down[0].rearrange("r n -> (r n)")[bass.ds(rows[a], P * DM)].rearrange("(p n) -> p n", p=P)).then_inc(wd_loaded[a], 16)
            for t in range(TT):
                sp.wait_ge(d_done, 2 + (FT // 2 - 1) * TT + t + 1)
                sp.dma_start(out[0, t * P:(t + 1) * P, :], x2[:, t, :]).then_inc(out_done, 16)
            sp.wait_ge(out_done, 16 * TT)

        @block.gpsimd
        def _(pool):
            nc.gpsimd.memset(ident[:, :], 0.0).then_inc(consts_made, 1)
            nc.gpsimd.memset(tri[:, :], 0.0).then_inc(consts_made, 1)
            nc.gpsimd.memset(wstart[:, :], 0.0).then_inc(consts_made, 1)
            nc.gpsimd.memset(cmask[:, :, :], 0.0).then_inc(consts_made, 1)
            nc.gpsimd.memset(any31[:, :], 1.0).then_inc(consts_made, 1)
            nc.gpsimd.memset(zc[:, :], 0.0).then_inc(consts_made, 1)
            pool.wait_ge(consts_made, 6)
            nc.gpsimd.affine_select(out=ident[:, :], in_=ident[:, :], compare_op=ALU.not_equal, fill=1.0,
                                    base=0, pattern=[[-1, P]], channel_multiplier=1).then_inc(consts_made, 1)
            nc.gpsimd.affine_select(out=tri[:, :], in_=tri[:, :], compare_op=ALU.is_ge, fill=NEG,
                                    base=0, pattern=[[-1, P]], channel_multiplier=1).then_inc(consts_made, 1)
            nc.gpsimd.affine_select(out=wstart[:, :], in_=wstart[:, :], compare_op=ALU.is_gt, fill=NEG,
                                    base=0, pattern=[[1, P]], channel_multiplier=-1).then_inc(consts_made, 1)
            nc.gpsimd.affine_select(out=cmask[:, :, :], in_=cmask[:, :, :], compare_op=ALU.is_ge, fill=NEG,
                                    base=1 - CMP_BLOCK, pattern=[[P, TT], [-CMP_STRIDE, CW]],
                                    channel_multiplier=1).then_inc(consts_made, 1)
            nc.gpsimd.affine_select(out=any31[:, :], in_=any31[:, :], compare_op=ALU.is_ge, fill=0.0,
                                    base=1 - CMP_BLOCK, pattern=[[0, 1]], channel_multiplier=1).then_inc(consts_made, 1)
            pool.wait_ge(consts_made, 11)
            nc.gpsimd.tensor_copy(identb[:, :], ident[:, :]).then_inc(consts_made, 1)

            with pool.Fori(0, GROUPS) as g:
                for slot in slots:
                    for at, n, r0, heads, c, w in slot["pieces"]:
                        if at + 1 == piece_end[n]:
                            pool.wait_ge(max_done, g * PIECES + piece_end[n])
                            if tasks[n][3] > HALF:
                                pool.wait_ge(both_done, g * BOTH + both_at[n] + 1)
                            if n >= MAXIMA:
                                pool.wait_ge(s_done, g * UNITS + last_unit[n - MAXIMA] + 1)
                            nc.gpsimd.tensor_tensor(shift[:, n % MAXIMA, :, :], ident[:, :].unsqueeze(1).broadcast_to([P, REP, P]),
                                                    nmx[:, n % MAXIMA, 0, :].unsqueeze(2).broadcast_to([P, REP, P]),
                                                    ALU.mult).then_inc(shift_done, 1)
                    if slot["sum"] is not None:
                        i = slot["sum"]
                        pool.wait_ge(gated, g * NT + 3 * i + 3)
                        o = [o_gated[:, (3 * i + b) % 4, :] for b in range(3)]
                        nc.gpsimd.tensor_tensor(o[0], o[0], o[1], ALU.add).then_inc(pool_chain, 1)
                        pool.wait_ge(pool_chain, g * TT + i + 1)
                        nc.gpsimd.tensor_tensor(o[0], o[0], o[2], ALU.add).then_inc(summed, 1)

            pool.wait_ge(mm_done, 2 + CHUNK["pool"])
            nc.gpsimd.iota(pool_t16[:, :], pattern=[[1, 16]], base=1, channel_multiplier=0,
                           allow_small_or_imprecise_dtypes=True).then_inc(iota_done, 1)
            pool.wait_ge(v_mm, TT)
            pool.dma_start(sgu_g[:, :], sgu_norm_g[0].partition_broadcast(P)).then_inc(sguc_loaded, 16)
            pool.dma_start(sgu_bias[:, :, :].rearrange("p g t -> p (g t)"),
                           sgu_b[0].rearrange("g t -> (g t)").partition_broadcast(P)).then_inc(sguc_loaded, 16)
            pool.dma_start(sgu_w32[:, :, :], sgu_w[0].rearrange("g t s -> t g s")).then_inc(sguc_loaded, 16)
            pool.wait_ge(sguc_loaded, 48)
            nc.gpsimd.affine_select(out=sgu_w32[:, :, :], in_=sgu_w32[:, :, :], compare_op=ALU.is_ge, fill=0.0,
                                    base=0, pattern=[[0, BK], [-1, P]], channel_multiplier=1).then_inc(sguw_masked, 1)

        @block.scalar
        def _(act):
            for t in range(TT + 2):
                if t < TT:
                    act.wait_ge(x_loaded[t], 16)
                    nc.scalar.activation(junk[:, :], x_in[:, t, :], ACT.Square,
                                         accum_out=ssq[:, t:t + 1]).then_inc(sq_done, 1)
                    act.wait_ge(xa_done, t + 1)
                    nc.scalar.activation(xa[:, t % 2, 1:2], xa[:, t % 2, 0:1], ACT.Sqrt).then_inc(xr_done, 1)
                if 1 <= t <= TT:
                    act.wait_ge(xv_done, t)
                    nc.scalar.activation(actT_h[:, :, (t - 1) * P:t * P], xv[:, (t - 1) % 2, :, :],
                                         ACT.Copy).then_inc(xh_done, 1)
            act.wait_ge(xn_done, TT)
            for j in range(2):
                for half in range(2):
                    rows = cmp_w1[0, j, half * L16 * HD:(half + 1) * L16 * HD, :]
                    act.dma_start(w1[half * HD:(half + 1) * HD, j, :, :],
                                  rows.rearrange("(l d) e -> d l e", d=HD)).then_inc(w1_loaded, 16)

            with act.Fori(0, GROUPS) as g:
                for c in range(SPLITS):
                    if c < 6:
                        act.wait_ge(raw_loaded[c % 2], g * 80 + RAW_AT[c])
                    else:
                        act.wait_ge(graw_loaded, g * 16 + 16)
                    nc.scalar.activation(wp_piece(wp_h, c), raw_piece(c), ACT.Copy).then_inc(wph_done, 1)

                def evacuate_transposes(t):
                    act.wait_ge(qkT_done, g * TT + t + 1)
                    nc.scalar.activation(qT[:, :, t * P:(t + 1) * P],
                                         bank[:, 4, :].rearrange("p (r n) -> p r n", r=REP), ACT.Copy)
                    kc = bank[:, 6, 0:2 * P].rearrange("p (j n) -> p j n", j=2)
                    nc.scalar.activation(kcT[0:HD, :, t * P:(t + 1) * P], kc[0:HD, :, :], ACT.Copy)
                    lo = CMP_STRIDE if t == 0 else 0
                    nc.scalar.activation(kcT[HD:P, :, t * P + lo - CMP_STRIDE:(t + 1) * P - CMP_STRIDE],
                                         kc[HD:P, :, lo:P], ACT.Copy).then_inc(evq_done, 1)

                for t in range(TT + 1):
                    if t < TT:
                        act.wait_ge(proj_done, g * TT + t + 1)
                        after(act, qkl_done, g * TT, t - 1)
                        nc.scalar.activation(proj[:, t % 2, 0:QW], bank[:, 2 * (t % 2), 0:QW], ACT.Copy)
                        nc.scalar.activation(proj[:, t % 2, QW:PW], bank[:, 2 * (t % 2) + 1, 0:PW - QW],
                                             ACT.Copy).then_inc(pcopy_done, 1)
                    if t >= 1:
                        evacuate_transposes(t - 1)
                    if t < TT:
                        act.wait_ge(qa_done, g * TT + t + 1)
                        nc.scalar.activation(qr[:, :], qa[:, :], ACT.Sqrt).then_inc(qr_done, 1)
                        after(act, qkT_done, g * TT, t - 1)
                        act.wait_ge(qn_done, g * TT + t + 1)
                        d = dup[:, t % 2, :, :]
                        nc.scalar.activation(d[:, 0:REP, 0:HD].bitcast(F32R), qkn[:, 0:REP, :], ACT.Copy)
                        kd = d[:, 4:8, :].rearrange("p (t a) (u d) -> p t a u d", a=2, u=2)
                        for ty in range(2):
                            nc.scalar.activation(kd[:, ty, 0, :, :].bitcast(F32R),
                                                 qkn[:, 4 + ty, :].unsqueeze(1).broadcast_to([P, 2, HD]), ACT.Copy)
                        pv = proj[:, t % 2, QW:QW + 6 * HD].rearrange("p (t d) -> p t d", d=HD)
                        cd = d[:, 8:10, :].rearrange("p t (u d) -> p t u d", u=2)
                        nc.scalar.activation(cd, pv[:, 0:2, :].unsqueeze(2).broadcast_to([P, 2, 2, HD]), ACT.Copy)
                        nc.scalar.activation(v_h[:, :, t, 0:HD], pv[:, 3:6:2, :], ACT.Copy).then_inc(qkh_done, 1)

                def compressed(step):
                    act.wait_ge(c_pe, g * 3 + step + 1)
                    if step == 0:
                        act.wait_ge(c_dve, g * 4 + 2)
                        for j in range(2):
                            ins = nc.scalar.activation(h1[:, j, 0:NCMP], bank[0:HD, 7, j * HD:j * HD + NCMP], ACT.Silu,
                                                       bias=cbias[:, j:j + 1])
                    elif step == 1:
                        act.wait_ge(c_dve, g * 4 + 3)
                        ins = nc.scalar.activation(qr[0:NCMP, 0:1], qa[0:NCMP, 0:1], ACT.Sqrt)
                    else:
                        ins = nc.scalar.activation(kcAB[:, :, 0:NCMP], bank[:, 7, 384:384 + 2 * CW].rearrange(
                            "p (a n) -> p a n", a=2)[:, :, 0:NCMP], ACT.Copy)
                    ins.then_inc(c_act, 1)

                act.wait_ge(glog_done, g * TT + TT)
                nc.scalar.activation(glog[:, :, :], glog[:, :, :], ACT.Sigmoid).then_inc(gate_done, 1)

                for slot in slots:
                    if slot["n"] in COMPRESS:
                        compressed(COMPRESS.index(slot["n"]))
                    if slot["unit"]:
                        u, n, j = slot["unit"]
                        nr = CW if tasks[n][1] == "cmp" else P
                        act.wait_ge(s_done, g * UNITS + u + 1)
                        after(act, ptl_done, g * UNITS, u - RING + 1)
                        nc.scalar.activation(pT[0:nr, u % RING, :], bank[0:nr, 3 + u % 2, :], ACT.Exp).then_inc(exp_done, 1)
                        act.wait_ge(exp_done, g * UNITS + u + 1)
                        after(act, pv_done, g * UNITS, u - RING + 1)
                        nc.scalar.activation(pT_h[0:nr, u % RING, :], pT[0:nr, u % RING, :], ACT.Copy).then_inc(pth_done, 1)
                    if slot["evacuate"] is not None:
                        n = slot["evacuate"]
                        act.wait_ge(pv_done, g * UNITS + last_unit[n] + 1)
                        after(act, turned, g * NT, n - 1)
                        nc.scalar.activation(oT[:, n % 2, :], bank[0:HD + 1, 5 + n % 2, :], ACT.Copy).then_inc(evac_done, 1)
                    if slot["final"] is not None:
                        i = slot["final"]
                        act.wait_ge(final_done, g * TT + i + 1)
                        q0 = TILE_ORDER[i] * P
                        nc.scalar.activation(outb_h[:, bass.ds(g * 2, 2), q0:q0 + P],
                                             bank[:, 2, 0:2 * P].rearrange("p (b n) -> p b n", b=2), ACT.Copy).then_inc(oh_done, 1)
                act.wait_ge(pv_done, g * UNITS + UNITS)

            def high(m, slot, dst, src):
                act.wait_ge(piece_loaded[slot], (m // 2) * 16 + 16 if isinstance(m, int) else m)
                nc.scalar.activation(dst, src, ACT.Copy).then_inc(ph_done, 1)

            def high_ring(turn, per, m, c, slot):
                act.wait_ge(piece_loaded[slot], turn * (per // 2 * 16) + (m // 2 * 16 + 16))
                act.wait_ge(mm_done, turn * per + (c + 1))
                nc.scalar.activation(ring_h[:, slot, :], raw[:, slot, :], ACT.Copy).then_inc(ph_done, 1)

            def merge(b, turn, m0, c0, t0, last=False):
                for a in range(2):
                    for p in (2 * a, 2 * a + 1):
                        if not (last and p == 3):
                            high_ring(turn, 4, m0 + p + 1, c0 + p + 1, (p + 1) % 2)
                        if p == 2 * a:
                            act.wait_ge(mm_done, turn * 4 + (2 + c0 + p + 1))
                            act.wait_ge(acc_done, turn * 2 + (t0 + a + 1))
                            nc.scalar.activation(sig[:, a, :], flat[:, p * 1024:(p + 1) * 1024], ACT.Sigmoid).then_inc(sig_done, 1)

            high_ring(0, 4, 0, 0, 0)
            with act.Fori(0, KT // 2) as t:
                merge(1, t, PIECE["merge1"], CHUNK["merge1"], 0)

            for c in range(3 * BK):
                m, ck_ = PIECE["conv"] + c, CHUNK["conv"] + c
                high_ring(0, 4, m + 1, ck_ + 1, (c + 1) % 2)
                q = c // 3
                if c % 3 == 0:
                    act.wait_ge(mm_done, 2 + ck_ + 1)
                    if q >= 2:
                        act.wait_ge(freed, 4 + ck_ - 6 + 2)
                    nc.scalar.activation(conv_c[:, q % 2, :], flat[:, (ck_ % 4) * 1024:(ck_ % 4 + 1) * 1024], ACT.Copy).then_inc(convc_done, 1)
                if c % 3 == 2:
                    act.wait_ge(freed, 4 + ck_ + 1)
                    nc.scalar.activation(outb_h[:, q, :], conv_o[:, q % 2, :], ACT.Copy).then_inc(obh_done, 1)
            with act.Fori(0, KT // 2) as t:
                merge(0, t, PIECE["merge0"], CHUNK["merge0"], KT)

            act.wait_ge(poolw_loaded, 16)
            nc.scalar.activation(pool_wh[:, :, :], pool_w32[:, :, :], ACT.Copy).then_inc(poolw_h, 1)

            def pool_out(q):
                act.wait_ge(pooly_mm, q + 1)
                nc.scalar.activation(outb_h[:, q, :], flat[:, (2 + q % 2) * 1024:(3 + q % 2) * 1024], ACT.Copy,
                                     scale=chan[:, C_PS + q:C_PS + q + 1]).then_inc(obh_done, 1)

            for q in range(BK):
                m, ck_ = PIECE["pool"] + q, CHUNK["pool"] + q
                if q < BK - 1:
                    high_ring(0, 4, m + 1, ck_ + 1, (q + 1) % 2)
                act.wait_ge(mm_done, 2 + ck_ + 1)
                if q >= 2:
                    act.wait_ge(poold_done, q - 1)
                if q == 0:
                    act.wait_ge(acc_done, 2 + 2 * KT)
                nc.scalar.activation(pool_p[:, q % 2, 16:], flat[:, (q % 2) * 1024:(q % 2 + 1) * 1024], ACT.Copy).then_inc(poolp_done, 1)
                if q >= 1:
                    pool_out(q - 1)
                act.wait_ge(poold_done, q + 1)
                if q >= 1:
                    act.wait_ge(pooly_mm, q)
                nc.scalar.activation(pool_dh[:, :], pool_d[:, :], ACT.Copy).then_inc(pooldh_done, 1)
            pool_out(BK - 1)

            act.wait_ge(obl_done, 2 * BK)
            for c in range(4):
                high(PIECE["v"] + c, c % 2, wv_h[:, 2 * c:2 * c + 2, :], raw[:, c % 2, :].rearrange("p (k n) -> p k n", k=2))
            high_ring(0, 4, PIECE["merge2"], CHUNK["merge2"], 0)
            for t in range(TT):
                act.wait_ge(v_mm, t + 1)
                nc.scalar.activation(sgu_v[:, t, :], bank[:, t, :], ACT.Gelu).then_inc(gelu_done, 1)
            act.wait_ge(va_done, 1)
            nc.scalar.activation(va[:, 1, :], va[:, 0, :], ACT.Sqrt).then_inc(vr_done, 1)
            with act.Fori(0, KT // 2) as t:
                merge(2, t, PIECE["merge2"], CHUNK["merge2"], 2 * KT)
            for q in range(BK):
                m, ck_ = PIECE["u"] + q, CHUNK["u"] + q
                high_ring(0, 4, m + 1, ck_ + 1, (q + 1) % 2)
                act.wait_ge(mm_done, 2 + ck_ + 1)
                nc.scalar.activation(sgu_u[:, q, :], flat[:, (ck_ % 4) * 1024:(ck_ % 4 + 1) * 1024], ACT.Gelu).then_inc(u_done, 1)
            act.wait_ge(swT_done, 1)
            nc.scalar.activation(sgu_wh[:, :, :], bank[:, 4, :].rearrange("p (g t) -> p g t", g=BK), ACT.Copy).then_inc(swh_done, 1)
            act.wait_ge(acc_done, 2 + 3 * KT)
            act.wait_ge(vn_done, TT)
            for t in range(TT + 1):
                if t < TT:
                    if t >= 2:
                        act.wait_ge(mix_mm, t - 1)
                    nc.scalar.activation(sgu_vh[:, t % 2, :], sgu_v[:, t, :], ACT.Copy).then_inc(vsh_done, 1)
                if t >= 1:
                    act.wait_ge(mix_done, t)
                    nc.scalar.activation(outb_h[:, :, (t - 1) * P:t * P], sgu_m[(t - 1) % 2][:, :, :], ACT.Copy).then_inc(obh_done, 1)
            act.wait_ge(mix_mm, TT)
            with act.Fori(0, KT // 2 - 1) as t:
                merge(3, t, PIECE["merge3"], CHUNK["merge3"], 3 * KT)
            merge(3, KT // 2 - 1, PIECE["merge3"], CHUNK["merge3"], 3 * KT, last=True)

            act.wait_ge(mm_done, 2 + CHUNK["ff"])
            for k in range(KT):
                act.wait_ge(acc_done, 2 + 3 * KT + k + 1)
                nc.scalar.activation(actT_h[:, k, :], merged[:, k, :], ACT.Copy).then_inc(mgh_done, 1)
                high(PIECE["wo"] + k, k % 2, wo_h[:, k, :], raw[:, k % 2, :])

            for tg in range(2):
                for t in range(4 * tg, 4 * tg + 4):
                    act.wait_ge(x2_done, t + 1)
                    if t:
                        act.wait_ge(sq_done, TT + t)
                    nc.scalar.activation(xv2[:, 1, :, :].rearrange("p k n -> p (k n)"), x2[:, t, :], ACT.Square,
                                         accum_out=ssq[:, t:t + 1]).then_inc(sq_done, 1)
                act.wait_ge(xa_done, TT + tg + 1)
                nc.scalar.activation(x2a[:, 1, 4 * tg:4 * tg + 4], x2a[:, 0, 4 * tg:4 * tg + 4], ACT.Sqrt).then_inc(xr_done, 1)
            for t in range(TT):
                act.wait_ge(xv_done, TT + t + 1)
                nc.scalar.activation(actT_h[:, :, t * P:(t + 1) * P], xv2[:, t % 2, :, :], ACT.Copy).then_inc(xh_done, 1)
            high_ring(0, 4, PIECE["ff"], CHUNK["ff"], 0)

            def ff(turn, last=False):
                m0, c0 = PIECE["ff"], CHUNK["ff"]
                for a in range(2):
                    high_ring(turn, 4, m0 + 2 * a + 1, c0 + 2 * a + 1, 1)
                    act.wait_ge(mm_done, turn * 4 + (2 + c0 + 2 * a + 1))
                    nc.scalar.activation(ffg[:, a, 2:], flat[:, 0:1024], ACT.Copy).then_inc(gcopy_done, 1)
                    if a == 1:
                        for k in range(2):
                            act.wait_ge(wd_loaded[k], turn * 16 + 16)
                            if not (isinstance(turn, int) and turn == 0):
                                act.wait_ge(d_mm, turn * TT)
                            nc.scalar.activation(wd_h[:, k, :], wd_raw[:, k, :], ACT.Copy).then_inc(wdh_done, 1)
                    if not (last and a == 1):
                        high_ring(turn, 4, m0 + 2 * a + 2, c0 + 2 * a + 2, 0)
                    act.wait_ge(ffc_done, turn * 2 + (a + 1))
                    nc.scalar.activation(ffc[:, a, :], ffc[:, a, :], ACT.Silu).then_inc(silu_done, 1)
                    act.wait_ge(freed, turn * 4 + (4 + c0 + 2 * a + 2))
                    nc.scalar.activation(ffa_h[:, a, :], ffc[:, a, :], ACT.Copy).then_inc(ffh_done, 1)

            ff(0)
            with act.Fori(1, FT // 2 - 1) as t:
                ff(t)
            ff(FT // 2 - 1, last=True)

        @block.vector
        def _(dve):
            ch = Chain(dve, dve_chain)

            def inverse_root(a, root, y, t, n, root_done, count):
                dve.wait_ge(root_done, count)
                ch.link(nc.vector.reciprocal(y, root))
                ch.link(nc.vector.tensor_tensor(t, y, y, ALU.mult))
                ch.link(nc.vector.tensor_tensor(t, t, a, ALU.mult))
                ch.link(nc.vector.tensor_scalar(t, t, -0.5, 1.5, ALU.mult, ALU.add))
                ch.link(nc.vector.tensor_tensor(y, y, t, ALU.mult))

            dve.sem_inc(freed, 4)
            dve.sem_inc(pl_done, 2)
            dve.sem_inc(wdl_done, 2)
            dve.sem_inc(acc_done, 2)
            dve.sem_inc(d_done, 2)
            dve.wait_ge(chan_turned, 1)
            ch.link(nc.vector.tensor_copy(chan[:, :], bank[:, 6, 0:CHAN]))
            nc.vector.tensor_copy(peT[:, :, :], bank[:, 6, CHAN:CHAN + 2 * L16].rearrange("p (j l) -> p j l", j=2)).then_inc(chan_done, 1)
            for t in range(TT + 2):
                if t < TT:
                    dve.wait_ge(sq_done, t + 1)
                    xs = xa[:, t % 2, :]
                    nc.vector.tensor_scalar(xs[:, 0:1], ssq[:, t:t + 1], 1.0 / DM, EPS, ALU.mult, ALU.add).then_inc(xa_done, 1)
                    inverse_root(xs[:, 0:1], xs[:, 1:2], xs[:, 2:3], xs[:, 3:4], 1, xr_done, t + 1)
                    if t >= 2:
                        dve.wait_ge(xT_done, t - 1)
                    nc.vector.tensor_scalar(xn[:, t % 2, :], x_in[:, t, :], xs[:, 2:3], None, ALU.mult).then_inc(xn_done, 1)
                if 1 <= t <= TT:
                    dve.wait_ge(xT_done, t)
                    b = (t - 1) % 2
                    if t >= 3:
                        dve.wait_ge(xl_done, t - 2)
                    src = bank[:, 2 * b:2 * b + 2, :].rearrange("p b (k n) -> p (b k) n", n=P)
                    nc.vector.tensor_tensor(xv[:, b, :, :], src, chan[:, C_G1:C_G1 + KT].unsqueeze(2).broadcast_to([P, KT, P]),
                                            ALU.mult).then_inc(xv_done, 1)
                if t >= 2:
                    b = (t - 2) % 2
                    dve.wait_ge(xh_done, t - 1)
                    cols = slice((t - 2) * P, (t - 1) * P)
                    nc.vector.tensor_tensor(actT_l[:, :, cols], xv[:, b, :, :], actT_h[:, :, cols].bitcast(F32),
                                            ALU.subtract).then_inc(xl_done, 1)
            dve.wait_ge(const2_loaded, 32)
            ch.link(nc.vector.tensor_scalar(gains[:, 0, :], gains[:, 0, :], HD ** -0.5, None, ALU.mult))
            dve.wait_ge(consts_made, 6)
            ch.link(nc.vector.tensor_copy(vc_h[:, 0:HD], zc[0:CW, 0:HD]))
            ch.link(nc.vector.tensor_copy(vc_l[:, :], zc[0:CW, 0:HD + 1]))
            ch.link(nc.vector.tensor_scalar(vc_h[:, HD:HD + 1], zc[0:CW, 0:1], 1.0, None, ALU.add))
            for a, one in ((v_h, 1.0), (v_l, 0.0)):
                ch.link(nc.vector.tensor_scalar(a[:, :, :, HD:HD + 1],
                                                zc[:, 0:2 * TT].rearrange("p (a t) -> p a t", a=2).unsqueeze(3),
                                                one, None, ALU.add))

            with dve.Fori(0, GROUPS) as g:
                ch.enter(g, CHAIN_TURN)
                for c in range(SPLITS):
                    dve.wait_ge(wph_done, g * SPLITS + c + 1)
                    nc.vector.tensor_tensor(wp_piece(wp_l, c), raw_piece(c), wp_piece(wp_h, c).bitcast(F32),
                                            ALU.subtract).then_inc(wpl_done, 1)

                for t in range(TT + 1):
                    if t < TT:
                        dve.wait_ge(pcopy_done, g * TT + t + 1)
                        pr = proj[:, t % 2, :]
                        q = pr[:, 0:QW].rearrange("p (r d) -> p r d", d=HD)
                        kv = pr[:, QW:QW + 6 * HD].rearrange("p (t d) -> p t d", d=HD)
                        k = kv[:, 2:6:2, :]
                        nc.vector.tensor_copy(glog[:, t, :], pr[:, QW + 6 * HD:PW]).then_inc(glog_done, 1)
                        after(dve, qkh_done, g * TT, t)
                        after(dve, qkl_done, g * TT, t)
                        nc.vector.tensor_tensor(qkn[:, 0:4, :], q, q, ALU.mult)
                        ch.link(nc.vector.tensor_tensor(qkn[:, 4:6, :], k, k, ALU.mult))
                        ch.link(nc.vector.tensor_reduce(qt[:, :], qkn[:, :, :], AX, ALU.add))
                        nc.vector.tensor_scalar(qa[:, :], qt[:, :], 1.0 / HD, EPS, ALU.mult, ALU.add).then_inc(qa_done, 1)
                    if t >= 1:
                        dve.wait_ge(qkT_done, g * TT + t)
                        nc.vector.tensor_copy(kAB[:, :, (t - 1) * P:t * P],
                                              bank[:, 5, :].rearrange("p (a n) -> p a n", a=4)).then_inc(evk_done, 1)
                    if t < TT:
                        inverse_root(qa[:, :], qr[:, :], qy[:, :], qt[:, :], 6, qr_done, g * TT + t + 1)
                        nc.vector.tensor_tensor(qkn[:, 0:4, :], q, qy[:, 0:4].unsqueeze(2).broadcast_to([P, 4, HD]), ALU.mult)
                        ch.link(nc.vector.tensor_tensor(qkn[:, 4:6, :], k, qy[:, 4:6].unsqueeze(2).broadcast_to([P, 2, HD]), ALU.mult))
                        nc.vector.tensor_tensor(qkn[:, 0:4, :], qkn[:, 0:4, :], gains[:, 0:1, :].broadcast_to([P, 4, HD]), ALU.mult)
                        nc.vector.tensor_tensor(qkn[:, 4:6, :], qkn[:, 4:6, :], gains[:, 2:4, :], ALU.mult).then_inc(qn_done, 1)
                        dve.wait_ge(qkh_done, g * TT + t + 1)
                        d = dup[:, t % 2, :, :]
                        nc.vector.tensor_tensor(d[:, 0:REP, HD:P], qkn[:, 0:4, :], d[:, 0:REP, 0:HD], ALU.subtract)
                        kd = d[:, 4:8, :].rearrange("p (t a) (u d) -> p t a u d", a=2, u=2)
                        for ty in range(2):
                            nc.vector.tensor_tensor(kd[:, ty, 1, :, :], qkn[:, 4 + ty, :].unsqueeze(1).broadcast_to([P, 2, HD]),
                                                    kd[:, ty, 0, :, :], ALU.subtract)
                        nc.vector.tensor_tensor(v_l[:, :, t, 0:HD], kv[:, 3:6:2, :], v_h[:, :, t, 0:HD].bitcast(F32),
                                                ALU.subtract).then_inc(qkl_done, 1)

                dve.wait_ge(qkT_done, g * TT + TT)
                nc.vector.tensor_scalar(ones[:, :], ident[:, :], 0.0, 1.0, ALU.mult, ALU.add)
                nc.vector.tensor_scalar(kcAB[:, :, NCMP:CW], ident[:, 0:2].unsqueeze(2), 0.0, None, ALU.mult).then_inc(c_dve, 1)

                def compressed(step):
                    if step == 0:
                        dve.wait_ge(c_pe, g * 3 + 1)
                        nc.vector.tensor_copy(cbias[:, :], bank[0:HD, 7, 128:256:64]).then_inc(c_dve, 1)
                    elif step == 1:
                        dve.wait_ge(c_pe, g * 3 + 2)
                        ch.link(nc.vector.tensor_copy(ck[0:NCMP, :], bank[0:NCMP, 7, 256:256 + HD]))
                        nc.vector.tensor_copy(vc_h[0:NCMP, 0:HD], bank[0:NCMP, 7, 320:320 + HD])
                        ch.link(nc.vector.tensor_tensor(ck2[0:NCMP, :], ck[0:NCMP, :], ck[0:NCMP, :], ALU.mult))
                        nc.vector.tensor_tensor(vc_l[0:NCMP, 0:HD], bank[0:NCMP, 7, 320:320 + HD],
                                                vc_h[0:NCMP, 0:HD].bitcast(F32), ALU.subtract)
                        ch.link(nc.vector.tensor_reduce(qt[0:NCMP, 0:1], ck2[0:NCMP, :], AX, ALU.add))
                        nc.vector.tensor_scalar(qa[0:NCMP, 0:1], qt[0:NCMP, 0:1], 1.0 / HD, EPS, ALU.mult, ALU.add).then_inc(c_dve, 1)
                    else:
                        inverse_root(qa[0:NCMP, 0:1], qr[0:NCMP, 0:1], qy[0:NCMP, 0:1], qt[0:NCMP, 0:1], 1, c_act, g * 3 + 2)
                        ch.link(nc.vector.tensor_scalar(ck[0:NCMP, :], ck[0:NCMP, :], qy[0:NCMP, 0:1], None, ALU.mult))
                        ch.link(nc.vector.tensor_tensor(ck[0:NCMP, :], ck[0:NCMP, :], gains[0:NCMP, 1, :], ALU.mult))
                        twice = ck[0:NCMP, :].unsqueeze(1).broadcast_to([NCMP, 2, HD])
                        ch.link(nc.vector.tensor_copy(ckd[0:NCMP, 0, :, :].bitcast(F32R), twice))
                        nc.vector.tensor_tensor(ckd[0:NCMP, 1, :, :], twice, ckd[0:NCMP, 0, :, :], ALU.subtract).then_inc(c_dve, 1)

                dve.wait_ge(gate_done, g + 1)

                def low_part(u, n, j):
                    dve.wait_ge(pth_done, g * UNITS + u + 1)
                    nr = CW if tasks[n][1] == "cmp" else P
                    nc.vector.tensor_tensor(pT_l[0:nr, u % RING, :], pT[0:nr, u % RING, :],
                                            pT_h[0:nr, u % RING, :].bitcast(F32), ALU.subtract).then_inc(ptl_done, 1)

                last = None
                for slot in slots:
                    for at, n, r0, heads, c, w in slot["pieces"]:
                        dve.wait_ge(rows_done, g * PIECES + at + 1)
                        after(dve, shift_done, g * NT, n - MAXIMA + 1)
                        nc.vector.tensor_reduce(nmx[:, n % MAXIMA, c // HALF, r0:r0 + heads],
                                                bank[:, at % 2, 0:heads * w].rearrange("p (r n) -> p r n", r=heads),
                                                AX, ALU.max, negate=True).then_inc(max_done, 1)
                        if at + 1 == piece_end[n] and n in wide:
                            dve.wait_ge(max_done, g * PIECES + at + 1)
                            nc.vector.tensor_tensor(nmx[:, n % MAXIMA, 0, :], nmx[:, n % MAXIMA, 0, :], nmx[:, n % MAXIMA, 1, :],
                                                    ALU.min).then_inc(both_done, 1)
                    if last:
                        low_part(*last)
                    last = slot["unit"]
                    for step, n in enumerate((COMPRESS[0], COMPRESS[1], COMPRESS[1] + 2)):
                        if slot["n"] == n:
                            compressed(step)
                    if slot["turn"] is not None:
                        n = slot["turn"]
                        i, kind = tasks[n][0:2]
                        dve.wait_ge(turned, g * NT + n + 1)
                        o = bank[:, 7, 0:REP * (HD + 1)].rearrange("p (r d) -> p r d", r=REP)
                        ch.link(nc.vector.reciprocal(wtmp[:, :], o[:, :, HD:HD + 1].rearrange("p r d -> p (r d)")))
                        if kind == "cmp" and i == 0:
                            ch.link(nc.vector.tensor_scalar(wtmp[:, :], wtmp[:, :], any31[:, 0:1], None, ALU.mult))
                        gate = glog[:, i, :].rearrange("p (r b) -> p r b", b=3)[:, :, BRANCH[kind]]
                        ch.link(nc.vector.tensor_tensor(wgt[:, :], wtmp[:, :], gate, ALU.mult))
                        if n >= 4:
                            dve.wait_ge(final_done, g * TT + (n - 4) // 3 + 1)
                        nc.vector.tensor_tensor(o_gated[:, n % 4, :].rearrange("p (r d) -> p r d", r=REP), o[:, :, 0:HD],
                                                wgt[:, :].unsqueeze(2).broadcast_to([P, REP, HD]), ALU.mult).then_inc(gated, 1)
                    if slot["final"] is not None:
                        i = slot["final"]
                        dve.wait_ge(oh_done, g * TT + i + 1)
                        q0 = TILE_ORDER[i] * P
                        o = [a[:, bass.ds(g * 2, 2), q0:q0 + P] for a in (outb_h, outb_l)]
                        nc.vector.tensor_tensor(o[1], bank[:, 2, 0:2 * P].rearrange("p (b n) -> p b n", b=2),
                                                o[0].bitcast(F32), ALU.subtract).then_inc(ol_done, 1)
                ch.leave(GROUPS)

            def low(turn, per, m, dst, src, hi):
                dve.wait_ge(ph_done, turn * per + (m + 1))
                nc.vector.tensor_tensor(dst, src, hi.bitcast(F32), ALU.subtract).then_inc(pl_done, 1)

            def low_ring(turn, m, slot):
                low(turn, 4, m, ring_l[:, slot, :], raw[:, slot, :], ring_h[:, slot, :])

            def merge(b, turn, m0, c0, t0, last=False):
                for a in range(2):
                    low_ring(turn, m0 + 2 * a + 1, 1)
                    if not (last and a == 1):
                        low_ring(turn, m0 + 2 * a + 2, 0)
                    dve.wait_ge(sig_done, turn * 2 + (t0 + a + 1))
                    dve.wait_ge(mm_done, turn * 4 + (2 + c0 + 2 * a + 2))
                    for h in range(2):
                        o = sig[:, a, h * HALF:(h + 1) * HALF]
                        nc.vector.tensor_tensor(o, o, bank[:, 2 * (2 * a + 1) + h, :], ALU.mult).then_inc(freed, 1)
                    dve.wait_ge(freed, turn * 4 + (4 + c0 + 2 * a + 2))
                    dst = merged[:, bass.ds(turn * 2 + a, 1), :].rearrange("p a n -> p (a n)")
                    if b == 1:
                        nc.vector.tensor_copy(dst, sig[:, a, :]).then_inc(acc_done, 1)
                    else:
                        nc.vector.tensor_tensor(dst, dst, sig[:, a, :], ALU.add).then_inc(acc_done, 1)

            def own(semaphore, value):
                dve.wait_ge(semaphore, value)

            low_ring(0, 0, 0)
            with dve.Fori(0, KT // 2) as t:
                merge(1, t, PIECE["merge1"], CHUNK["merge1"], 0)

            ch.link(nc.vector.memset(conv_u[:, :, 0:2], 0.0))
            for c in range(3 * BK):
                m, ck_ = PIECE["conv"] + c, CHUNK["conv"] + c
                q = c // 3
                low_ring(0, m + 1, (c + 1) % 2)
                ps = flat[:, (ck_ % 4) * 1024:(ck_ % 4 + 1) * 1024]
                u_, o_ = conv_u[:, q % 2, :], conv_o[:, q % 2, :]
                if c % 3 == 1:
                    dve.wait_ge(convc_done, q + 1)
                    dve.wait_ge(mm_done, 2 + ck_ + 1)
                    for h in range(2):
                        nc.vector.tensor_tensor(u_[:, 2 + h * HALF:2 + (h + 1) * HALF], conv_c[:, q % 2, h * HALF:(h + 1) * HALF],
                                                ps[:, h * HALF:(h + 1) * HALF], ALU.mult).then_inc(freed, 1)
                    own(freed, 4 + ck_ + 1)
                    taps = [chan[:, C_CA + j * BK + q:C_CA + j * BK + q + 1] for j in range(3)]
                    if q >= 2:
                        dve.wait_ge(obl_done, q - 1)
                    ch.link(nc.vector.tensor_scalar(o_, u_[:, 0:S], taps[0], None, ALU.mult))
                    ch.link(nc.vector.scalar_tensor_tensor(o_, u_[:, 1:S + 1], taps[1], o_, ALU.mult, ALU.add))
                    ch.link(nc.vector.scalar_tensor_tensor(o_, u_[:, 2:S + 2], taps[2], o_, ALU.mult, ALU.add))
                if c % 3 == 2:
                    dve.wait_ge(mm_done, 2 + ck_ + 1)
                    nc.vector.tensor_tensor(o_, o_, ps, ALU.mult).then_inc(freed, 1)
                    dve.wait_ge(obh_done, q + 1)
                    nc.vector.tensor_tensor(outb_l[:, q, :], o_, outb_h[:, q, :].bitcast(F32), ALU.subtract).then_inc(obl_done, 1)
            with dve.Fori(0, KT // 2) as t:
                merge(0, t, PIECE["merge0"], CHUNK["merge0"], KT)

            dve.wait_ge(poolw_h, 1)
            own(obl_done, BK)
            nc.vector.tensor_tensor(pool_wl[:, :, :], pool_w32[:, :, :], pool_wh[:, :, :].bitcast(F32), ALU.subtract).then_inc(poolw_l, 1)
            dve.wait_ge(iota_done, 1)
            for q, w in enumerate(POOL_WINDOWS):
                ch.link(nc.vector.tensor_scalar(pool_inv[:, q, :], pool_t16[:, :], float(w), None, ALU.min))
            ch.link(nc.vector.reciprocal(pool_inv[:, :, :], pool_inv[:, :, :]))
            ch.link(nc.vector.memset(pool_p[:, :, 0:16], 0.0))
            ch.link(nc.vector.memset(pool_s[:, :, 0:16], 0.0))

            def pool_low(q):
                dve.wait_ge(obh_done, BK + q + 1)
                nc.vector.scalar_tensor_tensor(outb_l[:, q, :], flat[:, (2 + q % 2) * 1024:(3 + q % 2) * 1024],
                                               chan[:, C_PS + q:C_PS + q + 1], outb_h[:, q, :].bitcast(F32),
                                               ALU.mult, ALU.subtract).then_inc(obl_done, 1)

            for q, w in enumerate(POOL_WINDOWS):
                if q < BK - 1:
                    low_ring(0, PIECE["pool"] + q + 1, (q + 1) % 2)
                if q >= 1:
                    pool_low(q - 1)
                dve.wait_ge(poolp_done, q + 1)
                if q == 0:
                    dve.sem_inc(freed, 1)
                else:
                    dve.sem_inc(freed, 1)
                cur_, shift, k = pool_p[:, q % 2, :], 1, 0
                while shift < w:
                    nxt = pool_s[:, k % 2, :]
                    ch.link(nc.vector.tensor_tensor(nxt[:, 16:], cur_[:, 16:], cur_[:, 16 - shift:S + 16 - shift], ALU.add))
                    cur_, shift, k = nxt, shift * 2, k + 1
                p_ = pool_p[:, q % 2, 16:]
                if q >= 1:
                    dve.wait_ge(pooldl_done, q)
                ch.link(nc.vector.scalar_tensor_tensor(pool_d[:, :], cur_[:, 16:], 1.0 / w, p_, ALU.mult, ALU.subtract))
                ch.link(nc.vector.tensor_tensor(pool_t16[:, :], cur_[:, 16:32], pool_inv[:, q, :], ALU.mult))
                nc.vector.tensor_tensor(pool_d[:, 0:16], pool_t16[:, :], p_[:, 0:16], ALU.subtract).then_inc(poold_done, 1)
                dve.wait_ge(pooldh_done, q + 1)
                nc.vector.tensor_tensor(pool_dl[:, :], pool_d[:, :], pool_dh[:, :].bitcast(F32), ALU.subtract).then_inc(pooldl_done, 1)
            pool_low(BK - 1)

            own(obl_done, 2 * BK)
            for c in range(4):
                low(0, 4, PIECE["v"] + c, wv_l[:, 2 * c:2 * c + 2, :], raw[:, c % 2, :].rearrange("p (k n) -> p k n", k=2),
                    wv_h[:, 2 * c:2 * c + 2, :])
            low_ring(0, PIECE["merge2"], 0)
            for t in range(TT):
                dve.wait_ge(gelu_done, t + 1)
                ch.link(nc.vector.tensor_tensor(sgu_sq[:, :], sgu_v[:, t, :], sgu_v[:, t, :], ALU.mult))
                ch.link(nc.vector.tensor_reduce(va[:, 3, t:t + 1], sgu_sq[:, :], AX, ALU.add))
            nc.vector.tensor_scalar(va[:, 0, :], va[:, 3, :], 1.0 / BW, EPS, ALU.mult, ALU.add).then_inc(va_done, 1)
            inverse_root(va[:, 0, :], va[:, 1, :], va[:, 2, :], va[:, 3, :], TT, vr_done, 1)
            dve.wait_ge(sguc_loaded, 48)
            for t in range(TT):
                nc.vector.scalar_tensor_tensor(sgu_v[:, t, :], sgu_v[:, t, :], va[:, 2, t:t + 1], sgu_g[:, :],
                                               ALU.mult, ALU.mult).then_inc(vn_done, 1)
            with dve.Fori(0, KT // 2) as t:
                merge(2, t, PIECE["merge2"], CHUNK["merge2"], 2 * KT)
            for q in range(BK):
                low_ring(0, PIECE["u"] + q + 1, (q + 1) % 2)
                dve.wait_ge(u_done, q + 1)
                dve.sem_inc(freed, 1)
            dve.wait_ge(swh_done, 1)
            nc.vector.tensor_tensor(sgu_wl[:, :, :], bank[:, 4, :].rearrange("p (g t) -> p g t", g=BK),
                                    sgu_wh[:, :, :].bitcast(F32), ALU.subtract).then_inc(swl_done, 1)
            own(vn_done, TT)
            for t in range(TT + 1):
                if t < TT:
                    dve.wait_ge(vsh_done, t + 1)
                    nc.vector.tensor_tensor(sgu_vl[:, t % 2, :], sgu_v[:, t, :], sgu_vh[:, t % 2, :].bitcast(F32),
                                            ALU.subtract).then_inc(vsl_done, 1)
                if t >= 1:
                    k, o = t - 1, sgu_m[(t - 1) % 2][:, :, :]
                    dve.wait_ge(mix_mm, k + 1)
                    if k >= 2:
                        own(obl_done, 2 * BK + k - 1)
                    ch.link(nc.vector.tensor_tensor(o, bank[:, 6 + k % 2, :].rearrange("p (g t) -> p g t", g=BK),
                                                    sgu_bias[:, :, :], ALU.add))
                    nc.vector.tensor_tensor(o, o, sgu_u[:, :, k * P:(k + 1) * P], ALU.mult).then_inc(mix_done, 1)
                    dve.wait_ge(obh_done, 2 * BK + k + 1)
                    nc.vector.tensor_tensor(outb_l[:, :, k * P:(k + 1) * P], o, outb_h[:, :, k * P:(k + 1) * P].bitcast(F32),
                                            ALU.subtract).then_inc(obl_done, 1)
            with dve.Fori(0, KT // 2 - 1) as t:
                merge(3, t, PIECE["merge3"], CHUNK["merge3"], 3 * KT)
            merge(3, KT // 2 - 1, PIECE["merge3"], CHUNK["merge3"], 3 * KT, last=True)

            own(acc_done, 2 + 4 * KT)
            for k in range(KT):
                dve.wait_ge(mgh_done, k + 1)
                nc.vector.tensor_tensor(actT_l[:, k, :], merged[:, k, :], actT_h[:, k, :].bitcast(F32), ALU.subtract).then_inc(mgl_done, 1)
                low(0, 4, PIECE["wo"] + k, wo_l[:, k, :], raw[:, k % 2, :], wo_h[:, k, :])

            def normed(t):
                if t >= 2:
                    dve.wait_ge(xT_done, TT + t - 1)
                nc.vector.tensor_scalar(xn2[:, t % 2, :], x2[:, t, :], x2a[:, 2, t:t + 1], None, ALU.mult).then_inc(xn_done, 1)

            for tg in range(2):
                for t in range(4 * tg, 4 * tg + 4):
                    dve.wait_ge(x2_loaded, 16 * (t + 1))
                    dve.wait_ge(wo_mm, t + 1)
                    nc.vector.tensor_tensor(x2[:, t, :], x2[:, t, :], flat[:, (t % 4) * 1024:(t % 4 + 1) * 1024], ALU.add).then_inc(x2_done, 1)
                dve.wait_ge(sq_done, TT + 4 * tg + 4)
                some = slice(4 * tg, 4 * tg + 4)
                nc.vector.tensor_scalar(x2a[:, 0, some], ssq[:, some], 1.0 / DM, EPS, ALU.mult, ALU.add).then_inc(xa_done, 1)
                inverse_root(x2a[:, 0, some], x2a[:, 1, some], x2a[:, 2, some], x2a[:, 3, some], 4, xr_done, TT + tg + 1)
                if tg == 0:
                    normed(0)
                    normed(1)
            for t in range(TT + 1):
                if t < TT:
                    b = t % 2
                    dve.wait_ge(xT_done, TT + t + 1)
                    if t >= 2:
                        own(xl_done, TT + t - 1)
                    src = bank[:, 2 * b:2 * b + 2, :].rearrange("p b (k n) -> p (b k) n", n=P)
                    nc.vector.tensor_tensor(xv2[:, b, :, :], src, chan[:, C_G2:C_G2 + KT].unsqueeze(2).broadcast_to([P, KT, P]),
                                            ALU.mult).then_inc(xv_done, 1)
                    if t + 2 < TT:
                        normed(t + 2)
                if t >= 1:
                    dve.wait_ge(xh_done, TT + t)
                    cols = slice((t - 1) * P, t * P)
                    nc.vector.tensor_tensor(actT_l[:, :, cols], xv2[:, (t - 1) % 2, :, :], actT_h[:, :, cols].bitcast(F32),
                                            ALU.subtract).then_inc(xl_done, 1)
            low_ring(0, PIECE["ff"], 0)
            ch.link(nc.vector.memset(ffg[:, :, 0:2], 0.0))

            def add_down(turn):
                for t in range(TT):
                    dve.wait_ge(d_mm, (turn - 1) * TT + (t + 1))
                    nc.vector.tensor_tensor(x2[:, t, :], x2[:, t, :], flat[:, (2 + t % 2) * 1024:(3 + t % 2) * 1024],
                                            ALU.add).then_inc(d_done, 1)

            def ff(turn, last=False):
                m0, c0 = PIECE["ff"], CHUNK["ff"]
                for a in range(2):
                    low_ring(turn, m0 + 2 * a + 1, 1)
                    dve.wait_ge(gcopy_done, turn * 2 + (a + 1))
                    dve.sem_inc(freed, 1)
                    g_, o_ = ffg[:, a, :], ffc[:, a, :]
                    taps = [chan[:, bass.ds(turn * 2 + (C_CF + j * FT + a), 1)] for j in range(3)]
                    if not (isinstance(turn, int) and turn == 0):
                        own(ffl_done, (turn - 1) * 2 + (a + 1))
                    ch.link(nc.vector.tensor_scalar(o_, g_[:, 0:S], taps[0], None, ALU.mult))
                    ch.link(nc.vector.scalar_tensor_tensor(o_, g_[:, 1:S + 1], taps[1], o_, ALU.mult, ALU.add))
                    nc.vector.scalar_tensor_tensor(o_, g_[:, 2:S + 2], taps[2], o_, ALU.mult, ALU.add).then_inc(ffc_done, 1)
                    if a == 0 and not (isinstance(turn, int) and turn == 0):
                        add_down(turn)
                    if a == 1:
                        for k in range(2):
                            dve.wait_ge(wdh_done, turn * 2 + (k + 1))
                            nc.vector.tensor_tensor(wd_l[:, k, :], wd_raw[:, k, :], wd_h[:, k, :].bitcast(F32),
                                                    ALU.subtract).then_inc(wdl_done, 1)
                    if not (last and a == 1):
                        low_ring(turn, m0 + 2 * a + 2, 0)
                    dve.wait_ge(silu_done, turn * 2 + (a + 1))
                    dve.wait_ge(mm_done, turn * 4 + (2 + c0 + 2 * a + 2))
                    nc.vector.tensor_tensor(o_, o_, flat[:, 1024:2048], ALU.mult).then_inc(freed, 1)
                    dve.wait_ge(ffh_done, turn * 2 + (a + 1))
                    nc.vector.tensor_tensor(ffa_l[:, a, :], o_, ffa_h[:, a, :].bitcast(F32), ALU.subtract).then_inc(ffl_done, 1)

            ff(0)
            ch_base = ch.n
            with dve.Fori(1, FT // 2 - 1) as t:
                ch.enter(t - 1, 4)
                ff(t)
                ch.leave(FT // 2 - 2)
            ff(FT // 2 - 1, last=True)
            add_down(FT // 2)

        @block.tensor
        def _(pe):
            pe.wait_ge(consts_made, 12)
            pe.wait_ge(const_loaded, 16 * 7)
            nc.tensor.transpose(bank[:, 6, 0:CHAN], chan_rows[:, :], ident[0:CHAN, 0:CHAN])
            nc.tensor.transpose(bank[:, 6, CHAN:CHAN + 2 * L16], pe_rows[:, :], ident[0:2 * L16, 0:2 * L16]).then_inc(chan_turned, 1)
            for t in range(TT):
                pe.wait_ge(xn_done, t + 1)
                if t >= 2:
                    pe.wait_ge(xv_done, t - 1)
                for k in range(KT):
                    ins = nc.tensor.transpose(bank[:, 2 * (t % 2) + k // 4, (k % 4) * P:(k % 4 + 1) * P],
                                              xn[:, t % 2, k * P:(k + 1) * P], ident[:, :])
                ins.then_inc(xT_done, 1)
            pe.wait_ge(xv_done, TT)
            pe.wait_ge(chan_done, 1)

            with pe.Fori(0, GROUPS) as g:
                pe.wait_ge(wpl_done, g * SPLITS + SPLITS)

                def transposes(t):
                    pe.wait_ge(qkl_done, g * TT + t + 1)
                    after(pe, evq_done, g * TT, t)
                    after(pe, evk_done, g * TT, t)
                    for m in range(10):
                        ins = nc.tensor.transpose(bank[:, 4 + m // 4, (m % 4) * P:(m % 4 + 1) * P],
                                                  dup[:, t % 2, m, :], ident[:, :])
                    ins.then_inc(qkT_done, 1)

                for t in range(TT):
                    pe.wait_ge(xl_done, t + 1)
                    after(pe, pcopy_done, g * TT, t - 1)
                    A, B = bank[:, 2 * (t % 2), 0:QW], bank[:, 2 * (t % 2) + 1, 0:PW - QW]
                    for k in range(KT):
                        xh, xl = (a[:, k, t * P:(t + 1) * P] for a in (actT_h, actT_l))
                        first, last = k == 0, k == KT - 1
                        nc.tensor.matmul(A, xh, wp_h[:, k, 0:QW], start=first, stop=False)
                        nc.tensor.matmul(B, xh, wp_h[:, k, QW:PW], start=first, stop=False)
                        nc.tensor.matmul(A, xh, wp_l[:, k, 0:QW], start=False, stop=False)
                        nc.tensor.matmul(B, xh, wp_l[:, k, QW:PW], start=False, stop=False)
                        nc.tensor.matmul(A, xl, wp_h[:, k, 0:QW], start=False, stop=last)
                        ins = nc.tensor.matmul(B, xl, wp_h[:, k, QW:PW], start=False, stop=last)
                    ins.then_inc(proj_done, 1)
                    if t >= 1:
                        transposes(t - 1)
                transposes(TT - 1)

                def compressed(step):
                    if step == 0:
                        pe.wait_ge(w1_loaded, 16 * 4)
                        pe.wait_ge(evq_done, g * TT + TT)
                        for j in range(2):
                            for l in range(L16):
                                nc.tensor.matmul(bank[0:HD, 7, j * HD:j * HD + NCMP], w1[:, j, l, :],
                                                 kcT[:, j, l:l + CMP_STRIDE * (NCMP - 1) + 1:CMP_STRIDE],
                                                 start=l == 0, stop=l == L16 - 1)
                            for l in range(L16):
                                ins = nc.tensor.matmul(bank[0:HD, 7, 128 + 64 * j:129 + 64 * j], w1[:, j, l, :],
                                                       peT[:, j, l:l + 1], start=l == 0, stop=l == L16 - 1)
                    elif step == 1:
                        pe.wait_ge(c_act, g * 3 + 1)
                        pe.wait_ge(const2_loaded, 32)
                        pe.sem_inc(passed, 1)
                        for j in range(2):
                            ins = nc.tensor.matmul(bank[0:NCMP, 7, 256 + j * HD:256 + (j + 1) * HD], h1[:, j, 0:NCMP],
                                                   w2[:, j, :], start=True, stop=True)
                    else:
                        pe.wait_ge(c_dve, g * 4 + 4)
                        pe.sem_inc(passed, 1)
                        for a in range(2):
                            ins = nc.tensor.transpose(bank[:, 7, 384 + a * CW:384 + a * CW + NCMP],
                                                      ckd[0:NCMP, a, :, :].rearrange("n u d -> n (u d)"), ident[0:NCMP, 0:NCMP])
                    ins.then_inc(c_pe, 1)

                def rows(at, n, r0, heads, c, w):
                    i, kind, k0, keys, blocks = tasks[n]
                    after(pe, max_done, g * PIECES, at - 1)
                    masks = []
                    if kind == "cmp":
                        masks.append((0, CW, cmask[:, i, :]))
                    else:
                        if kind == "win" and i >= WIN // P and c == 0:
                            masks.append((0, P, wstart[:, :]))
                        if c + w == keys:
                            masks.append((w - P, P, tri[:, :]))
                    for r in range(heads):
                        o = bank[:, at % 2, r * w:(r + 1) * w]
                        kh = kcAB[:, 0, :] if kind == "cmp" else kAB[:, 2 * (kind == "win"), k0 + c:k0 + c + w]
                        ins = nc.tensor.matmul(o, qT[:, r0 + r, i * P:(i + 1) * P], kh, start=True, stop=not masks)
                        for m, (a, mw, mask) in enumerate(masks):
                            ins = nc.tensor.matmul(o[:, a:a + mw], identb[:, :], mask, start=False, stop=m == len(masks) - 1)
                    ins.then_inc(rows_done, 1)

                def scores(u, n, j):
                    i, kind, k0, keys, blocks = tasks[n]
                    if j == 0:
                        pe.wait_ge(shift_done, g * NT + n + 1)
                    after(pe, exp_done, g * UNITS, u - 1)
                    q = qT[:, :, i * P:(i + 1) * P]
                    if kind == "cmp":
                        pe.sem_inc(passed, 1)
                        nr, kh, kl, mask = CW, kcAB[:, 0, :], kcAB[:, 1, :], cmask[:, i, :]
                    else:
                        nr, at = P, k0 + j * P
                        kh, kl = (kAB[:, 2 * (kind == "win") + a, at:at + P] for a in range(2))
                        mask = tri[:, :] if j == blocks - 1 else None
                        if kind == "win" and i >= WIN // P and j == 0:
                            mask = wstart[:, :]
                    o = bank[0:nr, 3 + u % 2, :]
                    nc.tensor.matmul(o, kh, q, start=True, stop=False)
                    nc.tensor.matmul(o, kl, q, start=False, stop=False)
                    if mask is not None:
                        nc.tensor.matmul(o, mask, identb[:, :].unsqueeze(1).broadcast_to([P, REP, P]), start=False, stop=False)
                    nc.tensor.matmul(o, ones[:, 0:nr], shift[:, n % MAXIMA, :, :], start=False, stop=True).then_inc(s_done, 1)

                def values(u, n, j):
                    i, kind, k0, keys, blocks = tasks[n]
                    pe.wait_ge(ptl_done, g * UNITS + u + 1)
                    if j == 0:
                        after(pe, evac_done, g * NT, n - 1)
                    pe.sem_inc(passed, 1)
                    if kind == "cmp":
                        nr, vh, vl = CW, vc_h[:, :], vc_l[:, :]
                    else:
                        ty = 0 if kind == "slc" else 1
                        nr, vh, vl = P, v_h[:, ty, k0 // P + j, :], v_l[:, ty, k0 // P + j, :]
                    o = bank[0:HD + 1, 5 + n % 2, :]
                    nc.tensor.matmul(o, vh, pT_h[0:nr, u % RING, :], start=j == 0, stop=False)
                    nc.tensor.matmul(o, vh, pT_l[0:nr, u % RING, :], start=False, stop=False)
                    nc.tensor.matmul(o, vl, pT_h[0:nr, u % RING, :], start=False, stop=j == blocks - 1).then_inc(pv_done, 1)

                pe.wait_ge(c_dve, g * 4 + 1)
                pe.wait_ge(evq_done, g * TT + TT)
                pe.wait_ge(evk_done, g * TT + TT)
                for slot in slots:
                    if slot["n"] in COMPRESS:
                        compressed(COMPRESS.index(slot["n"]))
                    if slot["n"] == COMPRESS[2] + 1:
                        pe.wait_ge(c_act, g * 3 + 3)
                    for piece in slot["pieces"]:
                        rows(*piece)
                    if slot["unit"]:
                        scores(*slot["unit"])
                    if slot["values"]:
                        values(*slot["values"])
                    if slot["turn"] is not None:
                        n = slot["turn"]
                        pe.wait_ge(evac_done, g * NT + n + 1)
                        after(pe, gated, g * NT, n)
                        pe.sem_inc(passed, 1)
                        for r in range(REP):
                            ins = nc.tensor.transpose(bank[:, 7, r * (HD + 1):(r + 1) * (HD + 1)],
                                                      oT[:, n % 2, r * P:(r + 1) * P], ident[0:HD + 1, 0:HD + 1])
                        ins.then_inc(turned, 1)
                    if slot["final"] is not None:
                        i = slot["final"]
                        pe.wait_ge(summed, g * TT + i + 1)
                        after(pe, ol_done, g * TT, i)
                        for b in range(2):
                            ins = nc.tensor.transpose(bank[:, 2, b * P:(b + 1) * P],
                                                      o_gated[:, 3 * i % 4, b * P:(b + 1) * P], ident[:, :])
                        ins.then_inc(final_done, 1)
                pe.wait_ge(exp_done, g * UNITS + UNITS)
                pe.wait_ge(ol_done, g * TT + TT)

            def product(k_tiles, wh, wl, ah, al, out_bank):
                for h in range(2):
                    cols = slice(h * HALF, (h + 1) * HALF)
                    for k in range(k_tiles):
                        o = bank[:, out_bank + h, :]
                        nc.tensor.matmul(o, wh(k), ah[:, k, cols], start=k == 0, stop=False)
                        nc.tensor.matmul(o, wh(k), al[:, k, cols], start=False, stop=False)
                        ins = nc.tensor.matmul(o, wl(k), ah[:, k, cols], start=False, stop=k == k_tiles - 1)
                return ins

            def chunk(turn, m, c, slot, k_tiles, ah, al, tile):
                pe.wait_ge(pl_done, turn * 4 + (2 + m + 1))
                pe.wait_ge(freed, turn * 4 + (c + 1))
                product(k_tiles, lambda k: ring_h[:, slot, k * P:(k + 1) * P], lambda k: ring_l[:, slot, k * P:(k + 1) * P],
                        ah, al, 2 * tile).then_inc(mm_done, 1)

            def merge(turn, m0, c0, branch_ready):
                for a in range(2):
                    chunk(turn, m0 + 2 * a, c0 + 2 * a, 0, KT, actT_h, actT_l, 2 * a)
                    if branch_ready:
                        pe.wait_ge(obl_done, branch_ready)
                    chunk(turn, m0 + 2 * a + 1, c0 + 2 * a + 1, 1, BK, outb_h, outb_l, 2 * a + 1)

            pe.sem_inc(mm_done, 2)
            with pe.Fori(0, KT // 2) as t:
                merge(t, PIECE["merge1"], CHUNK["merge1"], 0)
            for c in range(3 * BK):
                chunk(0, PIECE["conv"] + c, CHUNK["conv"] + c, c % 2, KT, actT_h, actT_l, (CHUNK["conv"] + c) % 4)
            with pe.Fori(0, KT // 2) as t:
                merge(t, PIECE["merge0"], CHUNK["merge0"], BK)

            def pool_product(q):
                pe.wait_ge(poolw_l, 1)
                pe.wait_ge(pooldl_done, q + 1)
                if q < 2:
                    pe.wait_ge(freed, 4 + CHUNK["pool"] - 2 + q + 1)
                else:
                    pe.wait_ge(obl_done, BK + q - 1)
                for h in range(2):
                    cols = slice(h * HALF, (h + 1) * HALF)
                    o = bank[:, 2 * (2 + q % 2) + h, :]
                    nc.tensor.matmul(o, pool_wh[:, q, :], pool_dh[:, cols], start=True, stop=False)
                    nc.tensor.matmul(o, pool_wh[:, q, :], pool_dl[:, cols], start=False, stop=False)
                    ins = nc.tensor.matmul(o, pool_wl[:, q, :], pool_dh[:, cols], start=False, stop=True)
                ins.then_inc(pooly_mm, 1)

            for q in range(BK):
                ready = CHUNK["pool"] + q - (4 if q < 2 else 2)
                pe.wait_ge(freed, 4 + ready + 1)
                chunk(0, PIECE["pool"] + q, CHUNK["pool"] + q, q % 2, KT, actT_h, actT_l, q % 2)
                if q >= 1:
                    pool_product(q - 1)
            pool_product(BK - 1)

            pe.wait_ge(pl_done, 2 + PIECE["v"] + 4)
            pe.wait_ge(freed, 4 + CHUNK["merge2"])
            for t in range(TT):
                if t >= 4:
                    pe.wait_ge(obl_done, 2 * BK)
                for k in range(KT):
                    xh, xl = (a[:, k, t * P:(t + 1) * P] for a in (actT_h, actT_l))
                    nc.tensor.matmul(bank[:, t, :], xh, wv_h[:, k, :], start=k == 0, stop=False)
                    nc.tensor.matmul(bank[:, t, :], xh, wv_l[:, k, :], start=False, stop=False)
                    ins = nc.tensor.matmul(bank[:, t, :], xl, wv_h[:, k, :], start=False, stop=k == KT - 1)
                ins.then_inc(v_mm, 1)
            pe.wait_ge(gelu_done, TT)
            with pe.Fori(0, KT // 2) as t:
                merge(t, PIECE["merge2"], CHUNK["merge2"], 2 * BK)
            for q in range(BK):
                chunk(0, PIECE["u"] + q, CHUNK["u"] + q, q % 2, KT, actT_h, actT_l, q)
            pe.wait_ge(sguw_masked, 1)
            pe.wait_ge(freed, 4 + CHUNK["merge3"])
            for g4 in range(BK):
                ins = nc.tensor.transpose(bank[:, 4, g4 * P:(g4 + 1) * P], sgu_w32[:, g4, :], ident[:, :])
            ins.then_inc(swT_done, 1)
            pe.wait_ge(swl_done, 1)
            for t in range(TT):
                pe.wait_ge(vsl_done, t + 1)
                if t >= 2:
                    pe.wait_ge(mix_done, t - 1)
                for g4 in range(BK):
                    o = bank[:, 6 + t % 2, g4 * P:(g4 + 1) * P]
                    vh, vl = (a[:, t % 2, g4 * P:(g4 + 1) * P] for a in (sgu_vh, sgu_vl))
                    nc.tensor.matmul(o, vh, sgu_wh[:, g4, :], start=True, stop=False)
                    nc.tensor.matmul(o, vh, sgu_wl[:, g4, :], start=False, stop=False)
                    ins = nc.tensor.matmul(o, vl, sgu_wh[:, g4, :], start=False, stop=True)
                ins.then_inc(mix_mm, 1)
            with pe.Fori(0, KT // 2) as t:
                merge(t, PIECE["merge3"], CHUNK["merge3"], 2 * BK + TT)

            for tg in range(2):
                for k in range(KT):
                    if tg == 0:
                        pe.wait_ge(mgl_done, k + 1)
                        pe.wait_ge(pl_done, 2 + PIECE["wo"] + k + 1)
                        if k == 0:
                            pe.wait_ge(freed, 4 + CHUNK["ff"])
                    for tl in range(4):
                        t = 4 * tg + tl
                        if tg == 1 and k == 0:
                            pe.wait_ge(x2_done, tl + 1)
                        mh, ml = (a[:, k, t * P:(t + 1) * P] for a in (actT_h, actT_l))
                        o = [bank[:, 2 * tl + h, :] for h in range(2)]
                        w = [[a[:, k, h * HALF:(h + 1) * HALF] for h in range(2)] for a in (wo_h, wo_l)]
                        first, last = k == 0, k == KT - 1
                        for h in range(2):
                            nc.tensor.matmul(o[h], mh, w[0][h], start=first, stop=False)
                        for h in range(2):
                            nc.tensor.matmul(o[h], mh, w[1][h], start=False, stop=False)
                        for h in range(2):
                            ins = nc.tensor.matmul(o[h], ml, w[0][h], start=False, stop=last)
                        if last:
                            ins.then_inc(wo_mm, 1)
            for t in range(TT):
                pe.wait_ge(xn_done, TT + t + 1)
                pe.wait_ge(x2_done, min(t + 5, TT))
                if t >= 2:
                    pe.wait_ge(xv_done, TT + t - 1)
                for k in range(KT):
                    ins = nc.tensor.transpose(bank[:, 2 * (t % 2) + k // 4, (k % 4) * P:(k % 4 + 1) * P],
                                              xn2[:, t % 2, k * P:(k + 1) * P], ident[:, :])
                ins.then_inc(xT_done, 1)
            pe.wait_ge(xl_done, 2 * TT)

            def down(turn):
                pe.wait_ge(ffl_done, turn * 2)
                pe.wait_ge(wdl_done, turn * 2 + 2)
                for t in range(TT):
                    pe.wait_ge(d_done, (turn - 1) * TT + (t + 1))
                    o = [bank[:, 4 + 2 * (t % 2) + h, :] for h in range(2)]
                    for k in range(2):
                        ah, al = (a[:, k, t * P:(t + 1) * P] for a in (ffa_h, ffa_l))
                        for n, (av, w) in enumerate(((ah, wd_h), (ah, wd_l), (al, wd_h))):
                            for h in range(2):
                                ins = nc.tensor.matmul(o[h], av, w[:, k, h * HALF:(h + 1) * HALF],
                                                       start=k == 0 and n == 0, stop=k == 1 and n == 2)
                    ins.then_inc(d_mm, 1)

            def ff(turn):
                m0, c0 = PIECE["ff"], CHUNK["ff"]
                for c in range(4):
                    if not (isinstance(turn, int) and turn == 0 and c < 2):
                        pe.wait_ge(freed, turn * 4 + (4 + c0 + c - 1))
                    chunk(turn, m0 + c, c0 + c, c % 2, KT, actT_h, actT_l, c % 2)
                    if c == 0 and not (isinstance(turn, int) and turn == 0):
                        down(turn)

            ff(0)
            with pe.Fori(1, FT // 2 - 1) as t:
                ff(t)
            ff(FT // 2 - 1)
            down(FT // 2)


_INS = ["x", "norm1_g", "w_in", "conv_a_w", "qk_norm_g", "cmp_pe", "cmp_w1", "cmp_w2", "pool_w", "pool_scale",
        "sgu_norm_g", "sgu_w", "sgu_b", "w_branch", "w_o", "norm2_g", "w_up", "conv_ff_w", "w_down"]


def kernel(**inputs):
    import concourse.bacc as bacc
    from concourse.bass_utils import run_bass_kernel_spmd as run

    nc = bacc.Bacc("TRN2", target_bir_lowering=False, num_devices=1)
    arrays, args = {}, []
    for name in _INS:
        a = np.ascontiguousarray(inputs[name])
        arrays[f"in_{name}"] = a
        args.append(nc.dram_tensor(f"in_{name}", a.shape, mybir.dt.from_np(a.dtype), kind="ExternalInput").ap())
    args.append(nc.dram_tensor("out_0", (1, S, DM), F32, kind="ExternalOutput").ap())
    build(nc, *args)
    return run(nc, [arrays], core_ids=[0]).results[0]["out_0"]
```

```python
from contextlib import ExitStack

import numpy as np

import concourse.bass as bass
from concourse import mybir

ALU = mybir.AluOpType
ACT = mybir.ActivationFunctionType
F32 = mybir.dt.float32
F32R = mybir.dt.float32r
BF16 = mybir.dt.bfloat16
AX = mybir.AxisListType.X

P = 128
S = 1024
DM = 1024
BW = 512
HD = 64
GROUPS = 2
REP = 4
CMP_STRIDE = 16
CMP_BLOCK = 32
WIN = 512
D_FF = 2816
EPS = 1e-6
NEG = -1e30
POOL_WINDOWS = (2, 4, 8, 16)

TT = S // P
KT = DM // P
BK = BW // P
FT = D_FF // P
HALF = 512
NCMP = (S - CMP_BLOCK) // CMP_STRIDE + 1
CW = NCMP + 1
L16 = CMP_BLOCK // 2
KV = GROUPS * HD

COL_Q = 3 * BW
COL_KV = COL_Q + BW
COL_GATE = COL_KV + 6 * KV
COL_POOL = COL_GATE + 3 * GROUPS * REP
COL_SGU = COL_POOL + BW
COL_MERGE = COL_SGU + 2 * BW

QW = REP * HD
GW = 3 * REP
PW = QW + 6 * HD + GW
SPLITS = 7
SPLIT_ORDER = (6, 0, 2, 3, 1, 4, 5)
POOL_SPLITS = (4, 5)
SPLIT_DMAS = {c: 2 if 2 <= c < 6 else 1 for c in SPLIT_ORDER}
CHAIN_TURN = 8 * TT + 11 + 2 * 3 * TT + 1

C_CA = 0
C_CF = C_CA + 3 * BK
C_PS = C_CF + 3 * FT
CHAN = C_PS + BK
SBUF_BASE = 16512
KB = 1024


class Chain:

    def __init__(self, eng, sem):
        self.eng, self.sem, self.n, self.base, self.at = eng, sem, 0, 0, 0

    def enter(self, i, per_turn):
        self.base, self.at, self.per_turn = i * per_turn, self.n, per_turn

    def leave(self, turns):
        assert self.n - self.at == self.per_turn, (self.n - self.at, self.per_turn)
        self.n, self.base = self.at + turns * self.per_turn, 0

    def mark(self, ins):
        ins.then_inc(self.sem, 1)
        self.n += 1

    def wait(self):
        self.eng.wait_ge(self.sem, self.base + self.n)

    def link(self, ins):
        self.mark(ins)
        self.wait()


STAGES = (("merge1", 16, 16), ("conv", 12, 12), ("merge0", 16, 16), ("v", 4, 0), ("pool", 4, 4), ("merge2", 16, 16),
          ("u", 4, 4), ("merge3", 16, 16), ("wo", 8, 0), ("ff", 2 * FT, 2 * FT))
PIECE = {name: sum(n for _, n, _ in STAGES[:i]) for i, (name, _, _) in enumerate(STAGES)}
CHUNK = {name: sum(n for _, _, n in STAGES[:i]) for i, (name, _, _) in enumerate(STAGES)}


def after(eng, semaphore, base, n):
    if n > 0:
        eng.wait_ge(semaphore, base + n)


TILE_ORDER = list(range(TT - 1, -1, -1))
COMPRESS = (3, 6, 10)


def attention_tasks():
    tasks = []
    for i in TILE_ORDER:
        first = max(0, i - WIN // P)
        tasks.append((i, "slc", 0, (i + 1) * P, i + 1))
        tasks.append((i, "win", first * P, (i + 1 - first) * P, i + 1 - first))
        tasks.append((i, "cmp", 0, CW, 1))
    return tasks


def attention_pieces(keys):
    pieces = []
    for c in range(0, keys, HALF):
        w = min(HALF, keys - c)
        heads = min(REP, HALF // w)
        heads = REP if heads == REP else 2 if heads >= 2 else 1
        pieces += [(r, heads, c, w) for r in range(0, REP, heads)]
    return pieces


LAG = 3
LEAD = 12
RING = 4
MAXIMA = 4


def attention_slots(tasks):
    units = [(n, j) for n, t in enumerate(tasks) for j in range(t[4])]
    pieces = [(n,) + p for n, t in enumerate(tasks) for p in attention_pieces(t[3])]
    first_unit = [units.index((n, 0)) for n in range(len(tasks))]
    last_unit = [first_unit[n] + tasks[n][4] - 1 for n in range(len(tasks))]
    slots, at = [], 0
    for u in range(len(units) + LAG + 4):
        slot = dict(n=u, pieces=[], unit=None, values=None, turn=None, sum=None, final=None, evacuate=None)
        ahead = units[min(u, len(units) - 1)][0] + MAXIMA - 1
        while at < len(pieces) and pieces[at][0] <= ahead and (tasks[pieces[at][0]][1] != "cmp" or u > COMPRESS[2]) and (
                first_unit[pieces[at][0]] <= u + 3 or at <= u + LEAD and len(slot["pieces"]) < 2):
            slot["pieces"].append((at,) + pieces[at])
            at += 1
        if u < len(units):
            slot["unit"] = (u,) + units[u]
        if LAG <= u < len(units) + LAG:
            slot["values"] = (u - LAG,) + units[u - LAG]
        for n, last in enumerate(last_unit):
            if last + LAG == u:
                slot["evacuate"] = n
            if last + LAG + 1 == u:
                slot["turn"] = n
            if last + LAG + 2 == u and n % 3 == 2:
                slot["sum"] = n // 3
            if last + LAG + 3 == u and n % 3 == 2:
                slot["final"] = n // 3
        slots.append(slot)
    assert at == len(pieces)
    return slots, last_unit, len(units), len(pieces)


def build(nc, x, norm1_g, w_in, conv_a_w, qk_norm_g, cmp_pe, cmp_w1, cmp_w2, pool_w, pool_scale,
          sgu_norm_g, sgu_w, sgu_b, w_branch, w_o, norm2_g, w_up, conv_ff_w, w_down, out):
    tasks = attention_tasks()
    slots, last_unit, UNITS, PIECES = attention_slots(tasks)
    NT = len(tasks)
    piece_end = [0] * NT
    for slot in slots:
        for at, n, *_ in slot["pieces"]:
            piece_end[n] = at + 1
    wide = [n for n, t in enumerate(tasks) if t[3] > HALF]
    both_at, BOTH = {n: k for k, n in enumerate(wide)}, len(wide)
    BRANCH = {"cmp": 0, "slc": 1, "win": 2}

    with ExitStack() as ctx:
        def place(name, at_kb, shape, dt):
            return nc.alloc_sbuf_tensor_at(name, shape, dt, offset=SBUF_BASE + int(at_kb * KB))

        def sem(name):
            return ctx.enter_context(nc.semaphore(name))

        actT_h = place("actT_h", 0, [P, KT, S], F32R)
        actT_l = place("actT_l", 32, [P, KT, S], F32R)
        outb_h = place("outb_h", 64, [P, BK, S], F32R)
        outb_l = place("outb_l", 80, [P, BK, S], F32R)
        x_in = place("x_in", 64, [P, TT, DM], F32)
        w1 = place("w1", 72, [P, 2, L16, HD], F32)
        kcT = place("kcT", 88, [P, 2, S], F32)
        raw = place("raw", 96, [P, 2, 1024], F32)
        kv_raw = place("kv_raw", 190, [P, 4, 12 * HD], F32)

        wp_h = place("wp_h", 104, [P, KT, PW], F32R)
        wp_l = place("wp_l", 104 + KT * PW * 4 / KB, [P, KT, PW], F32R)
        pT = place("pT", 104, [P, RING, HALF], F32)
        pT_h = place("pT_h", 112, [P, RING, HALF], F32R)
        pT_l = place("pT_l", 120, [P, RING, HALF], F32R)
        shift = place("shift", 128, [P, MAXIMA, REP, P], F32R)
        oT = place("oT", 136, [HD + 1, 2, HALF], F32)
        o_gated = place("o_gated", 140.5, [P, 4, REP * HD], F32)
        qT = place("qT", 146, [P, REP, S], F32R)
        kAB = place("kAB", 162, [P, 4, S], F32R)
        v_h = place("v_h", 178, [P, 2, TT, HD + 1], F32R)
        v_l = place("v_l", 182.0625, [P, 2, TT, HD + 1], F32R)
        xn = place("xn", 146, [P, 2, DM], F32)
        norm1_b = place("norm1_b", 154, [P, DM], F32)
        squares = place("squares", 162, [P, DM], F32)
        proj = place("proj", 186.125, [P, 2, PW], F32)
        dup = place("dup", 191.25, [P, 2, 10, P], F32)
        qkn = place("qkn", 201.25, [P, 6, HD], F32)
        ones = place("ones", 189, [P, P], F32R)
        h1 = place("h1", 186.25, [HD, 2, CW], F32)
        ck = place("ck", 187, [CW, HD], F32)
        ck2 = place("ck2", 187.25, [CW, HD], F32)
        ckd = place("ckd", 187.5, [CW, 2, 2, HD], F32)

        ring_h = place("ring_h", 104, [P, 2, 1024], F32R)
        ring_l = place("ring_l", 112, [P, 2, 1024], F32R)
        merged = place("merged", 120, [P, KT, S], F32)
        x2 = place("x2", 120, [P, TT, DM], F32)
        sig_all = place("sig_all", 152, [P, 2, S], F32)
        conv_c = place("conv_c", 160, [P, 2, S], F32)
        conv_u = place("conv_u", 168, [P, 2, S + 2], F32)
        conv_o = place("conv_o", 176.25, [P, 2, S], F32)
        sig_0 = place("sig_0", 184.25, [P, 2, S], F32)
        pool_p = place("pool_p", 152, [P, 2, S + 16], F32)
        pool_s = place("pool_s", 160.25, [P, 2, S + 16], F32)
        pool_d = place("pool_d", 168.5, [P, S], F32)
        pool_w32 = place("pool_w32", 168.5, [P, BK, P], F32)
        pool_dh = place("pool_dh", 172.5, [P, S], F32R)
        pool_dl = place("pool_dl", 176.5, [P, S], F32R)
        pool_wl = place("pool_wl", 180.5, [P, BK, P], F32R)
        pool_wh = place("pool_wh", 200, [P, BK, P], F32R)
        pool_inv = place("pool_inv", 182.5, [P, BK, 16], F32)
        pool_t16 = place("pool_t16", 182.75, [P, 16], F32)
        wv_h = place("wv_h", 152, [P, KT, BW], F32R)
        wv_l = place("wv_l", 168, [P, KT, BW], F32R)
        sgu_v = place("sgu_v", 184, [P, TT, BW], F32)
        sgu_sq = place("sgu_sq", 200, [P, BW], F32)
        sgu_g = place("sgu_g", 160, [P, BW], F32)
        sgu_bias = place("sgu_bias", 162, [P, BK, P], F32)
        sgu_w32 = place("sgu_w32", 164, [P, BK, P], F32)
        sgu_wh = place("sgu_wh", 166, [P, BK, P], F32R)
        sgu_wl = place("sgu_wl", 200, [P, BK, P], F32R)
        sgu_u = place("sgu_u", 168, [P, BK, S], F32)
        sgu_vh = place("sgu_vh", 152, [P, 4, BW], F32R)
        sgu_vl = place("sgu_vl", 184, [P, TT, BW], F32R)
        sgu_m = place("sgu_m", 184, [P, TT, BK, P], F32)
        wo_h = place("wo_h", 160, [P, KT, DM], F32R)
        wo_l0 = place("wo_l0", 192, [P, 2, DM], F32R)
        wo_l2 = place("wo_l2", 64, [P, KT - 2, DM], F32R)
        x2a = place("x2a", 202.5, [P, 4, TT], F32)
        xn2 = place("xn2", 88, [P, 2, DM], F32)
        norm2_b = place("norm2_b", 152, [P, DM], F32)
        squares2 = place("squares2", 156, [P, DM], F32)
        wd_raw = place("wd_raw", 64, [P, 2, DM], F32)
        wd_h = place("wd_h", 72, [P, 2, DM], F32R)
        wd_l = place("wd_l", 80, [P, 2, DM], F32R)
        ffc = place("ffc", 88, [P, 2, S], F32)
        ffa_h = place("ffa_h", 152, [P, 2, S], F32R)
        ffa_l = place("ffa_l", 160, [P, 2, S], F32R)
        ffg = place("ffg", 168, [P, 2, S + 2], F32)

        cur = [202.75]

        def small(name, shape, dt=F32):
            n = int(np.prod(shape[1:])) * (2 if dt == BF16 else 4)
            t = place(name, cur[0], shape, dt)
            cur[0] += -(-n // 32) * 32 / KB
            assert cur[0] <= 207.8, cur[0]
            return t

        ident = small("ident", [P, P])
        identb = small("identb", [P, P], BF16)
        tri = small("tri", [P, P], BF16)
        wstart = small("wstart", [P, P], BF16)
        cmask = small("cmask", [P, TT, CW], BF16)
        gains = small("gains", [P, 4, HD])
        chan = small("chan", [P, CHAN])
        graw = small("graw", [P, KT, GW])
        glog = small("glog", [P, TT, GW])
        any31 = small("any31", [P, 1])
        ssq = small("ssq", [P, TT])
        xa = small("xa", [P, 2, 4])
        qa = small("qa", [P, 6])
        qr = small("qr", [P, 6])
        qy = small("qy", [P, 6])
        qt = small("qt", [P, 6])
        nmx = small("nmx", [P, MAXIMA, 2, REP])
        wgt = small("wgt", [P, REP])
        wtmp = small("wtmp", [P, REP])
        peT = small("peT", [P, 2, L16])
        cbias = small("cbias", [HD, 2])
        kcAB = place("kcAB", 140, [P, 2, CW], F32R)
        va = place("va", 202.25, [P, 4, TT], F32)
        vc_h = place("vc_h", 144.75, [CW, HD + 1], F32R)
        vc_l = place("vc_l", 145.03125, [CW, HD + 1], F32R)
        w2 = place("w2", 145.375, [HD, 2, HD], F32)
        zc = place("zc", 186.25, [P, 2 * CW], F32)
        chan_rows = place("chan_rows", 187, [CHAN, P], F32)
        pe_rows = place("pe_rows", 187.5, [2 * L16, P], F32)

        bank = ctx.enter_context(nc.psum_tensor("bank", [P, 8, HALF], F32))
        flat = bank[:, :, :].rearrange("p b n -> p (b n)")

        x_loaded = [sem(f"x_loaded{t}") for t in range(TT)]
        const_loaded = sem("const_loaded")
        const2_loaded = sem("const2_loaded")
        w1_loaded = sem("w1_loaded")
        chan_turned = sem("chan_turned")
        chan_done = sem("chan_done")
        consts_made = sem("consts_made")
        sq_done = sem("sq_done")
        xa_done = sem("xa_done")
        xr_done = sem("xr_done")
        xn_done = sem("xn_done")
        xT_done = sem("xT_done")
        norm_loaded = sem("norm_loaded")
        xh_done = sem("xh_done")
        xl_done = sem("xl_done")
        wp_loaded = [sem(f"wp_loaded{c}") for c in range(SPLITS)]
        wph_pool = sem("wph_pool")
        wpl_pool = sem("wpl_pool")
        wph_done = sem("wph_done")
        wpl_done = sem("wpl_done")
        proj_done = sem("proj_done")
        pcopy_done = sem("pcopy_done")
        qa_done = sem("qa_done")
        qr_done = sem("qr_done")
        qn_done = sem("qn_done")
        qkh_done = sem("qkh_done")
        qkl_done = sem("qkl_done")
        qkT_done = sem("qkT_done")
        evq_done = sem("evq_done")
        evk_done = sem("evk_done")
        cbias_mm = sem("cbias_mm")
        cbias_done = sem("cbias_done")
        compress_pe = sem("compress_pe")
        compress_act = sem("compress_act")
        compress_dve = sem("compress_dve")
        glog_done = sem("glog_done")
        gate_done = sem("gate_done")
        rows_done = sem("rows_done")
        max_done = sem("max_done")
        both_done = sem("both_done")
        shift_done = sem("shift_done")
        s_done = sem("s_done")
        exp_done = sem("exp_done")
        pth_done = sem("pth_done")
        ptl_done = sem("ptl_done")
        pv_done = sem("pv_done")
        evac_done = sem("evac_done")
        turned = sem("turned")
        gated = sem("gated")
        summed = sem("summed")
        pool_chain = sem("pool_chain")
        final_done = sem("final_done")
        oh_done = sem("oh_done")
        ol_done = sem("ol_done")
        piece_loaded = [sem("piece_loaded0"), sem("piece_loaded1")]
        ph_done = sem("ph_done")
        pl_done = sem("pl_done")
        mm_done = sem("mm_done")
        freed = sem("freed")
        sig_done = sem("sig_done")
        acc_done = sem("acc_done")
        convc_done = sem("convc_done")
        obh_done = sem("obh_done")
        obl_done = sem("obl_done")
        poolw_loaded = sem("poolw_loaded")
        poolw_h = sem("poolw_h")
        poolw_l = sem("poolw_l")
        iota_done = sem("iota_done")
        poolp_done = sem("poolp_done")
        poold_done = sem("poold_done")
        pooldh_done = sem("pooldh_done")
        pooldl_done = sem("pooldl_done")
        pooly_mm = sem("pooly_mm")
        v_mm = sem("v_mm")
        gelu_done = sem("gelu_done")
        sguc_loaded = sem("sguc_loaded")
        sguw_masked = sem("sguw_masked")
        va_done = sem("va_done")
        vr_done = sem("vr_done")
        vn_done = sem("vn_done")
        swT_done = sem("swT_done")
        swh_done = sem("swh_done")
        swl_done = sem("swl_done")
        vsh_done = sem("vsh_done")
        vsl_done = sem("vsl_done")
        mix_mm = sem("mix_mm")
        mb_done = sem("mb_done")
        mix_done = sem("mix_done")
        u_done = sem("u_done")
        mgh_done = sem("mgh_done")
        mgl_done = sem("mgl_done")
        wo_mm = sem("wo_mm")
        x2_done = sem("x2_done")
        gcopy_done = sem("gcopy_done")
        ffc_done = sem("ffc_done")
        silu_done = sem("silu_done")
        ffh_done = sem("ffh_done")
        ffl_done = sem("ffl_done")
        wd_loaded = [sem("wd_loaded0"), sem("wd_loaded1")]
        wdh_done = sem("wdh_done")
        wdl_done = sem("wdl_done")
        d_mm = sem("d_mm")
        d_done = sem("d_done")
        out_done = sem("out_done")
        passed = sem("passed")
        dve_chain = sem("dve_chain")

        w_in_k = w_in[0].rearrange("(k p) n -> p k n", p=P)

        def wp_piece(t, c):
            if c < 2:
                return t[:, 4 * c:4 * c + 4, 0:QW]
            if c < 6:
                return t[:, 2 * (c - 2):2 * (c - 2) + 2, QW:QW + 6 * HD]
            return t[:, :, QW + 6 * HD:PW]

        def raw_piece(c):
            if c < 2:
                return raw[:, c, 0:4 * QW].rearrange("p (k n) -> p k n", k=4)
            if c < 6:
                return kv_raw[:, c - 2, :].rearrange("p (k n) -> p k n", k=2)
            return graw[:, :, :]


        def wo_low(k):
            return wo_l0[:, k, :] if k < 2 else wo_l2[:, k - 2, :]

        def turned_tile(first_bank, t):
            b = first_bank + 2 * (t % 2)
            return bank[:, b:b + 2, :].rearrange("p b (k n) -> p (b k) n", n=P)

        MIXED = ((), (0, 1, 2, 3), (4, 5, 6, 7), ())

        block = ctx.enter_context(nc.Block())

        @block.sync
        def _(sp):
            sp.dma_start(x_in[:, 0, :], x[0, 0:P, :]).then_inc(x_loaded[0], 16)
            sp.dma_start(norm1_b[:, :], norm1_g[0].partition_broadcast(P)).then_inc(norm_loaded, 16)
            for t in range(1, TT):
                sp.dma_start(x_in[:, t, :], x[0, t * P:(t + 1) * P, :]).then_inc(x_loaded[t], 16)
            for at, src, n in ((C_CA, conv_a_w[0].rearrange("j c -> (j c)"), 3 * BK),
                               (C_CF, conv_ff_w[0].rearrange("j c -> (j c)"), 3 * FT), (C_PS, pool_scale[0], BK)):
                sp.dma_start(chan_rows[at:at + n, :], src.rearrange("(k p) -> k p", p=P)).then_inc(const_loaded, 16)
            for j in range(2):
                sp.dma_start(pe_rows[j * L16:(j + 1) * L16, :].rearrange("l (h d) -> l h d", h=2),
                             cmp_pe[0, j].rearrange("(h l) d -> l h d", h=2)).then_inc(const_loaded, 16)
            sp.dma_start(gains[:, :, :].rearrange("p a d -> p (a d)"),
                         qk_norm_g[0].rearrange("a d -> (a d)").partition_broadcast(P)).then_inc(const2_loaded, 16)
            sp.dma_start(w2[:, :, :], cmp_w2[0].rearrange("j d e -> d j e")).then_inc(const2_loaded, 16)
            for g in range(GROUPS):
                if g:
                    sp.wait_ge(wpl_done, g * (SPLITS - len(POOL_SPLITS)))
                    sp.wait_ge(wpl_pool, g * len(POOL_SPLITS))
                for c in SPLIT_ORDER:
                    if c < 2:
                        sp.dma_start(raw_piece(c), w_in_k[:, 4 * c:4 * c + 4,
                                COL_Q + g * QW:COL_Q + (g + 1) * QW]).then_inc(wp_loaded[c], 16)
                    elif c < 6:
                        if g and c == 2:
                            sp.wait_ge(qkT_done, g * TT)
                        for k in range(2):
                            kt = 2 * (c - 2) + k
                            cols = w_in[0, kt * P:(kt + 1) * P, COL_KV:COL_KV + 6 * KV].rearrange("p (j n) -> p j n", n=KV)
                            sp.dma_start(kv_raw[:, c - 2, k * 6 * HD:(k + 1) * 6 * HD].rearrange("p (j n) -> p j n", j=6),
                                         cols[:, :, g * HD:(g + 1) * HD]).then_inc(wp_loaded[c], 16)
                    else:
                        sp.dma_start(graw[:, :, :], w_in_k[:, :,
                                COL_GATE + g * GW:COL_GATE + (g + 1) * GW]).then_inc(wp_loaded[c], 16)
                if g == 0:
                    sp.wait_ge(xn_done, 4)
                    for j in range(2):
                        for half in range(2):
                            rows = cmp_w1[0, j, half * L16 * HD:(half + 1) * L16 * HD, :]
                            sp.dma_start(w1[half * HD:(half + 1) * HD, j, :, :],
                                          rows.rearrange("(l d) e -> d l e", d=HD)).then_inc(w1_loaded, 16)
            sp.wait_ge(wpl_done, GROUPS * (SPLITS - len(POOL_SPLITS)))

            def load(m, slot, dst, src):
                sp.wait_ge(pl_done, m + 1)
                sp.sem_inc(passed, 1)
                sp.dma_start(dst, src).then_inc(piece_loaded[slot], 16)

            def ring_piece(slot, k=KT):
                return raw[:, slot, 0:k * P].rearrange("p (k n) -> p k n", k=k)

            def load_merge(b, turn, m0):
                g0 = [sp_value((turn * 2 + a) * P + (COL_MERGE + b * DM)) for a in range(2)]
                y0 = [sp_value((turn * 2 + a) * P) for a in range(2)]
                wb = w_branch[0, b].rearrange("(k p) n -> p k n", p=P)
                for a in range(2):
                    load(turn * 4 + (m0 + 2 * a), 0, ring_piece(0), w_in_k[:, :, bass.ds(g0[a], P)])
                    load(turn * 4 + (m0 + 2 * a + 1), 1, ring_piece(1, BK), wb[:, :, bass.ds(y0[a], P)])

            def sp_value(v):
                return v if isinstance(v, int) else sp.snap(v)

            with sp.Fori(0, KT // 2) as t:
                load_merge(1, t, PIECE["merge1"])
            for c in range(3 * BK):
                col = (BW, 2 * BW, 0)[c % 3] + (c // 3) * P
                load(PIECE["conv"] + c, c % 2, ring_piece(c % 2), w_in_k[:, :, col:col + P])
            with sp.Fori(0, KT // 2) as t:
                load_merge(0, t, PIECE["merge0"])
            for c in range(4):
                load(PIECE["v"] + c, c % 2, raw[:, c % 2, :].rearrange("p (k n) -> p k n", k=2),
                     w_in_k[:, 2 * c:2 * c + 2, COL_SGU + BW:COL_SGU + 2 * BW])
            for c in range(BK):
                if c == 1:
                    sp.wait_ge(v_mm, TT)
                    sp.dma_start(pool_w32[:, :, :], pool_w[0].rearrange("g c d -> c g d")).then_inc(poolw_loaded, 16)
                load(PIECE["pool"] + c, c % 2, ring_piece(c % 2), w_in_k[:, :, COL_POOL + c * P:COL_POOL + (c + 1) * P])
            with sp.Fori(0, KT // 2) as t:
                load_merge(2, t, PIECE["merge2"])
            for c in range(BK):
                load(PIECE["u"] + c, c % 2, ring_piece(c % 2), w_in_k[:, :, COL_SGU + c * P:COL_SGU + (c + 1) * P])
            with sp.Fori(0, KT // 2) as t:
                load_merge(3, t, PIECE["merge3"])
            for c in range(KT):
                load(PIECE["wo"] + c, c % 2, raw[:, c % 2, :], w_o[0, c * P:(c + 1) * P, :])
            sp.wait_ge(mgl_done, 1)
            sp.dma_start(norm2_b[:, :], norm2_g[0].partition_broadcast(P)).then_inc(norm_loaded, 16)
            for t in range(TT):
                sp.wait_ge(mgl_done, t + 1)
                sp.dma_start(x2[:, t, :], x[0, t * P:(t + 1) * P, :]).then_inc(x_loaded[t], 16)
            with sp.Fori(0, FT // 2) as t:
                cols = [sp.snap((t * 2 + a) * P + up * D_FF) for a in range(2) for up in range(2)]
                rows = [sp.snap(t * (2 * P * DM) + a * P * DM) for a in range(2)]
                for c in range(4):
                    load(t * 4 + (PIECE["ff"] + c), c % 2, ring_piece(c % 2),
                         w_up[0].rearrange("(k p) n -> p k n", p=P)[:, :, bass.ds(cols[c], P)])
                for a in range(2):
                    sp.wait_ge(wdl_done, t * 2 + (a + 1))
                    sp.dma_start(wd_raw[:, a, :], w_down[0].rearrange("r n -> (r n)")[bass.ds(rows[a],
                            P * DM)].rearrange("(p n) -> p n", p=P)).then_inc(wd_loaded[a], 16)
            for t in range(TT):
                sp.wait_ge(d_done, 2 + (FT // 2 - 1) * TT + t + 1)
                sp.dma_start(out[0, t * P:(t + 1) * P, :], x2[:, t, :]).then_inc(out_done, 16)
            sp.wait_ge(out_done, 16 * TT)

        @block.gpsimd
        def _(pool):
            nc.gpsimd.memset(ident[:, :], 0.0).then_inc(consts_made, 1)
            nc.gpsimd.memset(tri[:, :], 0.0).then_inc(consts_made, 1)
            nc.gpsimd.memset(wstart[:, :], 0.0).then_inc(consts_made, 1)
            nc.gpsimd.memset(cmask[:, :, :], 0.0).then_inc(consts_made, 1)
            nc.gpsimd.memset(any31[:, :], 1.0).then_inc(consts_made, 1)
            nc.gpsimd.memset(zc[:, :], 0.0).then_inc(consts_made, 1)
            pool.wait_ge(consts_made, 6)
            nc.gpsimd.affine_select(out=ident[:, :], in_=ident[:, :], compare_op=ALU.not_equal, fill=1.0,
                                    base=0, pattern=[[-1, P]], channel_multiplier=1).then_inc(consts_made, 1)
            nc.gpsimd.affine_select(out=tri[:, :], in_=tri[:, :], compare_op=ALU.is_ge, fill=NEG,
                                    base=0, pattern=[[-1, P]], channel_multiplier=1).then_inc(consts_made, 1)
            nc.gpsimd.affine_select(out=wstart[:, :], in_=wstart[:, :], compare_op=ALU.is_gt, fill=NEG,
                                    base=0, pattern=[[1, P]], channel_multiplier=-1).then_inc(consts_made, 1)
            nc.gpsimd.affine_select(out=cmask[:, :, :], in_=cmask[:, :, :], compare_op=ALU.is_ge, fill=NEG,
                                    base=1 - CMP_BLOCK, pattern=[[P, TT], [-CMP_STRIDE, CW]],
                                    channel_multiplier=1).then_inc(consts_made, 1)
            nc.gpsimd.affine_select(out=any31[:, :], in_=any31[:, :], compare_op=ALU.is_ge, fill=0.0,
                                    base=1 - CMP_BLOCK, pattern=[[0, 1]], channel_multiplier=1).then_inc(consts_made, 1)
            pool.wait_ge(consts_made, 11)
            nc.gpsimd.tensor_copy(identb[:, :], ident[:, :]).then_inc(consts_made, 1)

            with pool.Fori(0, GROUPS) as g:
                for m, c in enumerate(POOL_SPLITS):
                    pool.wait_ge(wp_loaded[c], g * (16 * SPLIT_DMAS[c]) + 16 * SPLIT_DMAS[c])
                    pool.sem_inc(passed, 1)
                    nc.gpsimd.tensor_copy(wp_piece(wp_h, c), raw_piece(c)).then_inc(wph_pool, 1)
                for m, c in enumerate(POOL_SPLITS):
                    pool.wait_ge(wph_pool, g * len(POOL_SPLITS) + m + 1)
                    nc.gpsimd.tensor_tensor(wp_piece(wp_l, c), raw_piece(c), wp_piece(wp_h, c).bitcast(F32),
                                            ALU.subtract).then_inc(wpl_pool, 1)
                for slot in slots:
                    for at, n, r0, heads, c, w in slot["pieces"]:
                        if at + 1 == piece_end[n]:
                            pool.wait_ge(max_done, g * PIECES + piece_end[n])
                            if tasks[n][3] > HALF:
                                pool.wait_ge(both_done, g * BOTH + both_at[n] + 1)
                            if n >= MAXIMA:
                                pool.wait_ge(s_done, g * UNITS + last_unit[n - MAXIMA] + 1)
                            nc.gpsimd.tensor_tensor(shift[:, n % MAXIMA, :, :],
                                    ident[:, :].unsqueeze(1).broadcast_to([P, REP, P]),
                                                    nmx[:, n % MAXIMA, 0, :].unsqueeze(2).broadcast_to([P, REP, P]),
                                                    ALU.mult).then_inc(shift_done, 1)
                    if slot["sum"] is not None:
                        i = slot["sum"]
                        pool.wait_ge(gated, g * NT + 3 * i + 3)
                        o = [o_gated[:, (3 * i + b) % 4, :] for b in range(3)]
                        nc.gpsimd.tensor_tensor(o[0], o[0], o[1], ALU.add).then_inc(pool_chain, 1)
                        pool.wait_ge(pool_chain, g * TT + i + 1)
                        nc.gpsimd.tensor_tensor(o[0], o[0], o[2], ALU.add).then_inc(summed, 1)
                pool.wait_ge(ol_done, g * TT + TT)

            pool.wait_ge(v_mm, TT)
            nc.gpsimd.iota(pool_t16[:, :], pattern=[[1, 16]], base=1, channel_multiplier=0,
                           allow_small_or_imprecise_dtypes=True).then_inc(iota_done, 1)
            pool.wait_ge(obl_done, 2 * BK)
            pool.dma_start(sgu_g[:, :], sgu_norm_g[0].partition_broadcast(P)).then_inc(sguc_loaded, 16)
            pool.dma_start(sgu_bias[:, :, :].rearrange("p g t -> p (g t)"),
                           sgu_b[0].rearrange("g t -> (g t)").partition_broadcast(P)).then_inc(sguc_loaded, 16)
            pool.dma_start(sgu_w32[:, :, :], sgu_w[0].rearrange("g t s -> t g s")).then_inc(sguc_loaded, 16)
            pool.wait_ge(sguc_loaded, 48)
            nc.gpsimd.affine_select(out=sgu_w32[:, :, :], in_=sgu_w32[:, :, :], compare_op=ALU.is_ge, fill=0.0,
                                    base=0, pattern=[[0, BK], [-1, P]], channel_multiplier=1).then_inc(sguw_masked, 1)

        @block.scalar
        def _(act):
            def input_squares(t):
                act.wait_ge(x_loaded[t], 16)
                if t:
                    act.wait_ge(sq_done, t)
                nc.scalar.activation(squares[:, :], x_in[:, t, :], ACT.Square,
                        accum_out=ssq[:, t:t + 1]).then_inc(sq_done, 1)

            input_squares(0)
            for t in range(TT + 1):
                if 1 <= t < TT - 1:
                    input_squares(t + 1)
                if t < TT:
                    act.wait_ge(xa_done, t + 1)
                    nc.scalar.activation(xa[:, t % 2, 1:2], xa[:, t % 2, 0:1], ACT.Sqrt).then_inc(xr_done, 1)
                if t == 0:
                    input_squares(1)
                if t >= 1:
                    act.wait_ge(xT_done, t)
                    nc.scalar.activation(actT_h[:, :, (t - 1) * P:t * P], turned_tile(0, t - 1),
                            ACT.Copy).then_inc(xh_done, 1)

            with act.Fori(0, GROUPS) as g:
                for c in SPLIT_ORDER:
                    if c not in POOL_SPLITS:
                        act.wait_ge(wp_loaded[c], g * (16 * SPLIT_DMAS[c]) + 16 * SPLIT_DMAS[c])
                        nc.scalar.activation(wp_piece(wp_h, c), raw_piece(c), ACT.Copy).then_inc(wph_done, 1)

                def evacuate_transposes(t):
                    act.wait_ge(qkT_done, g * TT + t + 1)
                    nc.scalar.activation(qT[:, :, t * P:(t + 1) * P],
                                         bank[:, 4, :].rearrange("p (r n) -> p r n", r=REP), ACT.Copy)
                    kc = bank[:, 6, 0:2 * P].rearrange("p (j n) -> p j n", j=2)
                    nc.scalar.activation(kcT[0:HD, :, t * P:(t + 1) * P], kc[0:HD, :, :], ACT.Copy)
                    lo = CMP_STRIDE if t == 0 else 0
                    nc.scalar.activation(kcT[HD:P, :, t * P + lo - CMP_STRIDE:(t + 1) * P - CMP_STRIDE],
                                         kc[HD:P, :, lo:P], ACT.Copy).then_inc(evq_done, 1)

                for t in range(TT + 1):
                    if t < TT:
                        act.wait_ge(proj_done, g * TT + t + 1)
                        after(act, qkl_done, g * TT, t - 1)
                        nc.scalar.activation(proj[:, t % 2, 0:QW], bank[:, 2 * (t % 2), 0:QW], ACT.Copy)
                        nc.scalar.activation(proj[:, t % 2, QW:PW], bank[:, 2 * (t % 2) + 1, 0:PW - QW],
                                             ACT.Copy).then_inc(pcopy_done, 1)
                    if t >= 1:
                        evacuate_transposes(t - 1)
                    if t < TT:
                        act.wait_ge(qa_done, g * TT + t + 1)
                        nc.scalar.activation(qr[:, :], qa[:, :], ACT.Sqrt).then_inc(qr_done, 1)
                        after(act, qkT_done, g * TT, t - 1)
                        act.wait_ge(qn_done, g * TT + t + 1)
                        d = dup[:, t % 2, :, :]
                        nc.scalar.activation(d[:, 0:REP, 0:HD].bitcast(F32R), qkn[:, 0:REP, :], ACT.Copy)
                        kd = d[:, 4:8, :].rearrange("p (t a) (u d) -> p t a u d", a=2, u=2)
                        for ty in range(2):
                            nc.scalar.activation(kd[:, ty, 0, :, :].bitcast(F32R),
                                                 qkn[:, 4 + ty, :].unsqueeze(1).broadcast_to([P, 2, HD]), ACT.Copy)
                        pv = proj[:, t % 2, QW:QW + 6 * HD].rearrange("p (t d) -> p t d", d=HD)
                        cd = d[:, 8:10, :].rearrange("p t (u d) -> p t u d", u=2)
                        nc.scalar.activation(cd, pv[:, 0:2, :].unsqueeze(2).broadcast_to([P, 2, 2, HD]), ACT.Copy)
                        nc.scalar.activation(v_h[:, :, t, 0:HD], pv[:, 3:6:2, :], ACT.Copy).then_inc(qkh_done, 1)

                def compressed(step):
                    act.wait_ge(compress_pe, g * 3 + step + 1)
                    if step == 0:
                        act.wait_ge(cbias_done, g + 1)
                        for j in range(2):
                            ins = nc.scalar.activation(h1[:, j, 0:NCMP], bank[0:HD, 7, j * HD:j * HD + NCMP], ACT.Silu,
                                                       bias=cbias[:, j:j + 1])
                    elif step == 1:
                        act.wait_ge(compress_dve, g * 3 + 2)
                        ins = nc.scalar.activation(qr[0:NCMP, 0:1], qa[0:NCMP, 0:1], ACT.Sqrt)
                    else:
                        ins = nc.scalar.activation(kcAB[:, :, 0:NCMP], bank[:, 7, 384:384 + 2 * CW].rearrange(
                            "p (a n) -> p a n", a=2)[:, :, 0:NCMP], ACT.Copy)
                    ins.then_inc(compress_act, 1)

                act.wait_ge(glog_done, g * TT + TT)
                nc.scalar.activation(glog[:, :, :], glog[:, :, :], ACT.Sigmoid).then_inc(gate_done, 1)

                for slot in slots:
                    if slot["n"] in COMPRESS:
                        compressed(COMPRESS.index(slot["n"]))
                    if slot["unit"]:
                        u, n, j = slot["unit"]
                        nr = CW if tasks[n][1] == "cmp" else P
                        act.wait_ge(s_done, g * UNITS + u + 1)
                        after(act, ptl_done, g * UNITS, u - RING + 1)
                        nc.scalar.activation(pT[0:nr, u % RING, :], bank[0:nr, 3 + u % 2, :], ACT.Exp).then_inc(exp_done, 1)
                        act.wait_ge(exp_done, g * UNITS + u + 1)
                        after(act, pv_done, g * UNITS, u - RING + 1)
                        nc.scalar.activation(pT_h[0:nr, u % RING, :], pT[0:nr, u % RING, :], ACT.Copy).then_inc(pth_done, 1)
                    if slot["evacuate"] is not None:
                        n = slot["evacuate"]
                        act.wait_ge(pv_done, g * UNITS + last_unit[n] + 1)
                        after(act, turned, g * NT, n - 1)
                        nc.scalar.activation(oT[:, n % 2, :], bank[0:HD + 1, 5 + n % 2, :], ACT.Copy).then_inc(evac_done, 1)
                    if slot["final"] is not None:
                        i = slot["final"]
                        act.wait_ge(final_done, g * TT + i + 1)
                        q0 = TILE_ORDER[i] * P
                        nc.scalar.activation(outb_h[:, bass.ds(g * 2, 2), q0:q0 + P],
                                             bank[:, 2, 0:2 * P].rearrange("p (b n) -> p b n",
                                                     b=2), ACT.Copy).then_inc(oh_done, 1)
                act.wait_ge(pv_done, g * UNITS + UNITS)

            def high(m, slot, dst, src):
                act.wait_ge(piece_loaded[slot], (m // 2) * 16 + 16 if isinstance(m, int) else m)
                nc.scalar.activation(dst, src, ACT.Copy).then_inc(ph_done, 1)

            def high_ring(turn, per, m, c, slot):
                act.wait_ge(piece_loaded[slot], turn * (per // 2 * 16) + (m // 2 * 16 + 16))
                act.wait_ge(mm_done, turn * per + (c + 1))
                nc.scalar.activation(ring_h[:, slot, :], raw[:, slot, :], ACT.Copy).then_inc(ph_done, 1)

            def merge(b, turn, m0, c0, t0, last=False, beside=None, beside_at=0):
                sig = sig_0 if b == 0 else sig_all
                for a in range(2):
                    for p in (2 * a, 2 * a + 1):
                        if not (last and p == 3):
                            nxt = m0 + p + 1 + (4 if b == 0 and beside and p == 3 else 0)
                            high_ring(turn, 4, nxt, c0 + p + 1, (p + 1) % 2)
                        if p == 2 * a:
                            if beside and a == beside_at:
                                beside()
                            act.wait_ge(mm_done, turn * 4 + (2 + c0 + p + 1))
                            act.wait_ge(acc_done, turn * 2 + (t0 + a + 1))
                            nc.scalar.activation(sig[:, a, :], flat[:, p * 1024:(p + 1) * 1024],
                                    ACT.Sigmoid).then_inc(sig_done, 1)

            high_ring(0, 4, 0, 0, 0)
            with act.Fori(0, KT // 2) as t:
                merge(1, t, PIECE["merge1"], CHUNK["merge1"], 0)

            for c in range(3 * BK):
                m, ck_ = PIECE["conv"] + c, CHUNK["conv"] + c
                high_ring(0, 4, m + 1, ck_ + 1, (c + 1) % 2)
                q = c // 3
                if c % 3 == 0:
                    act.wait_ge(mm_done, 2 + ck_ + 1)
                    if q >= 2:
                        act.wait_ge(freed, 4 + ck_ - 6 + 2)
                    nc.scalar.activation(conv_c[:, q % 2, :], flat[:, (ck_ % 4) * 1024:(ck_ % 4 + 1) * 1024],
                            ACT.Copy).then_inc(convc_done, 1)
                if c % 3 == 2:
                    act.wait_ge(freed, 4 + ck_ + 1)
                    nc.scalar.activation(outb_h[:, q, :], conv_o[:, q % 2, :], ACT.Copy).then_inc(obh_done, 1)
            def value_weights():
                for c in range(4):
                    high(PIECE["v"] + c, c % 2, wv_h[:, 2 * c:2 * c + 2, :],
                            raw[:, c % 2, :].rearrange("p (k n) -> p k n", k=2))

            with act.Fori(0, KT // 2 - 1) as t:
                merge(0, t, PIECE["merge0"], CHUNK["merge0"], KT)
            merge(0, KT // 2 - 1, PIECE["merge0"], CHUNK["merge0"], KT, beside=value_weights, beside_at=1)

            act.wait_ge(acc_done, 2 + 2 * KT)
            for t in range(TT):
                act.wait_ge(v_mm, t + 1)
                nc.scalar.activation(sgu_v[:, t, :], bank[:, t, :], ACT.Gelu).then_inc(gelu_done, 1)
            act.wait_ge(va_done, 1)
            nc.scalar.activation(va[:, 1, :], va[:, 0, :], ACT.Sqrt).then_inc(vr_done, 1)

            act.wait_ge(poolw_loaded, 16)
            nc.scalar.activation(pool_wh[:, :, :], pool_w32[:, :, :], ACT.Copy).then_inc(poolw_h, 1)

            def pool_out(q):
                act.wait_ge(pooly_mm, q + 1)
                nc.scalar.activation(outb_h[:, q, :], flat[:, (2 + q % 2) * 1024:(3 + q % 2) * 1024], ACT.Copy,
                                     scale=chan[:, C_PS + q:C_PS + q + 1]).then_inc(obh_done, 1)

            for q in range(BK):
                m, ck_ = PIECE["pool"] + q, CHUNK["pool"] + q
                high_ring(0, 4, m + 1, ck_ + 1, (q + 1) % 2)
                act.wait_ge(mm_done, 2 + ck_ + 1)
                if q >= 2:
                    act.wait_ge(poold_done, q - 1)
                nc.scalar.activation(pool_p[:, q % 2, 16:], flat[:, (q % 2) * 1024:(q % 2 + 1) * 1024],
                        ACT.Copy).then_inc(poolp_done, 1)
                if q >= 1:
                    pool_out(q - 1)
                act.wait_ge(poold_done, q + 1)
                if q >= 1:
                    act.wait_ge(pooly_mm, q)
                nc.scalar.activation(pool_dh[:, :], pool_d[:, :], ACT.Copy).then_inc(pooldh_done, 1)
            merge(2, 0, PIECE["merge2"], CHUNK["merge2"], 2 * KT, beside=lambda: pool_out(BK - 1))
            with act.Fori(1, KT // 2) as t:
                merge(2, t, PIECE["merge2"], CHUNK["merge2"], 2 * KT)
            def gate_out(q):
                act.wait_ge(mix_done, q + 1)
                nc.scalar.activation(outb_h[:, q, :], sgu_u[:, q, :], ACT.Copy).then_inc(obh_done, 1)

            for q in range(BK):
                m, ck_ = PIECE["u"] + q, CHUNK["u"] + q
                high_ring(0, 4, m + 1, ck_ + 1, (q + 1) % 2)
                if q == 1:
                    act.wait_ge(swT_done, 1)
                    nc.scalar.activation(sgu_wh[:, :, :], bank[:, 4, :].rearrange("p (g t) -> p g t", g=BK),
                            ACT.Copy).then_inc(swh_done, 1)
                for t in MIXED[q]:
                    act.wait_ge(vn_done, t + 1)
                    if t >= 4:
                        act.wait_ge(mix_mm, t - 3)
                    nc.scalar.activation(sgu_vh[:, t % 4, :], sgu_v[:, t, :], ACT.Copy).then_inc(vsh_done, 1)
                if q == BK - 1:
                    for k in range(BK - 1):
                        gate_out(k)
                act.wait_ge(mm_done, 2 + ck_ + 1)
                nc.scalar.activation(sgu_u[:, q, :], flat[:, (q % 2) * 1024:(q % 2 + 1) * 1024],
                        ACT.Gelu).then_inc(u_done, 1)
            gate_out(BK - 1)
            with act.Fori(0, KT // 2 - 1) as t:
                merge(3, t, PIECE["merge3"], CHUNK["merge3"], 3 * KT)
            merge(3, KT // 2 - 1, PIECE["merge3"], CHUNK["merge3"], 3 * KT, last=True)

            act.wait_ge(mm_done, 2 + CHUNK["ff"] - 1)
            for k in range(KT):
                act.wait_ge(acc_done, 2 + 3 * KT + k + 1)
                nc.scalar.activation(actT_h[:, k, :], merged[:, k, :], ACT.Copy).then_inc(mgh_done, 1)
                high(PIECE["wo"] + k, k % 2, wo_h[:, k, :], raw[:, k % 2, :])

            high_ring(0, 4, PIECE["ff"], CHUNK["ff"], 0)

            def sum_of_squares(t):
                act.wait_ge(x2_done, t + 1)
                if t:
                    act.wait_ge(sq_done, TT + t)
                nc.scalar.activation(squares2[:, :], x2[:, t, :], ACT.Square, accum_out=ssq[:, t:t + 1]).then_inc(sq_done, 1)

            def root(t0, t1, count):
                act.wait_ge(xa_done, TT + count)
                nc.scalar.activation(x2a[:, 1, t0:t1], x2a[:, 0, t0:t1], ACT.Sqrt).then_inc(xr_done, 1)

            for t in range(4):
                sum_of_squares(t)
            root(0, 4, 1)
            for t in range(TT):
                if t < 4:
                    sum_of_squares(4 + t)
                act.wait_ge(xT_done, TT + t + 1)
                nc.scalar.activation(actT_h[:, :, t * P:(t + 1) * P], turned_tile(4, t), ACT.Copy).then_inc(xh_done, 1)
                if t < 4:
                    root(4 + t, 5 + t, 2 + t)

            def ff(turn, last=False):
                m0, c0 = PIECE["ff"], CHUNK["ff"]
                for a in range(2):
                    high_ring(turn, 4, m0 + 2 * a + 1, c0 + 2 * a + 1, 1)
                    act.wait_ge(mm_done, turn * 4 + (2 + c0 + 2 * a + 1))
                    nc.scalar.activation(ffg[:, a, 2:], flat[:, 0:1024], ACT.Copy).then_inc(gcopy_done, 1)
                    if a == 1:
                        for k in range(2):
                            act.wait_ge(wd_loaded[k], turn * 16 + 16)
                            if not (isinstance(turn, int) and turn == 0):
                                act.wait_ge(d_mm, turn * TT)
                            nc.scalar.activation(wd_h[:, k, :], wd_raw[:, k, :], ACT.Copy).then_inc(wdh_done, 1)
                    if not (last and a == 1):
                        high_ring(turn, 4, m0 + 2 * a + 2, c0 + 2 * a + 2, 0)
                    act.wait_ge(ffc_done, turn * 2 + (a + 1))
                    nc.scalar.activation(ffc[:, a, :], ffc[:, a, :], ACT.Silu).then_inc(silu_done, 1)
                    act.wait_ge(freed, turn * 4 + (4 + c0 + 2 * a + 2))
                    nc.scalar.activation(ffa_h[:, a, :], ffc[:, a, :], ACT.Copy).then_inc(ffh_done, 1)

            ff(0)
            with act.Fori(1, FT // 2 - 1) as t:
                ff(t)
            ff(FT // 2 - 1, last=True)

        @block.vector
        def _(dve):
            ch = Chain(dve, dve_chain)

            def inverse_root(a, root, y, t, n, root_done, count):
                dve.wait_ge(root_done, count)
                ch.link(nc.vector.reciprocal(y, root))
                ch.link(nc.vector.tensor_tensor(t, y, y, ALU.mult))
                ch.link(nc.vector.tensor_tensor(t, t, a, ALU.mult))
                ch.link(nc.vector.tensor_scalar(t, t, -0.5, 1.5, ALU.mult, ALU.add))
                ch.link(nc.vector.tensor_tensor(y, y, t, ALU.mult))

            dve.sem_inc(freed, 4)
            dve.sem_inc(pl_done, 2)
            dve.sem_inc(wdl_done, 2)
            dve.sem_inc(acc_done, 2)
            dve.sem_inc(d_done, 2)
            dve.wait_ge(consts_made, 6)
            ch.link(nc.vector.tensor_copy(vc_h[:, 0:HD], zc[0:CW, 0:HD]))
            ch.link(nc.vector.tensor_copy(vc_l[:, :], zc[0:CW, 0:HD + 1]))
            ch.link(nc.vector.tensor_scalar(vc_h[:, HD:HD + 1], zc[0:CW, 0:1], 1.0, None, ALU.add))
            for a, one in ((v_h, 1.0), (v_l, 0.0)):
                ch.link(nc.vector.tensor_scalar(a[:, :, :, HD:HD + 1],
                                                zc[:, 0:2 * TT].rearrange("p (a t) -> p a t", a=2).unsqueeze(3),
                                                one, None, ALU.add))
            dve.wait_ge(norm_loaded, 16)
            for t in range(TT + 2):
                if t == TT - 1:
                    dve.wait_ge(chan_turned, 1)
                    ch.link(nc.vector.tensor_copy(chan[:, :], bank[:, 6, 0:CHAN]))
                    nc.vector.tensor_copy(peT[:, :, :], bank[:, 6, CHAN:CHAN + 2 * L16].rearrange("p (j l) -> p j l",
                            j=2)).then_inc(chan_done, 1)
                    dve.wait_ge(const2_loaded, 32)
                    ch.link(nc.vector.tensor_scalar(gains[:, 0, :], gains[:, 0, :], HD ** -0.5, None, ALU.mult))
                xs = xa[:, t % 2, :]
                if t < TT:
                    dve.wait_ge(sq_done, t + 1)
                    nc.vector.tensor_scalar(xs[:, 0:1], ssq[:, t:t + 1], 1.0 / DM, EPS, ALU.mult,
                            ALU.add).then_inc(xa_done, 1)
                if 1 <= t <= TT:
                    if t >= 3:
                        dve.wait_ge(xT_done, t - 2)
                    nc.vector.scalar_tensor_tensor(xn[:, (t - 1) % 2, :], x_in[:, t - 1, :], xa[:, (t - 1) % 2, 2:3],
                                                   norm1_b[:, :], ALU.mult, ALU.mult).then_inc(xn_done, 1)
                if t >= 2:
                    dve.wait_ge(xh_done, t - 1)
                    cols = slice((t - 2) * P, (t - 1) * P)
                    nc.vector.tensor_tensor(actT_l[:, :, cols], turned_tile(0, t - 2), actT_h[:, :, cols].bitcast(F32),
                                            ALU.subtract).then_inc(xl_done, 1)
                if t < TT:
                    inverse_root(xs[:, 0:1], xs[:, 1:2], xs[:, 2:3], xs[:, 3:4], 1, xr_done, t + 1)

            with dve.Fori(0, GROUPS) as g:
                ch.enter(g, CHAIN_TURN)
                for m, c in enumerate([c for c in SPLIT_ORDER if c not in POOL_SPLITS]):
                    dve.wait_ge(wph_done, g * (SPLITS - len(POOL_SPLITS)) + m + 1)
                    nc.vector.tensor_tensor(wp_piece(wp_l, c), raw_piece(c), wp_piece(wp_h, c).bitcast(F32),
                                            ALU.subtract).then_inc(wpl_done, 1)
                for t in range(TT + 1):
                    if t < TT:
                        dve.wait_ge(pcopy_done, g * TT + t + 1)
                        pr = proj[:, t % 2, :]
                        q = pr[:, 0:QW].rearrange("p (r d) -> p r d", d=HD)
                        kv = pr[:, QW:QW + 6 * HD].rearrange("p (t d) -> p t d", d=HD)
                        k = kv[:, 2:6:2, :]
                        nc.vector.tensor_copy(glog[:, t, :], pr[:, QW + 6 * HD:PW]).then_inc(glog_done, 1)
                        after(dve, qkh_done, g * TT, t)
                        after(dve, qkl_done, g * TT, t)
                        nc.vector.tensor_tensor(qkn[:, 0:4, :], q, q, ALU.mult)
                        ch.link(nc.vector.tensor_tensor(qkn[:, 4:6, :], k, k, ALU.mult))
                        ch.link(nc.vector.tensor_reduce(qt[:, :], qkn[:, :, :], AX, ALU.add))
                        nc.vector.tensor_scalar(qa[:, :], qt[:, :], 1.0 / HD, EPS, ALU.mult, ALU.add).then_inc(qa_done, 1)
                    if t >= 1:
                        dve.wait_ge(qkT_done, g * TT + t)
                        nc.vector.tensor_copy(kAB[:, :, (t - 1) * P:t * P],
                                              bank[:, 5, :].rearrange("p (a n) -> p a n", a=4)).then_inc(evk_done, 1)
                    if t < TT:
                        inverse_root(qa[:, :], qr[:, :], qy[:, :], qt[:, :], 6, qr_done, g * TT + t + 1)
                        nc.vector.tensor_tensor(qkn[:, 0:4, :], q, qy[:, 0:4].unsqueeze(2).broadcast_to([P, 4, HD]),
                                ALU.mult)
                        ch.link(nc.vector.tensor_tensor(qkn[:, 4:6, :], k,
                                qy[:, 4:6].unsqueeze(2).broadcast_to([P, 2, HD]), ALU.mult))
                        nc.vector.tensor_tensor(qkn[:, 0:4, :], qkn[:, 0:4, :],
                                gains[:, 0:1, :].broadcast_to([P, 4, HD]), ALU.mult)
                        nc.vector.tensor_tensor(qkn[:, 4:6, :], qkn[:, 4:6, :], gains[:, 2:4, :],
                                ALU.mult).then_inc(qn_done, 1)
                        dve.wait_ge(qkh_done, g * TT + t + 1)
                        d = dup[:, t % 2, :, :]
                        nc.vector.tensor_tensor(d[:, 0:REP, HD:P], qkn[:, 0:4, :], d[:, 0:REP, 0:HD], ALU.subtract)
                        kd = d[:, 4:8, :].rearrange("p (t a) (u d) -> p t a u d", a=2, u=2)
                        for ty in range(2):
                            nc.vector.tensor_tensor(kd[:, ty, 1, :, :],
                                    qkn[:, 4 + ty, :].unsqueeze(1).broadcast_to([P, 2, HD]),
                                                    kd[:, ty, 0, :, :], ALU.subtract)
                        nc.vector.tensor_tensor(v_l[:, :, t, 0:HD], kv[:, 3:6:2, :], v_h[:, :, t, 0:HD].bitcast(F32),
                                                ALU.subtract).then_inc(qkl_done, 1)

                dve.wait_ge(cbias_mm, g + 1)
                nc.vector.tensor_copy(cbias[:, :], bank[0:HD, 7, 0:128:64]).then_inc(cbias_done, 1)
                dve.wait_ge(qkT_done, g * TT + TT)
                nc.vector.tensor_scalar(ones[:, :], ident[:, :], 0.0, 1.0, ALU.mult, ALU.add)
                nc.vector.tensor_scalar(kcAB[:, :, NCMP:CW], ident[:, 0:2].unsqueeze(2), 0.0, None,
                        ALU.mult).then_inc(compress_dve, 1)

                def compressed(step):
                    if step == 1:
                        dve.wait_ge(compress_pe, g * 3 + 2)
                        ch.link(nc.vector.tensor_copy(ck[0:NCMP, :], bank[0:NCMP, 7, 256:256 + HD]))
                        nc.vector.tensor_copy(vc_h[0:NCMP, 0:HD], bank[0:NCMP, 7, 320:320 + HD])
                        ch.link(nc.vector.tensor_tensor(ck2[0:NCMP, :], ck[0:NCMP, :], ck[0:NCMP, :], ALU.mult))
                        nc.vector.tensor_tensor(vc_l[0:NCMP, 0:HD], bank[0:NCMP, 7, 320:320 + HD],
                                                vc_h[0:NCMP, 0:HD].bitcast(F32), ALU.subtract)
                        ch.link(nc.vector.tensor_reduce(qt[0:NCMP, 0:1], ck2[0:NCMP, :], AX, ALU.add))
                        nc.vector.tensor_scalar(qa[0:NCMP, 0:1], qt[0:NCMP, 0:1], 1.0 / HD, EPS, ALU.mult,
                                ALU.add).then_inc(compress_dve, 1)
                    else:
                        inverse_root(qa[0:NCMP, 0:1], qr[0:NCMP, 0:1], qy[0:NCMP, 0:1], qt[0:NCMP, 0:1], 1, compress_act,
                                g * 3 + 2)
                        ch.link(nc.vector.tensor_scalar(ck[0:NCMP, :], ck[0:NCMP, :], qy[0:NCMP, 0:1], None, ALU.mult))
                        ch.link(nc.vector.tensor_tensor(ck[0:NCMP, :], ck[0:NCMP, :], gains[0:NCMP, 1, :], ALU.mult))
                        twice = ck[0:NCMP, :].unsqueeze(1).broadcast_to([NCMP, 2, HD])
                        ch.link(nc.vector.tensor_copy(ckd[0:NCMP, 0, :, :].bitcast(F32R), twice))
                        nc.vector.tensor_tensor(ckd[0:NCMP, 1, :, :], twice, ckd[0:NCMP, 0, :, :],
                                ALU.subtract).then_inc(compress_dve, 1)

                dve.wait_ge(gate_done, g + 1)

                def low_part(u, n, j):
                    dve.wait_ge(pth_done, g * UNITS + u + 1)
                    nr = CW if tasks[n][1] == "cmp" else P
                    nc.vector.tensor_tensor(pT_l[0:nr, u % RING, :], pT[0:nr, u % RING, :],
                                            pT_h[0:nr, u % RING, :].bitcast(F32), ALU.subtract).then_inc(ptl_done, 1)

                last = None
                for slot in slots:
                    for at, n, r0, heads, c, w in slot["pieces"]:
                        dve.wait_ge(rows_done, g * PIECES + at + 1)
                        after(dve, shift_done, g * NT, n - MAXIMA + 1)
                        nc.vector.tensor_reduce(nmx[:, n % MAXIMA, c // HALF, r0:r0 + heads],
                                                bank[:, at % 2, 0:heads * w].rearrange("p (r n) -> p r n", r=heads),
                                                AX, ALU.max, negate=True).then_inc(max_done, 1)
                        if at + 1 == piece_end[n] and n in wide:
                            dve.wait_ge(max_done, g * PIECES + at + 1)
                            nc.vector.tensor_tensor(nmx[:, n % MAXIMA, 0, :], nmx[:, n % MAXIMA, 0, :],
                                    nmx[:, n % MAXIMA, 1, :],
                                                    ALU.min).then_inc(both_done, 1)
                    if last:
                        low_part(*last)
                    last = slot["unit"]
                    if slot["n"] in (COMPRESS[1], COMPRESS[1] + 2):
                        compressed(1 + (slot["n"] > COMPRESS[1]))
                    if slot["turn"] is not None:
                        n = slot["turn"]
                        i, kind = tasks[n][0:2]
                        dve.wait_ge(turned, g * NT + n + 1)
                        o = bank[:, 7, 0:REP * (HD + 1)].rearrange("p (r d) -> p r d", r=REP)
                        ch.link(nc.vector.reciprocal(wtmp[:, :], o[:, :, HD:HD + 1].rearrange("p r d -> p (r d)")))
                        if kind == "cmp" and i == 0:
                            ch.link(nc.vector.tensor_scalar(wtmp[:, :], wtmp[:, :], any31[:, 0:1], None, ALU.mult))
                        gate = glog[:, i, :].rearrange("p (r b) -> p r b", b=3)[:, :, BRANCH[kind]]
                        ch.link(nc.vector.tensor_tensor(wgt[:, :], wtmp[:, :], gate, ALU.mult))
                        if n >= 4:
                            dve.wait_ge(final_done, g * TT + (n - 4) // 3 + 1)
                        nc.vector.tensor_tensor(o_gated[:, n % 4, :].rearrange("p (r d) -> p r d", r=REP), o[:, :, 0:HD],
                                                wgt[:, :].unsqueeze(2).broadcast_to([P, REP,
                                                        HD]), ALU.mult).then_inc(gated, 1)
                    if slot["final"] is not None:
                        i = slot["final"]
                        dve.wait_ge(oh_done, g * TT + i + 1)
                        q0 = TILE_ORDER[i] * P
                        o = [a[:, bass.ds(g * 2, 2), q0:q0 + P] for a in (outb_h, outb_l)]
                        nc.vector.tensor_tensor(o[1], bank[:, 2, 0:2 * P].rearrange("p (b n) -> p b n", b=2),
                                                o[0].bitcast(F32), ALU.subtract).then_inc(ol_done, 1)
                ch.leave(GROUPS)

            def low(turn, per, m, dst, src, hi):
                dve.wait_ge(ph_done, turn * per + (m + 1))
                nc.vector.tensor_tensor(dst, src, hi.bitcast(F32), ALU.subtract).then_inc(pl_done, 1)

            def low_ring(turn, m, slot):
                low(turn, 4, m, ring_l[:, slot, :], raw[:, slot, :], ring_h[:, slot, :])

            def merge(b, turn, m0, c0, t0, last=False, beside=None, beside_at=0):
                sig = sig_0 if b == 0 else sig_all
                for a in range(2):
                    low_ring(turn, m0 + 2 * a + 1, 1)
                    if beside and a == beside_at:
                        beside()
                    if not (last and a == 1):
                        low_ring(turn, m0 + 2 * a + 2 + (4 if b == 0 and beside and a == 1 else 0), 0)
                    dve.wait_ge(sig_done, turn * 2 + (t0 + a + 1))
                    dve.wait_ge(mm_done, turn * 4 + (2 + c0 + 2 * a + 2))
                    for h in range(2):
                        o = sig[:, a, h * HALF:(h + 1) * HALF]
                        nc.vector.tensor_tensor(o, o, bank[:, 2 * (2 * a + 1) + h, :], ALU.mult).then_inc(freed, 1)
                    dve.wait_ge(freed, turn * 4 + (4 + c0 + 2 * a + 2))
                    dst = merged[:, bass.ds(turn * 2 + a, 1), :].rearrange("p a n -> p (a n)")
                    if b == 1:
                        nc.vector.tensor_copy(dst, sig[:, a, :]).then_inc(acc_done, 1)
                    else:
                        nc.vector.tensor_tensor(dst, dst, sig[:, a, :], ALU.add).then_inc(acc_done, 1)

            def own(semaphore, value):
                dve.wait_ge(semaphore, value)

            low_ring(0, 0, 0)
            with dve.Fori(0, KT // 2) as t:
                merge(1, t, PIECE["merge1"], CHUNK["merge1"], 0)

            ch.link(nc.vector.memset(conv_u[:, :, 0:2], 0.0))
            for c in range(3 * BK):
                m, ck_ = PIECE["conv"] + c, CHUNK["conv"] + c
                q = c // 3
                low_ring(0, m + 1, (c + 1) % 2)
                ps = flat[:, (ck_ % 4) * 1024:(ck_ % 4 + 1) * 1024]
                u_, o_ = conv_u[:, q % 2, :], conv_o[:, q % 2, :]
                if c % 3 == 1:
                    dve.wait_ge(convc_done, q + 1)
                    dve.wait_ge(mm_done, 2 + ck_ + 1)
                    for h in range(2):
                        nc.vector.tensor_tensor(u_[:, 2 + h * HALF:2 + (h + 1) * HALF],
                                conv_c[:, q % 2, h * HALF:(h + 1) * HALF],
                                                ps[:, h * HALF:(h + 1) * HALF], ALU.mult).then_inc(freed, 1)
                    own(freed, 4 + ck_ + 1)
                    taps = [chan[:, C_CA + j * BK + q:C_CA + j * BK + q + 1] for j in range(3)]
                    if q >= 2:
                        dve.wait_ge(obl_done, q - 1)
                    ch.link(nc.vector.tensor_scalar(o_, u_[:, 0:S], taps[0], None, ALU.mult))
                    ch.link(nc.vector.scalar_tensor_tensor(o_, u_[:, 1:S + 1], taps[1], o_, ALU.mult, ALU.add))
                    ch.link(nc.vector.scalar_tensor_tensor(o_, u_[:, 2:S + 2], taps[2], o_, ALU.mult, ALU.add))
                if c % 3 == 2:
                    dve.wait_ge(mm_done, 2 + ck_ + 1)
                    nc.vector.tensor_tensor(o_, o_, ps, ALU.mult).then_inc(freed, 1)
                    dve.wait_ge(obh_done, q + 1)
                    nc.vector.tensor_tensor(outb_l[:, q, :], o_, outb_h[:, q, :].bitcast(F32),
                            ALU.subtract).then_inc(obl_done, 1)
            def value_weights():
                for c in range(4):
                    low(0, 4, PIECE["v"] + c, wv_l[:, 2 * c:2 * c + 2, :],
                            raw[:, c % 2, :].rearrange("p (k n) -> p k n", k=2),
                        wv_h[:, 2 * c:2 * c + 2, :])

            with dve.Fori(0, KT // 2 - 1) as t:
                merge(0, t, PIECE["merge0"], CHUNK["merge0"], KT)
            merge(0, KT // 2 - 1, PIECE["merge0"], CHUNK["merge0"], KT, beside=value_weights, beside_at=1)

            for t in range(TT):
                dve.wait_ge(gelu_done, t + 1)
                ch.link(nc.vector.tensor_tensor(sgu_sq[:, :], sgu_v[:, t, :], sgu_v[:, t, :], ALU.mult))
                ch.link(nc.vector.tensor_reduce(va[:, 3, t:t + 1], sgu_sq[:, :], AX, ALU.add))
            nc.vector.tensor_scalar(va[:, 0, :], va[:, 3, :], 1.0 / BW, EPS, ALU.mult, ALU.add).then_inc(va_done, 1)
            inverse_root(va[:, 0, :], va[:, 1, :], va[:, 2, :], va[:, 3, :], TT, vr_done, 1)

            dve.wait_ge(poolw_h, 1)
            nc.vector.tensor_tensor(pool_wl[:, :, :], pool_w32[:, :, :], pool_wh[:, :, :].bitcast(F32),
                    ALU.subtract).then_inc(poolw_l, 1)
            dve.wait_ge(iota_done, 1)
            for q, w in enumerate(POOL_WINDOWS):
                ch.link(nc.vector.tensor_scalar(pool_inv[:, q, :], pool_t16[:, :], float(w), None, ALU.min))
            ch.link(nc.vector.reciprocal(pool_inv[:, :, :], pool_inv[:, :, :]))
            ch.link(nc.vector.memset(pool_p[:, :, 0:16], 0.0))
            ch.link(nc.vector.memset(pool_s[:, :, 0:16], 0.0))

            def pool_low(q):
                dve.wait_ge(obh_done, BK + q + 1)
                nc.vector.scalar_tensor_tensor(outb_l[:, q, :], flat[:, (2 + q % 2) * 1024:(3 + q % 2) * 1024],
                                               chan[:, C_PS + q:C_PS + q + 1], outb_h[:, q, :].bitcast(F32),
                                               ALU.mult, ALU.subtract).then_inc(obl_done, 1)

            for q, w in enumerate(POOL_WINDOWS):
                low_ring(0, PIECE["pool"] + q + 1, (q + 1) % 2)
                dve.wait_ge(poolp_done, q + 1)
                dve.sem_inc(freed, 1)
                if q >= 1:
                    pool_low(q - 1)
                cur_, shift, k = pool_p[:, q % 2, :], 1, 0
                while shift < w:
                    nxt = pool_s[:, k % 2, :]
                    ch.link(nc.vector.tensor_tensor(nxt[:, 16:], cur_[:, 16:], cur_[:, 16 - shift:S + 16 - shift], ALU.add))
                    cur_, shift, k = nxt, shift * 2, k + 1
                p_ = pool_p[:, q % 2, 16:]
                if q >= 1:
                    dve.wait_ge(pooldl_done, q)
                ch.link(nc.vector.scalar_tensor_tensor(pool_d[:, :], cur_[:, 16:], 1.0 / w, p_, ALU.mult, ALU.subtract))
                ch.link(nc.vector.tensor_tensor(pool_t16[:, :], cur_[:, 16:32], pool_inv[:, q, :], ALU.mult))
                nc.vector.tensor_tensor(pool_d[:, 0:16], pool_t16[:, :], p_[:, 0:16], ALU.subtract).then_inc(poold_done, 1)
                dve.wait_ge(pooldh_done, q + 1)
                nc.vector.tensor_tensor(pool_dl[:, :], pool_d[:, :], pool_dh[:, :].bitcast(F32),
                        ALU.subtract).then_inc(pooldl_done, 1)
            merge(2, 0, PIECE["merge2"], CHUNK["merge2"], 2 * KT, beside=lambda: pool_low(BK - 1))
            with dve.Fori(1, KT // 2) as t:
                merge(2, t, PIECE["merge2"], CHUNK["merge2"], 2 * KT)
            dve.wait_ge(sguc_loaded, 48)
            for t in range(TT):
                nc.vector.scalar_tensor_tensor(sgu_v[:, t, :], sgu_v[:, t, :], va[:, 2, t:t + 1], sgu_g[:, :],
                                               ALU.mult, ALU.mult).then_inc(vn_done, 1)
            def gate_product(q):
                o = sgu_u[:, q, :].rearrange("p (t n) -> p t n", t=TT)
                dve.wait_ge(u_done, q + 1)
                nc.vector.tensor_tensor(o, o, sgu_m[:, :, q, :], ALU.mult).then_inc(mix_done, 1)

            def gate_low(q):
                own(mix_done, q + 1)
                dve.wait_ge(obh_done, 2 * BK + q + 1)
                nc.vector.tensor_tensor(outb_l[:, q, :], sgu_u[:, q, :], outb_h[:, q, :].bitcast(F32),
                        ALU.subtract).then_inc(obl_done, 1)

            for q in range(BK):
                low_ring(0, PIECE["u"] + q + 1, (q + 1) % 2)
                if q == 1:
                    dve.wait_ge(swh_done, 1)
                    nc.vector.tensor_tensor(sgu_wl[:, :, :], bank[:, 4, :].rearrange("p (g t) -> p g t", g=BK),
                                            sgu_wh[:, :, :].bitcast(F32), ALU.subtract).then_inc(swl_done, 1)
                for t in (MIXED[q - 1] if q else ()):
                    dve.wait_ge(mix_mm, t + 1)
                    nc.vector.tensor_tensor(sgu_m[:, t, :, :], bank[:, 4 + t % 4, :].rearrange("p (g t) -> p g t", g=BK),
                                            sgu_bias[:, :, :], ALU.add).then_inc(mb_done, 1)
                for t in MIXED[q]:
                    own(vn_done, t + 1)
                    dve.wait_ge(vsh_done, t + 1)
                    nc.vector.tensor_tensor(sgu_vl[:, t, :], sgu_v[:, t, :], sgu_vh[:, t % 4, :].bitcast(F32),
                                            ALU.subtract).then_inc(vsl_done, 1)
                if q == BK - 1:
                    own(mb_done, TT)
                    for k in range(BK - 1):
                        gate_product(k)
                    for k in range(BK - 1):
                        gate_low(k)
                dve.wait_ge(u_done, q + 1)
                dve.sem_inc(freed, 1)
            gate_product(BK - 1)
            gate_low(BK - 1)
            with dve.Fori(0, KT // 2 - 1) as t:
                merge(3, t, PIECE["merge3"], CHUNK["merge3"], 3 * KT)

            def merged_low(k):
                own(acc_done, 2 + 3 * KT + k + 1)
                dve.wait_ge(mgh_done, k + 1)
                nc.vector.tensor_tensor(actT_l[:, k, :], merged[:, k, :], actT_h[:, k, :].bitcast(F32),
                        ALU.subtract).then_inc(mgl_done, 1)
                low(0, 4, PIECE["wo"] + k, wo_low(k), raw[:, k % 2, :], wo_h[:, k, :])

            def first_merged():
                merged_low(0)
                merged_low(1)

            merge(3, KT // 2 - 1, PIECE["merge3"], CHUNK["merge3"], 3 * KT, last=True, beside=first_merged, beside_at=1)
            for k in range(2, KT):
                merged_low(k)

            low_ring(0, PIECE["ff"], 0)

            def normed(t):
                if t >= 2:
                    dve.wait_ge(xT_done, TT + t - 1)
                nc.vector.scalar_tensor_tensor(xn2[:, t % 2, :], x2[:, t, :], x2a[:, 2, t:t + 1], norm2_b[:, :],
                                               ALU.mult, ALU.mult).then_inc(xn_done, 1)

            def residual(t):
                dve.wait_ge(x_loaded[t], 32)
                dve.wait_ge(wo_mm, t + 1)
                b = 2 * (t % 4) if t < 4 else 2 * (t % 2)
                nc.vector.tensor_tensor(x2[:, t, :], x2[:, t, :], flat[:, b * HALF:(b + 2) * HALF],
                        ALU.add).then_inc(x2_done, 1)

            def second_norm(t0, t1, count):
                dve.wait_ge(sq_done, TT + t1)
                nc.vector.tensor_scalar(x2a[:, 0, t0:t1], ssq[:, t0:t1], 1.0 / DM, EPS, ALU.mult,
                        ALU.add).then_inc(xa_done, 1)
                inverse_root(x2a[:, 0, t0:t1], x2a[:, 1, t0:t1], x2a[:, 2, t0:t1], x2a[:, 3, t0:t1], t1 - t0, xr_done,
                        TT + count)

            for t in range(4):
                residual(t)
            second_norm(0, 4, 1)
            dve.wait_ge(norm_loaded, 32)
            normed(0)
            normed(1)
            for t in range(TT):
                if t < 4:
                    residual(4 + t)
                dve.wait_ge(xh_done, TT + t + 1)
                cols = slice(t * P, (t + 1) * P)
                nc.vector.tensor_tensor(actT_l[:, :, cols], turned_tile(4, t), actT_h[:, :, cols].bitcast(F32),
                                        ALU.subtract).then_inc(xl_done, 1)
                if t + 2 < TT:
                    normed(t + 2)
                if t < 4:
                    second_norm(4 + t, 5 + t, 2 + t)
            ch.link(nc.vector.memset(ffg[:, :, 0:2], 0.0))

            def add_down(turn, tiles=range(TT)):
                for t in tiles:
                    dve.wait_ge(d_mm, (turn - 1) * TT + (t + 1))
                    nc.vector.tensor_tensor(x2[:, t, :], x2[:, t, :], flat[:, (2 + t % 2) * 1024:(3 + t % 2) * 1024],
                                            ALU.add).then_inc(d_done, 1)

            def ff(turn, last=False):
                m0, c0 = PIECE["ff"], CHUNK["ff"]
                for a in range(2):
                    low_ring(turn, m0 + 2 * a + 1, 1)
                    dve.wait_ge(gcopy_done, turn * 2 + (a + 1))
                    dve.sem_inc(freed, 1)
                    g_, o_ = ffg[:, a, :], ffc[:, a, :]
                    taps = [chan[:, bass.ds(turn * 2 + (C_CF + j * FT + a), 1)] for j in range(3)]
                    if not (isinstance(turn, int) and turn == 0):
                        own(ffl_done, (turn - 1) * 2 + (a + 1))
                    ch.link(nc.vector.tensor_scalar(o_, g_[:, 0:S], taps[0], None, ALU.mult))
                    ch.link(nc.vector.scalar_tensor_tensor(o_, g_[:, 1:S + 1], taps[1], o_, ALU.mult, ALU.add))
                    down_before = a == 0 and not (isinstance(turn, int) and turn == 0)
                    if down_before:
                        add_down(turn, range(1))
                    nc.vector.scalar_tensor_tensor(o_, g_[:, 2:S + 2], taps[2], o_, ALU.mult, ALU.add).then_inc(ffc_done, 1)
                    if down_before:
                        add_down(turn, range(1, TT))
                    if a == 1:
                        for k in range(2):
                            dve.wait_ge(wdh_done, turn * 2 + (k + 1))
                            nc.vector.tensor_tensor(wd_l[:, k, :], wd_raw[:, k, :], wd_h[:, k, :].bitcast(F32),
                                                    ALU.subtract).then_inc(wdl_done, 1)
                    if not (last and a == 1):
                        low_ring(turn, m0 + 2 * a + 2, 0)
                    dve.wait_ge(silu_done, turn * 2 + (a + 1))
                    dve.wait_ge(mm_done, turn * 4 + (2 + c0 + 2 * a + 2))
                    nc.vector.tensor_tensor(o_, o_, flat[:, 1024:2048], ALU.mult).then_inc(freed, 1)
                    dve.wait_ge(ffh_done, turn * 2 + (a + 1))
                    nc.vector.tensor_tensor(ffa_l[:, a, :], o_, ffa_h[:, a, :].bitcast(F32),
                            ALU.subtract).then_inc(ffl_done, 1)

            ff(0)
            with dve.Fori(1, FT // 2 - 1) as t:
                ch.enter(t - 1, 4)
                ff(t)
                ch.leave(FT // 2 - 2)
            ff(FT // 2 - 1, last=True)
            add_down(FT // 2)

        @block.tensor
        def _(pe):
            pe.wait_ge(consts_made, 12)
            for t in range(TT):
                if t == TT - 2:
                    pe.wait_ge(const_loaded, 16 * 5)
                    nc.tensor.transpose(bank[:, 6, 0:CHAN], chan_rows[:, :], ident[0:CHAN, 0:CHAN])
                    nc.tensor.transpose(bank[:, 6, CHAN:CHAN + 2 * L16], pe_rows[:, :],
                            ident[0:2 * L16, 0:2 * L16]).then_inc(chan_turned, 1)
                pe.wait_ge(xn_done, t + 1)
                if t >= 2:
                    pe.wait_ge(xl_done, t - 1)
                for k in range(KT):
                    ins = nc.tensor.transpose(bank[:, 2 * (t % 2) + k // 4, (k % 4) * P:(k % 4 + 1) * P],
                                              xn[:, t % 2, k * P:(k + 1) * P], ident[:, :])
                ins.then_inc(xT_done, 1)
            pe.wait_ge(xl_done, TT)
            pe.wait_ge(chan_done, 1)

            with pe.Fori(0, GROUPS) as g:

                def transposes(t):
                    pe.wait_ge(qkl_done, g * TT + t + 1)
                    after(pe, evq_done, g * TT, t)
                    after(pe, evk_done, g * TT, t)
                    for m in range(10):
                        ins = nc.tensor.transpose(bank[:, 4 + m // 4, (m % 4) * P:(m % 4 + 1) * P],
                                                  dup[:, t % 2, m, :], ident[:, :])
                    ins.then_inc(qkT_done, 1)

                for t in range(TT):
                    pe.wait_ge(xl_done, t + 1)
                    after(pe, pcopy_done, g * TT, t - 1)
                    A, B = bank[:, 2 * (t % 2), 0:QW], bank[:, 2 * (t % 2) + 1, 0:PW - QW]
                    for k in range(KT):
                        if t == 0 and k in (0, 2, 4):
                            pe.wait_ge(wpl_done, g * (SPLITS - len(POOL_SPLITS)) + {0: 3, 2: 4, 4: 5}[k])
                        if t == 0 and k in (4, 6):
                            pe.wait_ge(wpl_pool, g * len(POOL_SPLITS) + {4: 1, 6: 2}[k])
                        xh, xl = (a[:, k, t * P:(t + 1) * P] for a in (actT_h, actT_l))
                        first, last = k == 0, k == KT - 1
                        nc.tensor.matmul(A, xh, wp_h[:, k, 0:QW], start=first, stop=False)
                        nc.tensor.matmul(B, xh, wp_h[:, k, QW:PW], start=first, stop=False)
                        nc.tensor.matmul(A, xh, wp_l[:, k, 0:QW], start=False, stop=False)
                        nc.tensor.matmul(B, xh, wp_l[:, k, QW:PW], start=False, stop=False)
                        nc.tensor.matmul(A, xl, wp_h[:, k, 0:QW], start=False, stop=last)
                        ins = nc.tensor.matmul(B, xl, wp_h[:, k, QW:PW], start=False, stop=last)
                    ins.then_inc(proj_done, 1)
                    if t >= 1:
                        transposes(t - 1)
                pe.wait_ge(w1_loaded, 16 * 4)
                for j in range(2):
                    for l in range(L16):
                        ins = nc.tensor.matmul(bank[0:HD, 7, 64 * j:1 + 64 * j], w1[:, j, l, :],
                                               peT[:, j, l:l + 1], start=l == 0, stop=l == L16 - 1)
                ins.then_inc(cbias_mm, 1)
                transposes(TT - 1)

                def compressed(step, part=None):
                    if step == 0:
                        if part == 0:
                            pe.wait_ge(cbias_done, g + 1)
                        j = part // 2
                        for l in range(part % 2 * (L16 // 2), (part % 2 + 1) * (L16 // 2)):
                            ins = nc.tensor.matmul(bank[0:HD, 7, j * HD:j * HD + NCMP], w1[:, j, l, :],
                                                   kcT[:, j, l:l + CMP_STRIDE * (NCMP - 1) + 1:CMP_STRIDE],
                                                   start=l == 0, stop=l == L16 - 1)
                    elif step == 1:
                        pe.wait_ge(compress_act, g * 3 + 1)
                        pe.wait_ge(const2_loaded, 32)
                        pe.sem_inc(passed, 1)
                        for j in range(2):
                            ins = nc.tensor.matmul(bank[0:NCMP, 7, 256 + j * HD:256 + (j + 1) * HD], h1[:, j, 0:NCMP],
                                                   w2[:, j, :], start=True, stop=True)
                    else:
                        pe.wait_ge(compress_dve, g * 3 + 3)
                        pe.sem_inc(passed, 1)
                        for a in range(2):
                            ins = nc.tensor.transpose(bank[:, 7, 384 + a * CW:384 + a * CW + NCMP],
                                                      ckd[0:NCMP, a, :, :].rearrange("n u d -> n (u d)"), ident[0:NCMP,
                                                              0:NCMP])
                    if part is None or part == 3:
                        ins.then_inc(compress_pe, 1)

                def rows(at, n, r0, heads, c, w):
                    i, kind, k0, keys, blocks = tasks[n]
                    after(pe, max_done, g * PIECES, at - 1)
                    masks = []
                    if kind == "cmp":
                        masks.append((0, CW, cmask[:, i, :]))
                    else:
                        if kind == "win" and i >= WIN // P and c == 0:
                            masks.append((0, P, wstart[:, :]))
                        if c + w == keys:
                            masks.append((w - P, P, tri[:, :]))
                    for r in range(heads):
                        o = bank[:, at % 2, r * w:(r + 1) * w]
                        kh = kcAB[:, 0, :] if kind == "cmp" else kAB[:, 2 * (kind == "win"), k0 + c:k0 + c + w]
                        ins = nc.tensor.matmul(o, qT[:, r0 + r, i * P:(i + 1) * P], kh, start=True, stop=not masks)
                        for m, (a, mw, mask) in enumerate(masks):
                            ins = nc.tensor.matmul(o[:, a:a + mw], identb[:, :], mask, start=False, stop=m == len(masks) - 1)
                    ins.then_inc(rows_done, 1)

                def scores(u, n, j):
                    i, kind, k0, keys, blocks = tasks[n]
                    if j == 0:
                        pe.wait_ge(shift_done, g * NT + n + 1)
                    after(pe, exp_done, g * UNITS, u - 1)
                    q = qT[:, :, i * P:(i + 1) * P]
                    if kind == "cmp":
                        pe.sem_inc(passed, 1)
                        nr, kh, kl, mask = CW, kcAB[:, 0, :], kcAB[:, 1, :], cmask[:, i, :]
                    else:
                        nr, at = P, k0 + j * P
                        kh, kl = (kAB[:, 2 * (kind == "win") + a, at:at + P] for a in range(2))
                        mask = tri[:, :] if j == blocks - 1 else None
                        if kind == "win" and i >= WIN // P and j == 0:
                            mask = wstart[:, :]
                    o = bank[0:nr, 3 + u % 2, :]
                    nc.tensor.matmul(o, kh, q, start=True, stop=False)
                    nc.tensor.matmul(o, kl, q, start=False, stop=False)
                    if mask is not None:
                        nc.tensor.matmul(o, mask, identb[:, :].unsqueeze(1).broadcast_to([P, REP, P]), start=False,
                                stop=False)
                    nc.tensor.matmul(o, ones[:, 0:nr], shift[:, n % MAXIMA, :, :], start=False,
                            stop=True).then_inc(s_done, 1)

                def values(u, n, j):
                    i, kind, k0, keys, blocks = tasks[n]
                    pe.wait_ge(ptl_done, g * UNITS + u + 1)
                    if j == 0:
                        after(pe, evac_done, g * NT, n - 1)
                    pe.sem_inc(passed, 1)
                    if kind == "cmp":
                        nr, vh, vl = CW, vc_h[:, :], vc_l[:, :]
                    else:
                        ty = 0 if kind == "slc" else 1
                        nr, vh, vl = P, v_h[:, ty, k0 // P + j, :], v_l[:, ty, k0 // P + j, :]
                    o = bank[0:HD + 1, 5 + n % 2, :]
                    nc.tensor.matmul(o, vh, pT_h[0:nr, u % RING, :], start=j == 0, stop=False)
                    nc.tensor.matmul(o, vh, pT_l[0:nr, u % RING, :], start=False, stop=False)
                    nc.tensor.matmul(o, vl, pT_h[0:nr, u % RING, :], start=False, stop=j == blocks - 1).then_inc(pv_done, 1)

                pe.wait_ge(compress_dve, g * 3 + 1)
                pe.wait_ge(evq_done, g * TT + TT)
                pe.wait_ge(evk_done, g * TT + TT)
                for slot in slots:
                    if slot["n"] <= COMPRESS[0]:
                        compressed(0, slot["n"])
                    elif slot["n"] in COMPRESS:
                        compressed(COMPRESS.index(slot["n"]))
                    if slot["n"] == COMPRESS[2] + 1:
                        pe.wait_ge(compress_act, g * 3 + 3)
                    for piece in slot["pieces"]:
                        rows(*piece)
                    if slot["unit"]:
                        scores(*slot["unit"])
                    if slot["values"]:
                        values(*slot["values"])
                    if slot["turn"] is not None:
                        n = slot["turn"]
                        pe.wait_ge(evac_done, g * NT + n + 1)
                        after(pe, gated, g * NT, n)
                        pe.sem_inc(passed, 1)
                        for r in range(REP):
                            ins = nc.tensor.transpose(bank[:, 7, r * (HD + 1):(r + 1) * (HD + 1)],
                                                      oT[:, n % 2, r * P:(r + 1) * P], ident[0:HD + 1, 0:HD + 1])
                        ins.then_inc(turned, 1)
                    if slot["final"] is not None:
                        i = slot["final"]
                        pe.wait_ge(summed, g * TT + i + 1)
                        after(pe, ol_done, g * TT, i)
                        for b in range(2):
                            ins = nc.tensor.transpose(bank[:, 2, b * P:(b + 1) * P],
                                                      o_gated[:, 3 * i % 4, b * P:(b + 1) * P], ident[:, :])
                        ins.then_inc(final_done, 1)
                pe.wait_ge(exp_done, g * UNITS + UNITS)
                pe.wait_ge(ol_done, g * TT + TT)

            def product(k_tiles, wh, wl, ah, al, out_bank, normed_tiles=False):
                for h in range(2):
                    if normed_tiles:
                        pe.wait_ge(xl_done, TT + 4 * (h + 1))
                    cols = slice(h * HALF, (h + 1) * HALF)
                    for k in range(k_tiles):
                        if normed_tiles and (h, k) in ((0, 2), (0, 5), (0, 7)):
                            turn_normed(TT - 3 + (2, 5, 7).index(k))
                        o = bank[:, out_bank + h, :]
                        nc.tensor.matmul(o, wh(k), ah[:, k, cols], start=k == 0, stop=False)
                        nc.tensor.matmul(o, wh(k), al[:, k, cols], start=False, stop=False)
                        ins = nc.tensor.matmul(o, wl(k), ah[:, k, cols], start=False, stop=k == k_tiles - 1)
                return ins

            def chunk(turn, m, c, slot, k_tiles, ah, al, tile, normed_tiles=False):
                pe.wait_ge(pl_done, turn * 4 + (2 + m + 1))
                pe.wait_ge(freed, turn * 4 + (c + 1))
                product(k_tiles, lambda k: ring_h[:, slot, k * P:(k + 1) * P], lambda k: ring_l[:, slot, k * P:(k + 1) * P],
                        ah, al, 2 * tile, normed_tiles).then_inc(mm_done, 1)

            def merge(turn, m0, c0, branch_ready, beside=None):
                for a in range(2):
                    chunk(turn, m0 + 2 * a, c0 + 2 * a, 0, KT, actT_h, actT_l, 2 * a)
                    if beside and a == 0:
                        beside()
                    if branch_ready:
                        pe.wait_ge(obl_done, branch_ready)
                    chunk(turn, m0 + 2 * a + 1, c0 + 2 * a + 1, 1, BK, outb_h, outb_l, 2 * a + 1)

            pe.sem_inc(mm_done, 2)
            with pe.Fori(0, KT // 2) as t:
                merge(t, PIECE["merge1"], CHUNK["merge1"], 0)
            for c in range(3 * BK):
                chunk(0, PIECE["conv"] + c, CHUNK["conv"] + c, c % 2, KT, actT_h, actT_l, (CHUNK["conv"] + c) % 4)
            with pe.Fori(0, KT // 2) as t:
                merge(t, PIECE["merge0"], CHUNK["merge0"], BK)

            def pool_product(q):
                pe.wait_ge(poolw_l, 1)
                pe.wait_ge(pooldl_done, q + 1)
                if q < 2:
                    pe.wait_ge(gelu_done, TT)
                else:
                    pe.wait_ge(obl_done, BK + q - 1)
                for h in range(2):
                    cols = slice(h * HALF, (h + 1) * HALF)
                    o = bank[:, 2 * (2 + q % 2) + h, :]
                    nc.tensor.matmul(o, pool_wh[:, q, :], pool_dh[:, cols], start=True, stop=False)
                    nc.tensor.matmul(o, pool_wh[:, q, :], pool_dl[:, cols], start=False, stop=False)
                    ins = nc.tensor.matmul(o, pool_wl[:, q, :], pool_dh[:, cols], start=False, stop=True)
                ins.then_inc(pooly_mm, 1)

            pe.wait_ge(pl_done, 2 + PIECE["v"] + 4)
            for t in range(TT):
                pe.wait_ge(freed, 4 + CHUNK["pool"] - (2 if t < 4 else 0))
                for k in range(KT):
                    xh, xl = (a[:, k, t * P:(t + 1) * P] for a in (actT_h, actT_l))
                    nc.tensor.matmul(bank[:, t, :], xh, wv_h[:, k, :], start=k == 0, stop=False)
                    nc.tensor.matmul(bank[:, t, :], xh, wv_l[:, k, :], start=False, stop=False)
                    ins = nc.tensor.matmul(bank[:, t, :], xl, wv_h[:, k, :], start=False, stop=k == KT - 1)
                ins.then_inc(v_mm, 1)

            for q in range(BK):
                if q < 2:
                    pe.wait_ge(gelu_done, 2 * (q + 1))
                else:
                    pe.wait_ge(freed, 4 + CHUNK["pool"] + q - 1)
                chunk(0, PIECE["pool"] + q, CHUNK["pool"] + q, q % 2, KT, actT_h, actT_l, q % 2)
                if q >= 1:
                    pool_product(q - 1)
            pe.wait_ge(freed, 4 + CHUNK["merge2"])
            merge(0, PIECE["merge2"], CHUNK["merge2"], 2 * BK, beside=lambda: pool_product(BK - 1))
            with pe.Fori(1, KT // 2) as t:
                merge(t, PIECE["merge2"], CHUNK["merge2"], 2 * BK)
            for q in range(BK):
                if q >= 2:
                    pe.wait_ge(freed, 4 + CHUNK["u"] + q - 1)
                chunk(0, PIECE["u"] + q, CHUNK["u"] + q, q % 2, KT, actT_h, actT_l, q % 2)
                if q == 0:
                    pe.wait_ge(sguw_masked, 1)
                    pe.wait_ge(freed, 4 + CHUNK["u"])
                    for g4 in range(BK):
                        ins = nc.tensor.transpose(bank[:, 4, g4 * P:(g4 + 1) * P], sgu_w32[:, g4, :], ident[:, :])
                    ins.then_inc(swT_done, 1)
                for t in MIXED[q]:
                    if t == 0:
                        pe.wait_ge(swl_done, 1)
                    pe.wait_ge(vsl_done, t + 1)
                    if t >= 4:
                        pe.wait_ge(mb_done, t - 3)
                    for g4 in range(BK):
                        o = bank[:, 4 + t % 4, g4 * P:(g4 + 1) * P]
                        vh, vl = sgu_vh[:, t % 4, g4 * P:(g4 + 1) * P], sgu_vl[:, t, g4 * P:(g4 + 1) * P]
                        nc.tensor.matmul(o, vh, sgu_wh[:, g4, :], start=True, stop=False)
                        nc.tensor.matmul(o, vh, sgu_wl[:, g4, :], start=False, stop=False)
                        ins = nc.tensor.matmul(o, vl, sgu_wh[:, g4, :], start=False, stop=True)
                    ins.then_inc(mix_mm, 1)
            pe.wait_ge(freed, 4 + CHUNK["merge3"] - 1)
            with pe.Fori(0, KT // 2) as t:
                merge(t, PIECE["merge3"], CHUNK["merge3"], 3 * BK)

            def output_products(t, k, first_bank):
                mh, ml = (a[:, k, t * P:(t + 1) * P] for a in (actT_h, actT_l))
                for n, (m, w) in enumerate(((mh, wo_h[:, k, :]), (mh, wo_low(k)), (ml, wo_h[:, k, :]))):
                    for h in range(2):
                        ins = nc.tensor.matmul(bank[:, first_bank + h, :], m, w[:, h * HALF:(h + 1) * HALF],
                                               start=k == 0 and n == 0, stop=k == KT - 1 and n == 2)
                if k == KT - 1:
                    ins.then_inc(wo_mm, 1)

            for k in range(KT):
                pe.wait_ge(mgl_done, k + 1)
                pe.wait_ge(pl_done, 2 + PIECE["wo"] + k + 1)
                for t in range(4):
                    if k == 0:
                        pe.wait_ge(freed, 4 + CHUNK["ff"] - (2 if t < 2 else 0))
                    output_products(t, k, 2 * t)
            def turn_normed(t):
                pe.wait_ge(xn_done, TT + t + 1)
                if t < 2:
                    pe.wait_ge(x2_done, t + 3)
                else:
                    pe.wait_ge(xl_done, TT + t - 1)
                for k in range(KT):
                    ins = nc.tensor.transpose(bank[:, 4 + 2 * (t % 2) + k // 4, (k % 4) * P:(k % 4 + 1) * P],
                                              xn2[:, t % 2, k * P:(k + 1) * P], ident[:, :])
                ins.then_inc(xT_done, 1)

            for t in range(TT - 3):
                if t < 4:
                    pe.wait_ge(x2_done, t + 1 if t < 2 else t + 3)
                    for k in range(KT):
                        output_products(4 + t, k, 2 * (t % 2))
                turn_normed(t)

            def down(turn):
                pe.wait_ge(ffl_done, turn * 2)
                pe.wait_ge(wdl_done, turn * 2 + 2)
                for t in range(TT):
                    pe.wait_ge(d_done, (turn - 1) * TT + (t + 1))
                    o = [bank[:, 4 + 2 * (t % 2) + h, :] for h in range(2)]
                    for k in range(2):
                        ah, al = (a[:, k, t * P:(t + 1) * P] for a in (ffa_h, ffa_l))
                        for n, (av, w) in enumerate(((ah, wd_h), (ah, wd_l), (al, wd_h))):
                            for h in range(2):
                                ins = nc.tensor.matmul(o[h], av, w[:, k, h * HALF:(h + 1) * HALF],
                                                       start=k == 0 and n == 0, stop=k == 1 and n == 2)
                    ins.then_inc(d_mm, 1)

            def ff(turn):
                m0, c0 = PIECE["ff"], CHUNK["ff"]
                for c in range(4):
                    if not (isinstance(turn, int) and turn == 0 and c < 2):
                        pe.wait_ge(freed, turn * 4 + (4 + c0 + c - 1))
                    at_start = isinstance(turn, int) and turn == 0 and c == 0
                    if at_start:
                        pe.wait_ge(x2_done, TT - 1)
                    chunk(turn, m0 + c, c0 + c, c % 2, KT, actT_h, actT_l, c % 2, normed_tiles=at_start)
                    if c == 0 and not (isinstance(turn, int) and turn == 0):
                        down(turn)

            ff(0)
            with pe.Fori(1, FT // 2 - 1) as t:
                ff(t)
            ff(FT // 2 - 1)
            down(FT // 2)


_INS = ["x", "norm1_g", "w_in", "conv_a_w", "qk_norm_g", "cmp_pe", "cmp_w1", "cmp_w2", "pool_w", "pool_scale",
        "sgu_norm_g", "sgu_w", "sgu_b", "w_branch", "w_o", "norm2_g", "w_up", "conv_ff_w", "w_down"]


def kernel(**inputs):
    import concourse.bacc as bacc
    from concourse.bass_utils import run_bass_kernel_spmd as run

    nc = bacc.Bacc("TRN2", target_bir_lowering=False, num_devices=1)
    arrays, args = {}, []
    for name in _INS:
        a = np.ascontiguousarray(inputs[name])
        arrays[f"in_{name}"] = a
        args.append(nc.dram_tensor(f"in_{name}", a.shape, mybir.dt.from_np(a.dtype), kind="ExternalInput").ap())
    args.append(nc.dram_tensor("out_0", (1, S, DM), F32, kind="ExternalOutput").ap())
    build(nc, *args)
    return run(nc, [arrays], core_ids=[0]).results[0]["out_0"]
```
